# Optimizing a Trainium2 kernel written in Bass

```python
import jax
import jax.numpy as jnp
from jax import lax
import numpy as np
import math

D_MODEL = 1024
BATCH = 1
SEQ = 256
DEPTH = 2

GRID_W = 64
CTX_LEN = 256

NA_HEAD_DIM = 64
NA_HEADS = (D_MODEL // 2) // NA_HEAD_DIM
NA_WIDTH = NA_HEADS * NA_HEAD_DIM
NA_KH = 8
NA_KW = 16
ML_HEAD_DIM = 128
ML_HEADS = (D_MODEL // 2) // ML_HEAD_DIM
ML_WIDTH = ML_HEADS * ML_HEAD_DIM
ML_CHUNK = 128
ML_GATE_CAP = 15.0
AB_IN_WIDTH = 3 * NA_WIDTH + 4 * ML_WIDTH + 4 * ML_HEADS
RW_HEAD_DIM = 64
RW_HEADS = D_MODEL // RW_HEAD_DIM
RW_DECAY_LORA = 64
RW_AAA_LORA = 64
RW_GATE_LORA = 160
RW_GN_EPS = 64e-5
D_FF = 4 * D_MODEL
ROPE_BASE = 10000.0
NORM_EPS = 1e-6


def rms_norm(x, eps=NORM_EPS):
    xf = x.astype(jnp.float32)
    return (xf * lax.rsqrt(jnp.mean(xf * xf, axis=-1, keepdims=True) + eps)).astype(x.dtype)

def modulate(x, shift, scale):
    return rms_norm(x) * (1.0 + scale) + shift

def split_heads(t, n_heads, head_dim):
    return t.reshape(*t.shape[:-1], n_heads, head_dim)

def adaln(cond, w, b):
    return jnp.split(jax.nn.silu(cond) @ w + b, 6, axis=-1)

def squared_relu_mlp(h, w1, w2):
    return jnp.square(jax.nn.relu(h @ w1)) @ w2

def axial_rope_angles(n_tokens, head_dim):
    pos = jnp.arange(n_tokens)
    rows = (pos // GRID_W).astype(jnp.float32)
    cols = (pos % GRID_W).astype(jnp.float32)
    n_freq = head_dim // 4
    inv_freq = ROPE_BASE ** (-jnp.arange(n_freq, dtype=jnp.float32) / n_freq)
    return rows[:, None] * inv_freq, cols[:, None] * inv_freq

def rope_rotate(x, ang):
    x1, x2 = jnp.split(x, 2, axis=-1)
    cos = jnp.cos(ang)[:, None, :].astype(x.dtype)
    sin = jnp.sin(ang)[:, None, :].astype(x.dtype)
    return jnp.concatenate([x1 * cos - x2 * sin, x1 * sin + x2 * cos], axis=-1)

def axial_rope(x, ang_r, ang_c):
    x_row, x_col = jnp.split(x, 2, axis=-1)
    return jnp.concatenate([rope_rotate(x_row, ang_r), rope_rotate(x_col, ang_c)], axis=-1)

def context_attention(q, k, v):
    s = jnp.einsum('bqhd,bkhd->bhqk', q, k).astype(jnp.float32) * (q.shape[-1] ** -0.5)
    p = jax.nn.softmax(s, axis=-1).astype(v.dtype)
    return jnp.einsum('bhqk,bkhd->bqhd', p, v)

def neighbourhood_attention(q, k, v, k_ctx, v_ctx, rpb):
    n_b, n_tok, n_h, d_h = q.shape
    rows = n_tok // GRID_W
    kh = min(NA_KH, rows)
    n_win = kh * NA_KW
    scale = d_h ** -0.5
    qg = q.reshape(n_b, rows, GRID_W, n_h, d_h)
    kg = k.reshape(n_b, rows, GRID_W, n_h, d_h)
    vg = v.reshape(n_b, rows, GRID_W, n_h, d_h)
    row_idx = jnp.arange(rows)
    row_start = jnp.clip(row_idx - kh // 2, 0, rows - kh)
    col_idx = jnp.arange(GRID_W)
    col_win = jnp.clip(col_idx - NA_KW // 2, 0, GRID_W - NA_KW)[:, None] + jnp.arange(NA_KW)[None, :]
    rpb_c = rpb[:, :, col_win - col_idx[:, None] + NA_KW - 1]

    def one_row(args):
        r, rs, q_row = args
        k_nb = lax.dynamic_slice_in_dim(kg, rs, kh, axis=1)[:, :, col_win]
        v_nb = lax.dynamic_slice_in_dim(vg, rs, kh, axis=1)[:, :, col_win]
        bias = rpb_c[:, rs + jnp.arange(kh) - r + NA_KH - 1]
        s_nb = jnp.einsum('bchd,bicjhd->bhcij', q_row, k_nb).astype(jnp.float32) * scale + jnp.transpose(bias, (0, 2, 1, 3))
        s_cx = jnp.einsum('bchd,bnhd->bhcn', q_row, k_ctx).astype(jnp.float32) * scale
        p = jax.nn.softmax(jnp.concatenate([s_nb.reshape(n_b, n_h, GRID_W, n_win), s_cx], axis=-1), axis=-1).astype(v.dtype)
        p_nb = p[..., :n_win].reshape(n_b, n_h, GRID_W, kh, NA_KW)
        return jnp.einsum('bhcij,bicjhd->bchd', p_nb, v_nb) + jnp.einsum('bhcn,bnhd->bchd', p[..., n_win:], v_ctx)

    out = lax.map(one_row, (row_idx, row_start, jnp.moveaxis(qg, 1, 0)))
    return jnp.moveaxis(out, 0, 1).reshape(n_b, n_tok, n_h, d_h)

def mlstm_chunked(q, k, v, log_i, log_f, state, with_out):
    n_b, n_h, n_t, _ = q.shape
    n_c = n_t // ML_CHUNK

    def chunks(t):
        return jnp.moveaxis(t.reshape(n_b, n_h, n_c, ML_CHUNK, *t.shape[3:]), 2, 0)

    tril = jnp.tril(jnp.ones((ML_CHUNK, ML_CHUNK), dtype=bool))

    def step(carry, inp):
        c_st, n_st, m_st = carry
        qc, kc, vc, ic, fc = inp
        b = jnp.cumsum(fc, axis=-1)
        log_d = jnp.where(tril, b[..., :, None] - b[..., None, :] + ic[..., None, :], -jnp.inf)
        log_inter = b + m_st[..., None]
        m_t = jnp.maximum(log_inter, jnp.max(log_d, axis=-1))
        m_new = m_t[..., -1]
        w_s = jnp.exp(b[..., -1:] - b + ic - m_new[..., None])
        decay = jnp.exp(b[..., -1] + m_st - m_new)
        c_new = decay[..., None, None] * c_st + jnp.einsum('bhs,bhsd,bhse->bhde', w_s, kc, vc)
        n_new = decay[..., None] * n_st + jnp.einsum('bhs,bhsd->bhd', w_s, kc)
        if not with_out:
            return (c_new, n_new, m_new), None
        d_mat = jnp.exp(log_d - m_t[..., None])
        w_inter = jnp.exp(log_inter - m_t)
        s = jnp.einsum('bhtd,bhsd->bhts', qc, kc) * d_mat
        num = jnp.einsum('bhts,bhse->bhte', s, vc) + w_inter[..., None] * jnp.einsum('bhtd,bhde->bhte', qc, c_st)
        den = jnp.sum(s, axis=-1) + w_inter * jnp.einsum('bhtd,bhd->bht', qc, n_st)
        h = num / jnp.maximum(jnp.abs(den), jnp.exp(-m_t))[..., None]
        return (c_new, n_new, m_new), h

    state, hs = lax.scan(step, state, tuple(chunks(t) for t in (q, k, v, log_i, log_f)))
    if not with_out:
        return None, state
    return jnp.moveaxis(hs, 0, 2).reshape(n_b, n_h, n_t, -1), state

def mlstm_bidir(q_l, k_l, v_l, g_l, q_c, k_c, v_c, g_c, need_ctx):
    def heads_first(t):
        return jnp.swapaxes(t, 1, 2).astype(jnp.float32)

    def gates(g):
        g = ML_GATE_CAP * jnp.tanh(g.astype(jnp.float32) / ML_GATE_CAP)
        i_f, f_f, i_b, f_b = jnp.split(jnp.swapaxes(g, 1, 2), 4, axis=1)
        return i_f, jax.nn.log_sigmoid(f_f), i_b, jax.nn.log_sigmoid(f_b)

    def flip(t):
        return jnp.flip(t, axis=2)

    n_b = q_l.shape[0]
    zero = (jnp.zeros((n_b, ML_HEADS, ML_HEAD_DIM, ML_HEAD_DIM), jnp.float32),
            jnp.zeros((n_b, ML_HEADS, ML_HEAD_DIM), jnp.float32),
            jnp.zeros((n_b, ML_HEADS), jnp.float32))
    qc, kc, vc = heads_first(q_c), heads_first(k_c), heads_first(v_c)
    if_c, lf_c, ib_c, lb_c = gates(g_c)
    hc_f, st_f = mlstm_chunked(qc, kc, vc, if_c, lf_c, zero, need_ctx)
    hc_b, st_b = mlstm_chunked(flip(qc), flip(kc), flip(vc), flip(ib_c), flip(lb_c), zero, need_ctx)
    ql, kl, vl = heads_first(q_l), heads_first(k_l), heads_first(v_l)
    if_l, lf_l, ib_l, lb_l = gates(g_l)
    hl_f, _ = mlstm_chunked(ql, kl, vl, if_l, lf_l, st_f, True)
    hl_b, _ = mlstm_chunked(flip(ql), flip(kl), flip(vl), flip(ib_l), flip(lb_l), st_b, True)
    h_lat = jnp.swapaxes(hl_f + flip(hl_b), 1, 2)
    h_ctx = jnp.swapaxes(hc_f + flip(hc_b), 1, 2) if need_ctx else None
    return h_lat, h_ctx

def ab_mixer(h_l, h_c, w_in, gate_b, q_norm, k_norm, rpb, head_norm, w_out, ang_r, ang_c, need_ctx):
    splits = [NA_WIDTH, 2 * NA_WIDTH, 3 * NA_WIDTH, 3 * NA_WIDTH + ML_WIDTH, 3 * NA_WIDTH + 2 * ML_WIDTH,
              3 * NA_WIDTH + 3 * ML_WIDTH, 3 * NA_WIDTH + 4 * ML_WIDTH]

    def project(h):
        qa, ka, va, qb, kb, vb, ob, g = jnp.split(h @ w_in, splits, axis=-1)
        qa = rms_norm(split_heads(qa, NA_HEADS, NA_HEAD_DIM)) * q_norm
        ka = rms_norm(split_heads(ka, NA_HEADS, NA_HEAD_DIM)) * k_norm
        va = split_heads(va, NA_HEADS, NA_HEAD_DIM)
        qb = split_heads(qb, ML_HEADS, ML_HEAD_DIM)
        kb = split_heads(kb, ML_HEADS, ML_HEAD_DIM) * (ML_HEAD_DIM ** -0.5)
        vb = split_heads(vb, ML_HEADS, ML_HEAD_DIM)
        return qa, ka, va, qb, kb, vb, ob, g + gate_b

    qa_l, ka_l, va_l, qb_l, kb_l, vb_l, ob_l, g_l = project(h_l)
    qa_c, ka_c, va_c, qb_c, kb_c, vb_c, ob_c, g_c = project(h_c)
    qb_l = axial_rope(qb_l, ang_r, ang_c)
    kb_l = axial_rope(kb_l, ang_r, ang_c)
    na_l = neighbourhood_attention(qa_l, ka_l, va_l, ka_c, va_c, rpb)
    ml_l, ml_c = mlstm_bidir(qb_l, kb_l, vb_l, g_l, qb_c, kb_c, vb_c, g_c, need_ctx)

    def merge(na, ml, o):
        ml = (rms_norm(ml) * head_norm).astype(o.dtype) * jax.nn.sigmoid(split_heads(o, ML_HEADS, ML_HEAD_DIM))
        cat = jnp.concatenate([na.reshape(*na.shape[:2], NA_WIDTH), ml.reshape(*ml.shape[:2], ML_WIDTH)], axis=-1)
        return cat @ w_out

    out_l = merge(na_l, ml_l, ob_l)
    out_c = merge(context_attention(qa_c, ka_c, va_c), ml_c, ob_c) if need_ctx else None
    return out_l, out_c

def centred_shift(x):
    xp = jnp.pad(x, ((0, 0), (1, 1), (0, 0)))
    return 0.5 * (xp[:, :-2] + xp[:, 2:])

def rwkv_prepare(h, mu, w_rkv, w0, w1, w2, a0, a1, a2, g1, g2, k_k, k_a):
    xx = centred_shift(h) - h
    xr, xw, xk, xv, xa, xg = h[None] + xx[None] * mu[:, None, None, :]
    r, k, v = jnp.einsum('sbtd,sde->sbte', jnp.stack([xr, xk, xv]), w_rkv)
    w_logit = w0[:, None, None, :] + jnp.einsum('zbtr,zrd->zbtd', jnp.tanh(jnp.einsum('btd,zdr->zbtr', xw, w1)), w2)
    decay = jnp.exp(-jnp.exp(-jax.nn.softplus(-w_logit.astype(jnp.float32)) - 0.5))
    a = jax.nn.sigmoid(a0[:, None, None, :] + jnp.einsum('zbtr,zrd->zbtd', jnp.einsum('btd,zdr->zbtr', xa, a1), a2))
    g = jax.nn.sigmoid(xg @ g1) @ g2
    kk = split_heads((k * k_k).astype(jnp.float32), RW_HEADS, RW_HEAD_DIM)
    kk = (kk / jnp.maximum(jnp.linalg.norm(kk, axis=-1, keepdims=True), 1e-12)).reshape(k.shape)
    k_dir = k[None] * (1.0 + (a - 1.0) * k_a)
    return r, k_dir, v, decay, -kk, kk[None] * a, g

def rwkv7_scan(r, w, k, v, a, b, state, reverse, with_out):
    def time_major(t):
        return jnp.moveaxis(split_heads(t.astype(jnp.float32), RW_HEADS, RW_HEAD_DIM), 1, 0)

    def step(s, inp):
        rt, wt, kt, vt, at, bt = inp
        sa = jnp.einsum('bhij,bhj->bhi', s, at)
        s = s * wt[:, :, None, :] + sa[..., None] * bt[:, :, None, :] + vt[..., None] * kt[:, :, None, :]
        y = jnp.einsum('bhij,bhj->bhi', s, rt) if with_out else None
        return s, y

    state, ys = lax.scan(step, state, tuple(time_major(t) for t in (r, w, k, v, a, b)), reverse=reverse)
    return (jnp.moveaxis(ys, 0, 1) if with_out else None), state

def rwkv_mixer(h_l, h_c, mu, w_rkv, w0, w1, w2, a0, a1, a2, g1, g2, k_k, k_a, r_k, lnx_w, lnx_b, w_o, need_ctx):
    lat = rwkv_prepare(h_l, mu, w_rkv, w0, w1, w2, a0, a1, a2, g1, g2, k_k, k_a)
    cxt = rwkv_prepare(h_c, mu, w_rkv, w0, w1, w2, a0, a1, a2, g1, g2, k_k, k_a)
    s0 = jnp.zeros((h_l.shape[0], RW_HEADS, RW_HEAD_DIM, RW_HEAD_DIM), jnp.float32)

    def bidir(p, s_f, s_b, with_out):
        r, k_dir, v, decay, a, b_dir, _ = p
        y_f, s_f = rwkv7_scan(r, decay[0], k_dir[0], v, a, b_dir[0], s_f, False, with_out)
        y_b, s_b = rwkv7_scan(r, decay[1], k_dir[1], v, a, b_dir[1], s_b, True, with_out)
        return y_f, y_b, s_f, s_b

    yc_f, yc_b, st_f, st_b = bidir(cxt, s0, s0, need_ctx)
    yl_f, yl_b, _, _ = bidir(lat, st_f, st_b, True)

    def readout(p, y_f, y_b):
        r, k_dir, v, _, _, _, g = p
        y = y_f + y_b
        mean = jnp.mean(y, axis=-1, keepdims=True)
        var = jnp.mean(jnp.square(y - mean), axis=-1, keepdims=True)
        y = ((y - mean) * lax.rsqrt(var + RW_GN_EPS)).reshape(r.shape) * lnx_w + lnx_b
        coef = jnp.sum(split_heads(r, RW_HEADS, RW_HEAD_DIM)[None] * split_heads(k_dir, RW_HEADS, RW_HEAD_DIM)
                       * split_heads(r_k, RW_HEADS, RW_HEAD_DIM), axis=(0, -1))[..., None]
        bonus = (coef * split_heads(v, RW_HEADS, RW_HEAD_DIM)).reshape(r.shape)
        return ((y + bonus) * g).astype(h_l.dtype) @ w_o

    out_l = readout(lat, yl_f, yl_b)
    out_c = readout(cxt, yc_f, yc_b) if need_ctx else None
    return out_l, out_c

def first_inputs(seed: int = 0) -> dict:
    key = jax.random.key(seed)
    keys = iter(jax.random.split(key, 48))
    n_even = (DEPTH + 1) // 2
    n_odd = DEPTH // 2
    d = D_MODEL

    def normal(shape, scale):
        return scale * jax.random.normal(next(keys), shape, jnp.float32)

    def uniform(shape, lo, hi):
        return jax.random.uniform(next(keys), shape, jnp.float32, lo, hi)

    ab_gate_b = jnp.concatenate([normal((n_even, ML_HEADS), 0.1), uniform((n_even, ML_HEADS), 3.0, 6.0),
                                 normal((n_even, ML_HEADS), 0.1), uniform((n_even, ML_HEADS), 3.0, 6.0)], axis=-1)
    return {
        'x': normal((BATCH, SEQ, d), 1.0),
        'c': normal((BATCH, d), 1.0),
        'ctx': normal((BATCH, CTX_LEN, d), 1.0),
        'c_ctx': normal((d,), 1.0),
        'ada_w': normal((DEPTH, d, 6 * d), 0.5 * d ** -0.5),
        'ada_b': normal((DEPTH, 6 * d), 0.02),
        'ab_w_in': normal((n_even, d, AB_IN_WIDTH), d ** -0.5),
        'ab_gate_b': ab_gate_b,
        'na_q_norm': 1.0 + normal((n_even, NA_HEAD_DIM), 0.05),
        'na_k_norm': 1.0 + normal((n_even, NA_HEAD_DIM), 0.05),
        'na_rpb': normal((n_even, NA_HEADS, 2 * NA_KH - 1, 2 * NA_KW - 1), 0.1),
        'ml_head_norm': 1.0 + normal((n_even, ML_HEADS, ML_HEAD_DIM), 0.05),
        'ab_w_out': normal((n_even, d, d), d ** -0.5),
        'rw_mu': uniform((n_odd, 6, d), 0.0, 1.0),
        'rw_w_rkv': normal((n_odd, 3, d, d), d ** -0.5),
        'rw_w0': uniform((n_odd, 2, d), -6.0, -1.0),
        'rw_w1': normal((n_odd, 2, d, RW_DECAY_LORA), 0.1 * d ** -0.5),
        'rw_w2': normal((n_odd, 2, RW_DECAY_LORA, d), 0.1 * RW_DECAY_LORA ** -0.5),
        'rw_a0': normal((n_odd, 2, d), 0.1),
        'rw_a1': normal((n_odd, 2, d, RW_AAA_LORA), d ** -0.5),
        'rw_a2': normal((n_odd, 2, RW_AAA_LORA, d), 0.5 * RW_AAA_LORA ** -0.5),
        'rw_g1': normal((n_odd, d, RW_GATE_LORA), d ** -0.5),
        'rw_g2': normal((n_odd, RW_GATE_LORA, d), RW_GATE_LORA ** -0.5),
        'rw_k_k': 0.85 + normal((n_odd, d), 0.05),
        'rw_k_a': 1.0 + normal((n_odd, d), 0.05),
        'rw_r_k': normal((n_odd, d), 0.1),
        'rw_lnx_w': 1.0 + normal((n_odd, d), 0.05),
        'rw_lnx_b': normal((n_odd, d), 0.02),
        'rw_w_o': normal((n_odd, d, d), d ** -0.5),
        'mlp_w1': normal((DEPTH, d, D_FF), d ** -0.5),
        'mlp_w2': normal((DEPTH, D_FF, d), D_FF ** -0.5),
    }

def first_block(x, c, ctx, c_ctx, ada_w, ada_b, ab_w_in, ab_gate_b, na_q_norm, na_k_norm, na_rpb, ml_head_norm,
              ab_w_out, rw_mu, rw_w_rkv, rw_w0, rw_w1, rw_w2, rw_a0, rw_a1, rw_a2, rw_g1, rw_g2, rw_k_k, rw_k_a,
              rw_r_k, rw_lnx_w, rw_lnx_b, rw_w_o, mlp_w1, mlp_w2):
    ang_r, ang_c = axial_rope_angles(x.shape[1], ML_HEAD_DIM)
    for layer in range(DEPTH):
        need_ctx = layer < DEPTH - 1
        j = layer // 2
        sh_a, sc_a, gt_a, sh_m, sc_m, gt_m = adaln(c[:, None, :], ada_w[layer], ada_b[layer])
        csh_a, csc_a, cgt_a, csh_m, csc_m, cgt_m = adaln(c_ctx, ada_w[layer], ada_b[layer])
        h_l = modulate(x, sh_a, sc_a)
        h_c = modulate(ctx, csh_a, csc_a)
        if layer % 2 == 0:
            o_l, o_c = ab_mixer(h_l, h_c, ab_w_in[j], ab_gate_b[j], na_q_norm[j], na_k_norm[j], na_rpb[j],
                                ml_head_norm[j], ab_w_out[j], ang_r, ang_c, need_ctx)
        else:
            o_l, o_c = rwkv_mixer(h_l, h_c, rw_mu[j], rw_w_rkv[j], rw_w0[j], rw_w1[j], rw_w2[j], rw_a0[j],
                                  rw_a1[j], rw_a2[j], rw_g1[j], rw_g2[j], rw_k_k[j], rw_k_a[j], rw_r_k[j],
                                  rw_lnx_w[j], rw_lnx_b[j], rw_w_o[j], need_ctx)
        x = x + gt_a * o_l
        x = x + gt_m * squared_relu_mlp(modulate(x, sh_m, sc_m), mlp_w1[layer], mlp_w2[layer])
        if need_ctx:
            ctx = ctx + cgt_a * o_c
            ctx = ctx + cgt_m * squared_relu_mlp(modulate(ctx, csh_m, csc_m), mlp_w1[layer], mlp_w2[layer])
    return x


DEPTH_2 = 1

CHUNK = 64
CONV_K = 4
GDN_HEADS = D_MODEL // 128
GDN_DK = 128
GDN_DV = 128
GDN_QK = GDN_HEADS * GDN_DK
GDN_V = GDN_HEADS * GDN_DV
GDN_CONV_CH = 2 * GDN_QK + GDN_V
SSD_P = 64
SSD_HEADS = D_MODEL // SSD_P
SSD_G = 2
SSD_N = 128
SSD_INNER = SSD_HEADS * SSD_P
SSD_BC = SSD_G * SSD_N
SSD_CONV_CH = SSD_INNER + 2 * SSD_BC
MIX_WIDTH = GDN_V + SSD_INNER
IN_WIDTH = GDN_CONV_CH + GDN_V + 2 * GDN_HEADS + SSD_INNER + SSD_CONV_CH + SSD_HEADS
N_EXPERTS = 32
TOP_K = 4
D_FF_2 = D_MODEL
SWIGLU_ALPHA = 1.702
SWIGLU_LIMIT = 7.0
EXPERT_BLOCK = 128
EPS = 1e-6


def rmsnorm(x, g):
    xf = x.astype(jnp.float32)
    y = xf * lax.rsqrt(jnp.mean(xf * xf, axis=-1, keepdims=True) + EPS)
    return (y * g.astype(jnp.float32)).astype(x.dtype)

def l2norm(x):
    return x * lax.rsqrt(jnp.sum(x * x, axis=-1, keepdims=True) + EPS)

def causal_dwconv(x, w):
    k, ch = w.shape
    return lax.conv_general_dilated(x, w[:, None, :], window_strides=(1,), padding=[(k - 1, 0)],
                                    dimension_numbers=("NWC", "WIO", "NWC"), feature_group_count=ch)

def gated_delta_rule_chunked(q, k, v, beta, g):
    bsz, s, h, dk = q.shape
    dv = v.shape[-1]
    nc = s // CHUNK

    def blocks(t):
        return jnp.moveaxis(t.reshape((bsz, nc, CHUNK, h) + t.shape[3:]), 3, 1)

    qc, kc, vc, bc, gc = blocks(q), blocks(k), blocks(v), blocks(beta), blocks(g)
    gam = jnp.cumsum(gc, axis=-1)
    incl = jnp.tril(jnp.ones((CHUNK, CHUNK), bool))
    strict = jnp.tril(jnp.ones((CHUNK, CHUNK), bool), -1)
    decay = jnp.exp(jnp.where(incl, gam[..., :, None] - gam[..., None, :], -jnp.inf))
    kk = jnp.einsum("bhnld,bhnsd->bhnls", kc, kc)
    a_mat = jnp.where(strict, bc[..., :, None] * kk * decay, 0.0) + jnp.eye(CHUNK, dtype=q.dtype)
    rhs = jnp.concatenate([vc * bc[..., None], kc * (bc * jnp.exp(gam))[..., None]], axis=-1)
    sol = lax.linalg.triangular_solve(a_mat, rhs, left_side=True, lower=True, unit_diagonal=True)
    u, w = sol[..., :dv], sol[..., dv:]
    qk = jnp.einsum("bhnld,bhnsd->bhnls", qc, kc) * decay
    q_dec = qc * jnp.exp(gam)[..., None]
    k_dec = kc * jnp.exp(gam[..., -1:] - gam)[..., None]
    chunk_dec = jnp.exp(gam[..., -1])

    def step(state, inp):
        u_i, w_i, qk_i, qd_i, kd_i, cd_i = inp
        v_new = u_i - jnp.einsum("bhld,bhdv->bhlv", w_i, state)
        o_i = jnp.einsum("bhld,bhdv->bhlv", qd_i, state) + jnp.einsum("bhls,bhsv->bhlv", qk_i, v_new)
        state = cd_i[..., None, None] * state + jnp.einsum("bhld,bhlv->bhdv", kd_i, v_new)
        return state, o_i

    xs = (jnp.moveaxis(u, 2, 0), jnp.moveaxis(w, 2, 0), jnp.moveaxis(qk, 2, 0),
          jnp.moveaxis(q_dec, 2, 0), jnp.moveaxis(k_dec, 2, 0), jnp.moveaxis(chunk_dec, 2, 0))
    s0 = jnp.zeros((bsz, h, dk, dv), q.dtype)
    _, o = lax.scan(step, s0, xs)
    return jnp.transpose(o, (1, 0, 3, 2, 4)).reshape(bsz, s, h, dv)

def ssd_chunked(x, dt, a_log, bm, cm):
    bsz, s, h, p = x.shape
    g, n = bm.shape[2], bm.shape[3]
    e = h // g
    nc = s // CHUNK
    a = -jnp.exp(a_log) * dt
    xc = (x * dt[..., None]).reshape(bsz, nc, CHUNK, g, e, p)
    ac = a.reshape(bsz, nc, CHUNK, g, e)
    bc = bm.reshape(bsz, nc, CHUNK, g, n)
    cc = cm.reshape(bsz, nc, CHUNK, g, n)
    a_cum = jnp.cumsum(ac, axis=2)
    incl = jnp.tril(jnp.ones((CHUNK, CHUNK), bool))
    seg = a_cum[:, :, :, None] - a_cum[:, :, None, :]
    decay = jnp.exp(jnp.where(incl[:, :, None, None], seg, -jnp.inf))
    cb = jnp.einsum("bclgn,bcsgn->bclsg", cc, bc)
    y_diag = jnp.einsum("bclsge,bcsgep->bclgep", cb[..., None] * decay, xc)
    states = jnp.einsum("bclgn,bclge,bclgep->bcgepn", bc, jnp.exp(a_cum[:, :, -1:] - a_cum), xc)
    chunk_dec = jnp.exp(a_cum[:, :, -1])

    def step(hs, inp):
        st, cd = inp
        return cd[..., None, None] * hs + st, hs

    h0 = jnp.zeros((bsz, g, e, p, n), x.dtype)
    _, h_prev = lax.scan(step, h0, (jnp.moveaxis(states, 1, 0), jnp.moveaxis(chunk_dec, 1, 0)))
    h_prev = jnp.moveaxis(h_prev, 0, 1)
    y_off = jnp.einsum("bclgn,bcgepn,bclge->bclgep", cc, h_prev, jnp.exp(a_cum))
    return (y_diag + y_off).reshape(bsz, s, h, p)

def hybrid_mixer(h, w_in, gdn_conv_w, gdn_a_log, gdn_dt_bias, gdn_norm_g,
                 ssd_conv_w, ssd_conv_b, ssd_a_log, ssd_dt_bias, ssd_d, ssd_norm_g, w_out):
    bsz, s, _ = h.shape
    f32 = jnp.float32
    proj = h @ w_in
    off = 0
    gdn_qkv = proj[..., off:off + GDN_CONV_CH]; off += GDN_CONV_CH
    gdn_z = proj[..., off:off + GDN_V]; off += GDN_V
    gdn_b = proj[..., off:off + GDN_HEADS]; off += GDN_HEADS
    gdn_a = proj[..., off:off + GDN_HEADS]; off += GDN_HEADS
    ssd_z = proj[..., off:off + SSD_INNER]; off += SSD_INNER
    ssd_xbc = proj[..., off:off + SSD_CONV_CH]; off += SSD_CONV_CH
    ssd_dt = proj[..., off:off + SSD_HEADS]

    qkv = jax.nn.silu(causal_dwconv(gdn_qkv, gdn_conv_w)).astype(f32)
    q = l2norm(qkv[..., :GDN_QK].reshape(bsz, s, GDN_HEADS, GDN_DK)) * (GDN_DK ** -0.5)
    k = l2norm(qkv[..., GDN_QK:2 * GDN_QK].reshape(bsz, s, GDN_HEADS, GDN_DK))
    v = qkv[..., 2 * GDN_QK:].reshape(bsz, s, GDN_HEADS, GDN_DV)
    beta = jax.nn.sigmoid(gdn_b.astype(f32))
    g = -jnp.exp(gdn_a_log.astype(f32)) * jax.nn.softplus(gdn_a.astype(f32) + gdn_dt_bias.astype(f32))
    o = gated_delta_rule_chunked(q, k, v, beta, g)
    o = rmsnorm(o, gdn_norm_g) * jax.nn.silu(gdn_z.astype(f32).reshape(bsz, s, GDN_HEADS, GDN_DV))
    gdn_out = o.reshape(bsz, s, GDN_V).astype(h.dtype)

    xbc = jax.nn.silu(causal_dwconv(ssd_xbc, ssd_conv_w) + ssd_conv_b).astype(f32)
    xs = xbc[..., :SSD_INNER].reshape(bsz, s, SSD_HEADS, SSD_P)
    bm = xbc[..., SSD_INNER:SSD_INNER + SSD_BC].reshape(bsz, s, SSD_G, SSD_N)
    cm = xbc[..., SSD_INNER + SSD_BC:].reshape(bsz, s, SSD_G, SSD_N)
    dt = jax.nn.softplus(ssd_dt.astype(f32) + ssd_dt_bias.astype(f32))
    y = ssd_chunked(xs, dt, ssd_a_log.astype(f32), bm, cm) + ssd_d.astype(f32)[:, None] * xs
    y = y.reshape(bsz, s, SSD_INNER) * jax.nn.silu(ssd_z.astype(f32))
    y = rmsnorm(y.reshape(bsz, s, SSD_G, SSD_INNER // SSD_G),
                ssd_norm_g.reshape(SSD_G, SSD_INNER // SSD_G)).reshape(bsz, s, SSD_INNER)
    ssd_out = y.astype(h.dtype)

    return jnp.concatenate([gdn_out, ssd_out], axis=-1) @ w_out

def clamped_swiglu(gu):
    gate, up = gu[..., :D_FF_2], gu[..., D_FF_2:]
    gate = jnp.minimum(gate, SWIGLU_LIMIT)
    up = jnp.clip(up, -SWIGLU_LIMIT, SWIGLU_LIMIT)
    return (up + 1.0) * (gate * jax.nn.sigmoid(gate * SWIGLU_ALPHA))

def moe_ffn(h, router_w, router_b, w_gu, b_gu, w_down, b_down):
    bsz, s, d = h.shape
    n_tok = bsz * s
    hf = h.reshape(n_tok, d)
    logits = (hf @ router_w + router_b).astype(jnp.float32)
    top_logit, top_idx = lax.top_k(logits, TOP_K)
    gates = jax.nn.softmax(top_logit, axis=-1)
    n_assign = n_tok * TOP_K
    eid = top_idx.reshape(n_assign)
    tok = jnp.arange(n_assign, dtype=jnp.int32) // TOP_K
    order = jnp.argsort(eid)
    eid_s = eid[order]
    counts = jnp.bincount(eid, length=N_EXPERTS)
    padded = (counts + EXPERT_BLOCK - 1) // EXPERT_BLOCK * EXPERT_BLOCK
    pad_end = jnp.cumsum(padded)
    pad_start = pad_end - padded
    start = jnp.cumsum(counts) - counts
    dest = pad_start[eid_s] + jnp.arange(n_assign, dtype=jnp.int32) - start[eid_s]
    n_rows = (-(-n_assign // EXPERT_BLOCK) + N_EXPERTS) * EXPERT_BLOCK
    n_blocks = n_rows // EXPERT_BLOCK
    row_tok = jnp.full((n_rows,), n_tok, jnp.int32).at[dest].set(tok[order])
    row_gate = jnp.zeros((n_rows,), jnp.float32).at[dest].set(gates.reshape(n_assign)[order])
    blk_start = jnp.arange(n_blocks, dtype=jnp.int32) * EXPERT_BLOCK
    blk_expert = jnp.minimum(jnp.searchsorted(pad_end, blk_start, side="right"), N_EXPERTS - 1)
    h_pad = jnp.concatenate([hf, jnp.zeros((1, d), hf.dtype)], axis=0)
    x_rows = h_pad[row_tok].reshape(n_blocks, EXPERT_BLOCK, d)

    def expert_block(args):
        xb, e = args
        y = clamped_swiglu(xb @ w_gu[e] + b_gu[e])
        return y @ w_down[e] + b_down[e]

    y_rows = lax.map(expert_block, (x_rows, blk_expert)).reshape(n_rows, d)
    y_rows = y_rows * row_gate[:, None].astype(y_rows.dtype)
    out = jax.ops.segment_sum(y_rows, row_tok, num_segments=n_tok + 1)[:n_tok]
    return out.reshape(bsz, s, d)

def second_inputs(seed: int = 0) -> dict:
    key = jax.random.key(seed)
    ks = jax.random.split(key, 26)
    f32 = jnp.float32
    L = DEPTH_2

    def nrm(k, shape, scale):
        return jax.random.normal(k, shape, f32) * scale

    def a_log_init(k, h):
        return jnp.log(jax.random.uniform(k, (L, h), f32, minval=1.0, maxval=16.0))

    def dt_bias_init(k, h):
        dt = jnp.exp(jax.random.uniform(k, (L, h), f32, minval=math.log(1e-3), maxval=math.log(1e-1)))
        return dt + jnp.log(-jnp.expm1(-dt))

    return {
        "x": nrm(ks[0], (BATCH, SEQ, D_MODEL), 1.0),
        "c": nrm(ks[1], (BATCH, D_MODEL), 1.0),
        "ada_w": nrm(ks[2], (L, D_MODEL, 6 * D_MODEL), 0.5 * D_MODEL ** -0.5),
        "ada_b": nrm(ks[3], (L, 6 * D_MODEL), 0.02),
        "norm1_g": 1.0 + nrm(ks[4], (L, D_MODEL), 0.02),
        "norm2_g": 1.0 + nrm(ks[5], (L, D_MODEL), 0.02),
        "w_in": nrm(ks[6], (L, D_MODEL, IN_WIDTH), D_MODEL ** -0.5),
        "gdn_conv_w": nrm(ks[7], (L, CONV_K, GDN_CONV_CH), CONV_K ** -0.5),
        "gdn_a_log": a_log_init(ks[8], GDN_HEADS),
        "gdn_dt_bias": dt_bias_init(ks[9], GDN_HEADS),
        "gdn_norm_g": 1.0 + nrm(ks[10], (L, GDN_DV), 0.02),
        "ssd_conv_w": nrm(ks[11], (L, CONV_K, SSD_CONV_CH), CONV_K ** -0.5),
        "ssd_conv_b": nrm(ks[12], (L, SSD_CONV_CH), 0.02),
        "ssd_a_log": a_log_init(ks[13], SSD_HEADS),
        "ssd_dt_bias": dt_bias_init(ks[14], SSD_HEADS),
        "ssd_d": 1.0 + nrm(ks[15], (L, SSD_HEADS), 0.02),
        "ssd_norm_g": 1.0 + nrm(ks[16], (L, SSD_INNER), 0.02),
        "w_out": nrm(ks[17], (L, MIX_WIDTH, D_MODEL), MIX_WIDTH ** -0.5),
        "router_w": nrm(ks[18], (L, D_MODEL, N_EXPERTS), D_MODEL ** -0.5),
        "router_b": nrm(ks[19], (L, N_EXPERTS), 0.01),
        "moe_w_gu": nrm(ks[20], (L, N_EXPERTS, D_MODEL, 2 * D_FF_2), D_MODEL ** -0.5),
        "moe_b_gu": nrm(ks[21], (L, N_EXPERTS, 2 * D_FF_2), 0.01),
        "moe_w_down": nrm(ks[22], (L, N_EXPERTS, D_FF_2, D_MODEL), D_FF_2 ** -0.5),
        "moe_b_down": nrm(ks[23], (L, N_EXPERTS, D_MODEL), 0.01),
        "final_g": 1.0 + nrm(ks[24], (D_MODEL,), 0.02),
    }

def second_block(x, c, ada_w, ada_b, norm1_g, norm2_g, w_in, gdn_conv_w, gdn_a_log, gdn_dt_bias,
              gdn_norm_g, ssd_conv_w, ssd_conv_b, ssd_a_log, ssd_dt_bias, ssd_d, ssd_norm_g, w_out,
              router_w, router_b, moe_w_gu, moe_b_gu, moe_w_down, moe_b_down, final_g):
    c_act = jax.nn.silu(c)
    for l in range(DEPTH_2):
        mod = (c_act @ ada_w[l] + ada_b[l])[:, None, :]
        sh1, sc1, g1, sh2, sc2, g2 = jnp.split(mod, 6, axis=-1)
        h = rmsnorm(x, norm1_g[l]) * (1.0 + sc1) + sh1
        x = x + g1 * hybrid_mixer(h, w_in[l], gdn_conv_w[l], gdn_a_log[l], gdn_dt_bias[l], gdn_norm_g[l],
                                  ssd_conv_w[l], ssd_conv_b[l], ssd_a_log[l], ssd_dt_bias[l], ssd_d[l],
                                  ssd_norm_g[l], w_out[l])
        h = rmsnorm(x, norm2_g[l]) * (1.0 + sc2) + sh2
        x = x + g2 * moe_ffn(h, router_w[l], router_b[l], moe_w_gu[l], moe_b_gu[l],
                             moe_w_down[l], moe_b_down[l])
    return rmsnorm(x, final_g)


_first_inputs = second_inputs


def second_inputs(seed=0):
    import zlib

    import numpy as np

    out = dict(_first_inputs(seed))
    spreads = {}
    factors = {'norm1_g': 4.599,
     'norm2_g': 3.792,
     'gdn_norm_g': 8.0,
     'ssd_conv_b': 7.33,
     'ssd_d': 8.0,
     'ssd_norm_g': 8.0,
     'router_b': 5.266,
     'moe_b_gu': 8.0,
     'moe_b_down': 8.0,
     'final_g': 2.864}
    for name, (base, spread) in spreads.items():
        noise = np.random.default_rng([zlib.crc32(name.encode()), seed]).standard_normal(out[name].shape)
        drawn = base * np.exp(spread * noise) if base else spread * noise
        out[name] = jnp.asarray(drawn.astype(out[name].dtype))
    for name, factor in factors.items():
        out[name] = (out[name] * factor).astype(out[name].dtype)
    return out


_narrow_inputs = second_inputs


def second_inputs(seed=0):

    out = dict(_narrow_inputs(seed))
    wider = {'ssd_conv_b': 4.25,
     'ssd_d': 12.0,
     'ssd_norm_g': 7.8,
     'router_b': 3.57,
     'moe_b_gu': 6.16,
     'moe_b_down': 12.0,
     'final_g': 3.3}
    for name, times in wider.items():
        mean = out[name].mean()
        out[name] = (mean + times * (out[name] - mean)).astype(out[name].dtype)
    return out


def setup_inputs(seed=0):
    out = dict(first_inputs(seed))
    for name, value in second_inputs(seed + 1).items():
        if name != "x":
            out[name + "_2"] = value
    return out


def reference(
    x, c, ctx, c_ctx, ada_w, ada_b, ab_w_in, ab_gate_b, na_q_norm, na_k_norm, na_rpb,
    ml_head_norm, ab_w_out, rw_mu, rw_w_rkv, rw_w0, rw_w1, rw_w2, rw_a0, rw_a1, rw_a2, rw_g1,
    rw_g2, rw_k_k, rw_k_a, rw_r_k, rw_lnx_w, rw_lnx_b, rw_w_o, mlp_w1, mlp_w2, c_2, ada_w_2,
    ada_b_2, norm1_g_2, norm2_g_2, w_in_2, gdn_conv_w_2, gdn_a_log_2, gdn_dt_bias_2,
    gdn_norm_g_2, ssd_conv_w_2, ssd_conv_b_2, ssd_a_log_2, ssd_dt_bias_2, ssd_d_2, ssd_norm_g_2,
    w_out_2, router_w_2, router_b_2, moe_w_gu_2, moe_b_gu_2, moe_w_down_2, moe_b_down_2,
    final_g_2,
):
    x = first_block(
        x, c, ctx, c_ctx, ada_w, ada_b, ab_w_in, ab_gate_b, na_q_norm, na_k_norm, na_rpb,
        ml_head_norm, ab_w_out, rw_mu, rw_w_rkv, rw_w0, rw_w1, rw_w2, rw_a0, rw_a1, rw_a2,
        rw_g1, rw_g2, rw_k_k, rw_k_a, rw_r_k, rw_lnx_w, rw_lnx_b, rw_w_o, mlp_w1, mlp_w2,
    )
    return second_block(
        x, c_2, ada_w_2, ada_b_2, norm1_g_2, norm2_g_2, w_in_2, gdn_conv_w_2, gdn_a_log_2,
        gdn_dt_bias_2, gdn_norm_g_2, ssd_conv_w_2, ssd_conv_b_2, ssd_a_log_2, ssd_dt_bias_2,
        ssd_d_2, ssd_norm_g_2, w_out_2, router_w_2, router_b_2, moe_w_gu_2, moe_b_gu_2,
        moe_w_down_2, moe_b_down_2, final_g_2,
    )


_drawn_inputs = setup_inputs


def setup_inputs(seed=0):
    import zlib

    import numpy as np

    out = dict(_drawn_inputs(seed))
    spreads = {}
    factors = {'na_q_norm': 8.0,
     'na_k_norm': 8.0,
     'na_rpb': 8.0,
     'ml_head_norm': 3.933,
     'rw_w1': 8.0,
     'rw_w2': 8.0,
     'rw_a0': 3.806,
     'rw_lnx_w': 3.173,
     'rw_lnx_b': 6.42,
     'norm2_g_2': 3.041,
     'ssd_d_2': 8.0}
    for name, (base, spread) in spreads.items():
        noise = np.random.default_rng([zlib.crc32(name.encode()), seed]).standard_normal(out[name].shape)
        drawn = base * np.exp(spread * noise) if base else spread * noise
        out[name] = jnp.asarray(drawn.astype(out[name].dtype))
    for name, factor in factors.items():
        out[name] = (out[name] * factor).astype(out[name].dtype)
    return out
```

```python
import math
from contextlib import ExitStack

import numpy as np

import concourse.bass as bass
from concourse import mybir

F32 = mybir.dt.float32
U32 = mybir.dt.uint32
ALU = mybir.AluOpType
ACT = mybir.ActivationFunctionType
AX = mybir.AxisListType

P = 128
D = 1024
KT = D // P
TT = 4
CTX_TILES = (0, 1)
LAT_TILES = (2, 3)
ALL_TILES = (0, 1, 2, 3)
EPS = 1e-6
SLOTS = 3
SLOT = KT * 512

NA_H, NA_D = 8, 64
ML_H, ML_D = 4, 128
AB_W = 3 * 512 + 4 * 512 + 16
GRID_W, NA_KW, NA_KH = 64, 16, 8
GATE_CAP = 15.0
RW_H, RW_D = 16, 64
GN_EPS = 64e-5
G_LORA = 160
D_FF = 4096
GD_H = 8
SS_H, SS_P, SS_G = 16, 64, 2
CONV_CH_Q = 3072
CONV_CH_S = 1536
N_EXP, TOP_K = 32, 4
SWI_ALPHA, SWI_LIMIT = 1.702, 7.0
LEVELS = 7

C_ID, C_UP, C_UPS, C_LO, C_LOS, C_ONE = range(6)
C_LVL = 6
N_BLOCKS = 6 + 2 * LEVELS


def const_table():
    r, c = np.arange(P)[:, None], np.arange(P)[None, :]
    blocks = [r == c, r <= c, r < c, r >= c, r > c, r >= 0 * c]
    lower = []
    for level in range(LEVELS):
        b = 1 << level
        lower.append((r // (2 * b) == c // (2 * b)) & (r % (2 * b) >= b) & (c % (2 * b) < b))
    blocks += lower + [m.T for m in lower]
    return np.concatenate([np.broadcast_to(b, (P, P)) for b in blocks], axis=1).astype(np.float32)


def rope_table():
    pos = np.arange(256)
    inv = (np.float32(10000.0) ** (-np.arange(32, dtype=np.float32) / 32)).astype(np.float32)
    out = np.zeros((256, 2, ML_D), np.float32)
    for half, p in enumerate((pos // GRID_W, pos % GRID_W)):
        ang = p.astype(np.float32)[:, None] * inv
        o = 64 * half
        out[:, 0, o:o + 32] = out[:, 0, o + 32:o + 64] = np.cos(ang)
        out[:, 1, o:o + 32], out[:, 1, o + 32:o + 64] = -np.sin(ang), np.sin(ang)
    return np.ascontiguousarray(out.reshape(2, P, 2, ML_D).transpose(1, 0, 2, 3))


def window_table():
    c = np.arange(GRID_W)
    start = np.clip(c - NA_KW // 2, 0, GRID_W - NA_KW)[:, None]
    ok = (c[None, :] >= start) & (c[None, :] < start + NA_KW)
    return np.where(ok, 0.0, -1e30).astype(np.float32)


class Take:

    def __init__(self, eng):
        self.eng = eng
        self.n = {}

    def __call__(self, sem, k=1):
        self.n[sem.name] = self.n.get(sem.name, 0) + k
        self.eng.wait_ge(sem, self.n[sem.name])

    def skip_first(self, sem, first, k=1):
        seen = self.n.get("uses " + sem.name, 0)
        self.n["uses " + sem.name] = seen + 1
        if seen >= first:
            self(sem, k)


class Phase:

    def __init__(self, g, name):
        self.g, self.nc, self.name = g, g.nc, name
        self.stack = ExitStack()
        self.sems = []

    def __enter__(self):
        self.stack.__enter__()
        return self

    def sb(self, name, shape, dt=F32):
        return self.stack.enter_context(self.nc.sbuf_tensor(f"{self.name}_{name}", shape, dt))

    def ps(self, name, shape, dt=F32):
        return self.stack.enter_context(self.nc.psum_tensor(f"{self.name}_psum_{name}", shape, dt))

    def sem(self, name):
        s = self.nc.alloc_semaphore(f"{self.name}_{name}")
        self.sems.append(s)
        return s

    def __exit__(self, *a):
        if a[0] is None:
            self.nc.clear_and_free_semaphores(self.sems)
            self.nc.all_engine_barrier()
        return self.stack.__exit__(*a)


class Chain:

    def __init__(self, eng, sem):
        self.eng, self.sem, self.n = eng, sem, 0

    def mark(self, ins):
        self.n += 1
        ins.then_inc(self.sem, 1)

    def wait(self):
        if self.n:
            self.eng.wait_ge(self.sem, self.n)

    def link(self, ins):
        self.mark(ins)
        self.wait()


class Ring:

    def __init__(self, nc):
        self.nc = nc
        self.buf = nc.alloc_sbuf_tensor("ring", [P, SLOTS, SLOT], F32)
        self.loaded = [nc.alloc_semaphore(f"ring_loaded_{i}") for i in range(SLOTS)]
        self.gemm_done = nc.alloc_semaphore("gemm_done")
        self.plan, self.after = [], []
        self.issued = 0
        self.used = 0
        self.done = 0

    def add(self, src, units):
        self.plan.append(src)
        self.after.append((self.after[-1] if self.after else 0) + units)

    def view(self, i):
        a, b = self.plan[i].shape[1:]
        return self.buf[:, i % SLOTS, 0:a * b].rearrange("p (a b) -> p a b", a=a)

    def issue(self, sync, n):
        end = min(self.base_of_phase + n + SLOTS, len(self.plan))
        while self.issued < end:
            i = self.issued
            if i >= SLOTS:
                sync.wait_ge(self.gemm_done, self.after[i - SLOTS])
            sync.dma_start(self.view(i), self.plan[i]).then_inc(self.loaded[i % SLOTS], 16)
            self.issued += 1

    @property
    def base_of_phase(self):
        return self.used

    def take(self, pe):
        i = self.used
        pe.wait_ge(self.loaded[i % SLOTS], 16 * (i // SLOTS + 1))
        self.used += 1
        return self.view(i)

    def mark(self, ins):
        ins.then_inc(self.gemm_done, 1)
        self.done += 1


class G:
    pass


def blk(g, i):
    return g.const[:, i * P:(i + 1) * P]


def rep(ap, n, at=1):
    x = ap.unsqueeze(at)
    shape = list(x.shape)
    shape[at] = n
    return x.to_broadcast(shape)


def gemm_tok(g, name, chunks, xT, tiles, out, waits_done=None):
    nc, ring = g.nc, g.ring
    with Phase(g, name) as ph:
        banks = ph.ps("bank", [P, 8, 512])
        evac = ph.sem("evacuated")
        own = ph.sem("vector_chain")
        ph.extra = waits_done
        with nc.Block() as block:
            done0 = ring.done

            @block.sync
            def _(sync):
                ring.issue(sync, len(chunks))

            @block.tensor
            def _(pe):
                n = 0
                for w in chunks:
                    wv = ring.take(pe)
                    for t in tiles:
                        if n >= 8:
                            pe.wait_ge(evac, n - 7)
                        for kt in range(wv.shape[1]):
                            mm = nc.tensor.matmul(banks[:, n % 8, 0:w], xT(kt, t), wv[:, kt, :],
                                                  start=(kt == 0), stop=(kt == wv.shape[1] - 1))
                        ring.mark(mm)
                        n += 1

            @block.vector
            def _(dve):
                ch = Chain(dve, own)
                n, c0 = 0, 0
                for w in chunks:
                    for t in tiles:
                        dve.wait_ge(ring.gemm_done, done0 + n + 1)
                        out(ch, t, c0, w, banks[:, n % 8, 0:w]).then_inc(evac, 1)
                        n += 1
                    c0 += w


def widths(n):
    return [min(512, n - c) for c in range(0, n, 512)]


def plan_cols(ring, w, n_cols, units):
    wv = w.rearrange("(a p) n -> p a n", p=P)
    c = 0
    for wd in widths(n_cols):
        ring.add(wv[:, :, c:c + wd], units)
        c += wd


def plan_rows(ring, w, units):
    wv = w.rearrange("(a p) n -> p a n", p=P)
    for a in range(0, wv.shape[1], 4):
        ring.add(wv[:, a:a + 4, :], units)


def adaln(g, name, cond, bias, mod):
    nc, ring = g.nc, g.ring
    with Phase(g, name) as ph:
        c = ph.sb("cond", [P, KT, 2])
        sc = ph.sb("silu", [P, KT, 2])
        b = ph.sb("bias", [P, 48])
        ps = ph.ps("mod", [P, 48, 2])
        s_in, s_silu, own = ph.sem("loaded"), ph.sem("silu"), ph.sem("chain")
        with nc.Block() as block:
            done0 = ring.done

            @block.sync
            def _(sync):
                sync.dma_start(c[:, :, :], cond).then_inc(s_in, 16)
                sync.dma_start(b[:, :], bias).then_inc(s_in, 16)
                ring.issue(sync, 12)

            @block.scalar
            def _(act):
                act.wait_ge(s_in, 32)
                nc.scalar.activation(sc[:, :, :], c[:, :, :], ACT.Sigmoid).then_inc(own, 1)

            @block.vector
            def _(dve):
                dve.wait_ge(own, 1)
                dve.wait_ge(s_in, 32)
                nc.vector.tensor_tensor(sc[:, :, :], sc[:, :, :], c[:, :, :], ALU.mult).then_inc(s_silu, 1)
                dve.wait_ge(ring.gemm_done, done0 + 12)
                nc.vector.tensor_tensor(mod[:, :, :], ps[:, :, :], rep(b[:, :], 2, 2), ALU.add).then_inc(own, 1)
                dve.wait_ge(own, 2)

            @block.tensor
            def _(pe):
                pe.wait_ge(s_silu, 1)
                for n in range(12):
                    wv = ring.take(pe)
                    for f in range(4):
                        for kt in range(KT):
                            mm = nc.tensor.matmul(ps[:, 4 * n + f, :], wv[:, kt, f * P:(f + 1) * P], sc[:, kt, :],
                                                  start=(kt == 0), stop=(kt == KT - 1))
                    ring.mark(mm)


def gate_rows(g, name, cols, rows):
    nc = g.nc
    n_vec = len(cols)
    with Phase(g, name) as ph:
        wide = ph.sb("wide", [P, n_vec, KT, P])
        ps = ph.ps("rows", [P, 2 * n_vec, 512])
        s_w, s_mm, own = ph.sem("wide"), ph.sem("row"), ph.sem("chain")
        with nc.Block() as block:
            @block.vector
            def _(dve):
                for i in range(n_vec):
                    for kt in range(KT):
                        nc.vector.tensor_scalar(wide[:, i, kt, :], blk(g, C_ONE), cols[i](kt), None,
                                                ALU.mult).then_inc(s_w, 1)
                for i in range(2 * n_vec):
                    dve.wait_ge(s_mm, i + 1)
                    nc.vector.tensor_copy(rows[:, i // 2, (i % 2) * 512:(i % 2) * 512 + 512],
                                          ps[:, i, :]).then_inc(own, 1)
                dve.wait_ge(own, 2 * n_vec)

            @block.tensor
            def _(pe):
                for i in range(2 * n_vec):
                    for j in range(4):
                        kt = (i % 2) * 4 + j
                        pe.wait_ge(s_w, (i // 2) * KT + kt + 1)
                        mm = nc.tensor.matmul(ps[:, i, j * P:(j + 1) * P], wide[:, i // 2, kt, :], blk(g, C_ID),
                                              start=True, stop=True)
                    mm.then_inc(s_mm, 1)


def norm_T(g, name, tiles, dst, scale, shift, gain=None, off=0):
    nc = g.nc
    with Phase(g, name) as ph:
        sq = ph.sb("square", [P, D])
        xn = ph.sb("normed", [P, 2, D])
        ss = ph.sb("sums", [P, 4, TT])
        sp = ph.sb("scale1", [P, TT, KT])
        ps = ph.ps("turned", [P, 4, 512])
        s_ss, s_rt, s_ms = ph.sem("sum"), ph.sem("root"), ph.sem("mean")
        s_xn, s_tr, s_ev, own = ph.sem("normed"), ph.sem("turned"), ph.sem("evacuated"), ph.sem("chain")
        s_sc = ph.sem("act_chain")
        with nc.Block() as block:
            def drain(dve, i):
                t = tiles[i]
                for kt in range(KT):
                    dve.wait_ge(s_tr, 2 * i + kt // 4 + 1)
                    nc.vector.tensor_scalar(dst[:, kt, (t - off) * P:(t - off + 1) * P],
                                            ps[:, (2 * i + kt // 4) % 4, (kt % 4) * P:(kt % 4 + 1) * P],
                                            sp[:, i, kt:kt + 1], shift(t)[:, kt:kt + 1], ALU.mult, ALU.add)\
                        .then_inc(s_ev, 1)

            @block.scalar
            def _(act):
                for i, t in enumerate(tiles):
                    nc.scalar.activation(sq[:, :], g.x[:, t, :], ACT.Square, accum_out=ss[:, 0, i:i + 1])\
                        .then_inc(s_ss, 1)
                    act.wait_ge(s_ss, i + 1)
                act.wait_ge(s_ms, 1)
                nc.scalar.activation(ss[:, 2, 0:len(tiles)], ss[:, 1, 0:len(tiles)], ACT.Sqrt).then_inc(s_rt, 1)

            @block.vector
            def _(dve):
                ch = Chain(dve, own)
                n = len(tiles)
                for i, t in enumerate(tiles):
                    ch.link(nc.vector.tensor_scalar(sp[:, i, :], scale(t), 1.0, None, ALU.add))
                    if gain is not None:
                        ch.link(nc.vector.tensor_tensor(sp[:, i, :], sp[:, i, :], gain, ALU.mult))
                dve.wait_ge(s_ss, n)
                nc.vector.tensor_scalar(ss[:, 1, 0:n], ss[:, 0, 0:n], 1.0 / D, EPS, ALU.mult, ALU.add)\
                    .then_inc(s_ms, 1)
                dve.wait_ge(s_rt, 1)
                ch.link(nc.vector.reciprocal(ss[:, 3, 0:n], ss[:, 2, 0:n]))
                for i, t in enumerate(tiles):
                    if i >= 2:
                        dve.wait_ge(s_tr, 2 * (i - 1))
                    nc.vector.tensor_scalar(xn[:, i % 2, :], g.x[:, t, :], ss[:, 3, i:i + 1], None, ALU.mult)\
                        .then_inc(s_xn, 1)
                    if i >= 1:
                        drain(dve, i - 1)
                drain(dve, n - 1)
                dve.wait_ge(s_ev, KT * n)

            @block.tensor
            def _(pe):
                for i, t in enumerate(tiles):
                    pe.wait_ge(s_xn, i + 1)
                    if i >= 2:
                        pe.wait_ge(s_ev, KT * (i - 1))
                    for kt in range(KT):
                        mm = nc.tensor.transpose(ps[:, (2 * i + kt // 4) % 4, (kt % 4) * P:(kt % 4 + 1) * P],
                                                 xn[:, i % 2, kt * P:(kt + 1) * P], blk(g, C_ID))
                        if kt % 4 == 3:
                            mm.then_inc(s_tr, 1)


def turn(g, name, jobs, after=None):
    nc = g.nc
    with Phase(g, name) as ph:
        ps = ph.ps("turned", [P, 8, 512])
        s_tr, s_ev, s_ev2 = ph.sem("turned"), ph.sem("vector_evac"), ph.sem("scalar_evac")
        groups = [jobs[i:i + 4] for i in range(0, len(jobs), 4)]
        with nc.Block() as block:
            @block.tensor
            def _(pe):
                for n, grp in enumerate(groups):
                    if n >= 8:
                        pe.wait_ge((s_ev, s_ev2)[n % 2], sum(len(groups[m]) for m in range(n % 2, n - 7, 2)))
                    for j, (src, dst) in enumerate(grp):
                        mm = nc.tensor.transpose(ps[0:src.shape[1], n % 8, j * P:j * P + P], src, blk(g, C_ID))
                    mm.then_inc(s_tr, 1)

            def evacuate(eng, copy, s, parity):
                k = 0
                for n in range(parity, len(groups), 2):
                    eng.wait_ge(s_tr, n + 1)
                    for j, (src, dst) in enumerate(groups[n]):
                        copy(dst, ps[0:src.shape[1], n % 8, j * P:j * P + P]).then_inc(s, 1)
                        k += 1
                if k:
                    eng.wait_ge(s, k)

            @block.vector
            def _(dve):
                evacuate(dve, nc.vector.tensor_copy, s_ev, 0)

            @block.scalar
            def _(act):
                evacuate(act, nc.scalar.copy, s_ev2, 1)


def residual(g, rows, i):
    nc = g.nc

    def out(ch, t, c0, w, ps):
        k = ch.n % 2
        tmp = g.tmp[:, k * 512:k * 512 + w]
        ch.link(nc.vector.tensor_tensor(tmp, ps, rows(t)[:, c0:c0 + w], ALU.mult))
        return nc.vector.tensor_tensor(g.x[:, t, c0:c0 + w], g.x[:, t, c0:c0 + w], tmp, ALU.add)
    return out


def mlp(g, name, tiles, rows):
    nc, ring = g.nc, g.ring
    n_tok = len(tiles) * P
    t0 = tiles[0] * P
    FT = D_FF // P
    with Phase(g, name) as ph:
        hid = ph.sb("hidden", [P, FT, n_tok])
        relu = ph.sb("relu", [P, 4, n_tok])
        banks = ph.ps("bank", [P, 8, 512])
        s_relu, s_sq, own, s_own = ph.sem("relu"), ph.sem("squared"), ph.sem("chain"), ph.sem("evac")
        n_out = 2 * len(tiles)
        done0 = ring.done
        with nc.Block() as block:
            @block.sync
            def _(sync):
                ring.issue(sync, FT // 4 + FT // 4)

            @block.scalar
            def _(act):
                for f in range(FT):
                    act.wait_ge(ring.gemm_done, done0 + f + 1)
                    if f >= 4:
                        act.wait_ge(s_sq, f - 3)
                    nc.scalar.activation(relu[:, f % 4, :], banks[:, f % 8, 0:n_tok], ACT.Relu).then_inc(s_relu, 1)

            @block.vector
            def _(dve):
                ch = Chain(dve, own)
                for f in range(FT):
                    dve.wait_ge(s_relu, f + 1)
                    nc.vector.tensor_tensor(hid[:, f, :], relu[:, f % 4, :], relu[:, f % 4, :], ALU.mult)\
                        .then_inc(s_sq, 1)
                dve.wait_ge(ring.gemm_done, done0 + FT + FT // 4)
                for i in range(n_out):
                    t, c0 = tiles[i // 2], (i % 2) * 512
                    residual(g, rows, 0)(ch, t, c0, 512, banks[:, i, :]).then_inc(s_own, 1)
                dve.wait_ge(s_own, n_out)

            @block.tensor
            def _(pe):
                for n in range(FT // 4):
                    wv = ring.take(pe)
                    for j in range(4):
                        f = 4 * n + j
                        if f >= 8:
                            pe.wait_ge(s_relu, f - 7)
                        for kt in range(KT):
                            mm = nc.tensor.matmul(banks[:, f % 8, 0:n_tok], wv[:, kt, j * P:(j + 1) * P],
                                                  g.xT[:, kt, t0:t0 + n_tok], start=(kt == 0), stop=(kt == KT - 1))
                        ring.mark(mm)
                pe.wait_ge(s_relu, FT)
                for n in range(FT // 4):
                    wv = ring.take(pe)
                    for j in range(4):
                        f = 4 * n + j
                        pe.wait_ge(s_sq, f + 1)
                        for i in range(n_out):
                            mm = nc.tensor.matmul(banks[:, i, :], hid[:, f, (i // 2) * P:(i // 2 + 1) * P],
                                                  wv[:, j, (i % 2) * 512:(i % 2) * 512 + 512],
                                                  start=(f == 0), stop=(f == FT - 1))
                    ring.mark(mm)


def tok_bcast(g, name, loads):
    nc = g.nc
    with Phase(g, name) as ph:
        s = ph.sem("loaded")
        with nc.Block() as block:
            @block.sync
            def _(sync):
                for dst, src in loads:
                    sync.dma_start(dst, src.partition_broadcast(P) if len(src.shape) == 1 else src).then_inc(s, 16)
                sync.wait_ge(s, 16 * len(loads))


def ab_prepare(g, pa, pb, rows, rope, gates):
    nc = g.nc
    with Phase(g, "abprep") as ph:
        sq = ph.sb("square", [P, 2, 512])
        ss = ph.sb("sums", [P, 3, TT * 16])
        t1 = ph.sb("rope1", [P, 512])
        t2 = ph.sb("rope2", [P, 512])
        own = ph.sem("chain")
        s_ms, s_rt, s_g, s_t = ph.sem("mean"), ph.sem("root"), ph.sem("gates"), ph.sem("tanh")
        s_f, s_a = ph.sem("capped"), ph.sem("act_chain")
        with nc.Block() as block:
            @block.vector
            def _(dve):
                ch = Chain(dve, own)
                gate_bias = rows[:, 0:16]
                nc.vector.tensor_tensor(gates[:, :, :], pb[:, :, 2048:2064], rep(gate_bias, TT), ALU.add)\
                    .then_inc(s_g, 1)
                for t in range(TT):
                    for j in range(2):
                        x = pa[:, t, 512 * j:512 * j + 512]
                        ch.link(nc.vector.tensor_tensor(sq[:, j, :], x, x, ALU.mult))
                        o = (2 * t + j) * 8
                        ch.link(nc.vector.tensor_reduce(ss[:, 0, o:o + 8],
                                                        sq[:, j, :].rearrange("p (h d) -> p h d", h=8),
                                                        AX.X, ALU.add))
                nc.vector.tensor_scalar(ss[:, 1, :], ss[:, 0, :], 1.0 / NA_D, EPS, ALU.mult, ALU.add)\
                    .then_inc(s_ms, 1)
                dve.wait_ge(s_t, 1)
                nc.vector.tensor_scalar(gates[:, :, :], gates[:, :, :], GATE_CAP, None, ALU.mult).then_inc(s_f, 1)
                dve.wait_ge(s_rt, 1)
                ch.link(nc.vector.reciprocal(ss[:, 0, :], ss[:, 2, :]))
                for t in range(TT):
                    for j in range(2):
                        x = pa[:, t, 512 * j:512 * j + 512].rearrange("p (h d) -> p h d", h=8)
                        o = (2 * t + j) * 8
                        ch.link(nc.vector.tensor_tensor(x, x, rep(ss[:, 0, o:o + 8], NA_D, 2), ALU.mult))
                        ch.link(nc.vector.tensor_tensor(x, x, rep(rows[:, 16 + 64 * j:80 + 64 * j], 8), ALU.mult))
                    kb = pb[:, t, 512:1024]
                    ch.link(nc.vector.tensor_scalar(kb, kb, ML_D ** -0.5, None, ALU.mult))
                for t in LAT_TILES:
                    for o in (0, 512):
                        x = pb[:, t, o:o + 512]
                        x5 = x.rearrange("p (h a b c) -> p h a b c", h=4, a=2, b=2)
                        y5 = t2[:, :].rearrange("p (h a b c) -> p h a b c", h=4, a=2, b=2)
                        sn = rope[:, t - 2, 1, :].rearrange("p (a b c) -> p a b c", a=2, b=2)
                        ch.mark(nc.vector.tensor_tensor(t1[:, :].rearrange("p (h d) -> p h d", h=4),
                                                        x.rearrange("p (h d) -> p h d", h=4),
                                                        rep(rope[:, t - 2, 0, :], 4), ALU.mult))
                        for a in range(2):
                            for b in range(2):
                                ch.mark(nc.vector.tensor_tensor(y5[:, :, a, b, :], x5[:, :, a, 1 - b, :],
                                                                rep(sn[:, a, b, :], 4), ALU.mult))
                        ch.wait()
                        ch.link(nc.vector.tensor_tensor(x, t1[:, :], t2[:, :], ALU.add))

            @block.scalar
            def _(act):
                act.wait_ge(s_g, 1)
                nc.scalar.activation(gates[:, :, :], gates[:, :, :], ACT.Tanh, scale=1.0 / GATE_CAP).then_inc(s_t, 1)
                act.wait_ge(s_ms, 1)
                nc.scalar.activation(ss[:, 2, :], ss[:, 1, :], ACT.Sqrt).then_inc(s_rt, 1)
                act.wait_ge(s_f, 1)
                for o in (4, 12):
                    nc.scalar.activation(gates[:, :, o:o + 4], gates[:, :, o:o + 4], ACT.Sigmoid).then_inc(s_a, 1)
                act.wait_ge(s_a, 2)
                for o in (4, 12):
                    nc.scalar.activation(gates[:, :, o:o + 4], gates[:, :, o:o + 4], ACT.Ln).then_inc(s_a, 1)
                act.wait_ge(s_a, 4)


def attention(g, proj, qT, kT, cat, rpb_cols, window):
    nc = g.nc
    units = [(h, t) for h in range(NA_H) for t in ALL_TILES]
    scale = NA_D ** -0.5
    with Phase(g, "attn") as ph:
        bm = ph.sb("bias", [P, NA_H, 2, 256])
        win = ph.sb("window", [P, GRID_W])
        pr = ph.sb("probs", [P, 2, 512])
        pT = ph.sb("probsT", [P, 2, 512])
        st = ph.sb("stats", [P, 4, 2])
        S = ph.ps("scores", [P, 2, 512])
        T = ph.ps("turned", [P, 2, 512])
        O = ph.ps("out", [P, 2, 512])
        s_ld, s_bm, s_s, s_mx = ph.sem("loaded"), ph.sem("bias"), ph.sem("scores"), ph.sem("max")
        s_e, s_t, s_tc, s_o, s_ev, own = (ph.sem("exp"), ph.sem("turned"), ph.sem("copied"), ph.sem("out"),
                                          ph.sem("evacuated"), ph.sem("chain"))
        keys = lambda t: 2 if t < 2 else 4
        with nc.Block() as block:
            @block.sync
            def _(sync):
                for half in range(2):
                    sync.dma_start(win[64 * half:64 * half + 64, :], window).then_inc(s_ld, 16)
                for h in range(NA_H):
                    for r in range(4):
                        src = rpb_cols[h, 3 - r:7 - r].rearrange("i c k -> c i k")
                        dst = bm[64 * (r % 2):64 * (r % 2) + 64, h, r // 2, :].rearrange("p (i c) -> p i c", i=4)
                        sync.dma_start(dst, src).then_inc(s_ld, 16)

            @block.vector
            def _(dve):
                ch = Chain(dve, own)
                dve.wait_ge(s_ld, 16 * (2 + 4 * NA_H))
                for h in range(NA_H):
                    v = bm[:, h, :, :].rearrange("p a (i c) -> p (a i) c", i=4)
                    nc.vector.scalar_tensor_tensor(out=v, in0=v, scalar=1.0 / scale, in1=rep(win[:, :], 8),
                                                   op0=ALU.mult, op1=ALU.add).then_inc(s_bm, 1)
                dve.wait_ge(s_bm, NA_H)

                def top(u):
                    h, t = units[u]
                    b, n = u % 2, 128 * keys(t)
                    dve.wait_ge(s_s, u + 1)
                    if t >= 2:
                        lat = S[:, b, 256:512]
                        ch.link(nc.vector.tensor_tensor(lat, lat, bm[:, h, t - 2, :], ALU.add))
                    ch.link(nc.vector.tensor_reduce(st[:, 0, b:b + 1], S[:, b, 0:n], AX.X, ALU.max))
                    nc.vector.tensor_scalar(st[:, 1, b:b + 1], st[:, 0, b:b + 1], -scale, None, ALU.mult)\
                        .then_inc(s_mx, 1)

                def turn_copy(u):
                    h, t = units[u]
                    b, n = u % 2, 128 * keys(t)
                    dve.wait_ge(s_t, u + 1)
                    nc.vector.tensor_copy(pT[:, b, 0:n], T[:, b, 0:n]).then_inc(s_tc, 1)

                def store(u):
                    h, t = units[u]
                    b = u % 2
                    dve.wait_ge(s_o, u + 1)
                    ch.link(nc.vector.reciprocal(st[:, 3, b:b + 1], st[:, 2, b:b + 1]))
                    nc.vector.tensor_scalar(cat[:, t, h * 64:h * 64 + 64], O[:, b, 0:64], st[:, 3, b:b + 1], None,
                                            ALU.mult).then_inc(s_ev, 1)

                for u in range(len(units) + 1):
                    if u < len(units):
                        top(u)
                    if u >= 1:
                        turn_copy(u - 1)
                        store(u - 1)
                dve.wait_ge(s_ev, len(units))

            @block.scalar
            def _(act):
                for u, (h, t) in enumerate(units):
                    b, n = u % 2, 128 * keys(t)
                    act.wait_ge(s_mx, u + 1)
                    if u >= 2:
                        act.wait_ge(s_t, u - 1)
                        act.wait_ge(s_ev, u - 1)
                    nc.scalar.activation(pr[:, b, 0:n], S[:, b, 0:n], ACT.Exp, bias=st[:, 1, b:b + 1], scale=scale,
                                         accum_out=st[:, 2, b:b + 1]).then_inc(s_e, 1)

            @block.tensor
            def _(pe):
                def scores(u):
                    h, t = units[u]
                    b, n, o = u % 2, 128 * keys(t), 64 * (h % 2)
                    if u >= 2:
                        pe.wait_ge(s_e, u - 1)
                    nc.tensor.matmul(S[:, b, 0:n], qT[o:o + 64, h // 2, t * P:(t + 1) * P],
                                     kT[o:o + 64, h // 2, 0:n], start=True, stop=True).then_inc(s_s, 1)

                scores(0)
                for u, (h, t) in enumerate(units):
                    b = u % 2
                    if u + 1 < len(units):
                        scores(u + 1)
                    pe.wait_ge(s_e, u + 1)
                    if u >= 2:
                        pe.wait_ge(s_tc, u - 1)
                    for k in range(keys(t)):
                        mm = nc.tensor.transpose(T[:, b, k * P:(k + 1) * P], pr[:, b, k * P:(k + 1) * P],
                                                 blk(g, C_ID))
                    mm.then_inc(s_t, 1)
                    pe.wait_ge(s_tc, u + 1)
                    if u >= 2:
                        pe.wait_ge(s_ev, u - 1)
                    for k in range(keys(t)):
                        mm = nc.tensor.matmul(O[:, b, 0:64], pT[:, b, k * P:(k + 1) * P],
                                              proj[:, k, 1024 + h * 64:1088 + h * 64],
                                              start=(k == 0), stop=(k == keys(t) - 1))
                    mm.then_inc(s_o, 1)


def mlstm_rows(g, rowg, rowo, cols):
    nc = g.nc
    with Phase(g, "mlrows") as ph:
        F = ph.sb("F", [4, 2, 512])
        Gm = ph.sb("G", [4, 2, 512])
        one = ph.sb("one", [4, 512])
        own = ph.sem("chain")
        with nc.Block() as block:
            @block.vector
            def _(dve):
                ch = Chain(dve, own)
                ch.link(nc.vector.memset(one[:, :], 1.0))

                def scan(dst, src, d, op):
                    if d == 0:
                        ch.link(nc.vector.tensor_tensor_scan(dst[:, 0, :], one[:, :], src, 0.0, ALU.mult, op))
                    else:
                        ch.link(nc.vector.tensor_tensor_scan(dst[:, 1, 0:256][:, ::-1], one[:, 0:256],
                                                             src[:, 0:256][:, ::-1], 0.0, ALU.mult, op))
                        ch.link(nc.vector.tensor_tensor_scan(dst[:, 1, 256:512][:, ::-1], one[:, 0:256],
                                                             src[:, 256:512][:, ::-1], dst[:, 1, 0:1],
                                                             ALU.mult, op))
                for d in range(2):
                    scan(F, rowg[:, 2 * d + 1, :], d, ALU.add)
                    ch.link(nc.vector.tensor_tensor(rowo[:, 2 * d, :], rowg[:, 2 * d, :], F[:, d, :], ALU.subtract))
                    scan(Gm, rowo[:, 2 * d, :], d, ALU.max)
                    ch.link(nc.vector.tensor_tensor(rowo[:, 2 * d + 1, :], F[:, d, :], Gm[:, d, :], ALU.add))
                    ch.link(nc.vector.tensor_scalar(rowo[:, 4 + d, :], Gm[:, d, :], -1.0, None, ALU.mult))


def mlstm(g, proj, qT, kT, rowo, colg, sel, hs):
    nc = g.nc
    blocks = {0: {t: [s for s in range(TT) if s <= t] for t in range(TT)},
              1: {0: [0, 1], 1: [1], 2: [0, 1, 2, 3], 3: [0, 1, 3]}}
    units = [(h, d) for h in range(ML_H) for d in range(2)]
    with Phase(g, "mlstm") as ph:
        v1 = ph.sb("v1", [P, TT, ML_H, 129])
        dec = ph.sb("decay", [P, 2, 512])
        wt = ph.sb("weights", [P, 2, TT, 512])
        em = ph.sb("expm", [P, TT, 2, ML_H])
        den = ph.sb("den", [P, 3, 2, 2])
        raw = ph.ps("raw", [P, 2, 512])
        gb = ph.ps("G", [P, 2, 512])
        out = ph.ps("out", [P, 4, 512])
        s_v, s_em, s_gb, s_raw, s_d, s_x = (ph.sem("v"), ph.sem("em"), ph.sem("Gb"), ph.sem("raw"),
                                            ph.sem("diff"), ph.sem("exp"))
        own_act = ph.sem("act_chain")
        s_m, s_w, s_o, s_ev, own = ph.sem("masked"), ph.sem("weights"), ph.sem("out"), ph.sem("evac"), ph.sem("chain")
        with nc.Block() as block:
            @block.vector
            def _(dve):
                ch = Chain(dve, own)
                for t in range(TT):
                    ch.mark(nc.vector.tensor_copy(v1[:, t, :, 0:128],
                                                  proj[:, t, 1024:1536].rearrange("p (h d) -> p h d", h=4)))
                ch.link(nc.vector.memset(v1[:, :, :, 128:129], 1.0))
                nc.vector.sem_inc(s_v, 1)

                def weights(u):
                    h, d = units[u]
                    for s in range(TT):
                        n = 4 * u + s
                        if s == 0:
                            dve.wait_ge(s_gb, u + 1)
                        if n >= 2:
                            dve.wait_ge(s_m, n - 1)
                        if n >= 2:
                            dve.wait_ge(s_w, n - 1)
                        nc.vector.tensor_scalar(dec[:, n % 2, :], gb[:, u % 2, :], colg[:, s, 2 * d, h:h + 1], 0.0,
                                                ALU.add, ALU.min).then_inc(s_d, 1)
                        if n >= 1:
                            product(n - 1)
                    product(4 * u + 3)

                done = set()

                def product(n):
                    if n in done:
                        return
                    done.add(n)
                    u, s = n // 4, n % 4
                    dve.wait_ge(s_m, n + 1)
                    dve.wait_ge(s_raw, n + 1)
                    if u >= 2:
                        dve.wait_ge(s_o, u - 1)
                    nc.vector.tensor_tensor(wt[:, u % 2, s, :], raw[:, n % 2, :], dec[:, n % 2, :], ALU.mult)\
                        .then_inc(s_w, 1)

                def finish(u):
                    h, d = units[u]
                    dve.wait_ge(s_o, u + 1)
                    if u == 0:
                        dve.wait_ge(s_em, 1)
                    b = 2 * (u % 2)
                    dn = out[:, b:b + 2, 0:258].rearrange("p b (t e) -> p b t e", e=129)[:, :, :, 128]
                    ch.link(nc.vector.tensor_copy(den[:, 0, :, :], dn))
                    ch.link(nc.vector.scalar_tensor_tensor(out=den[:, 1, :, :], in0=den[:, 0, :, :], scalar=-1.0,
                                                           in1=den[:, 0, :, :], op0=ALU.mult, op1=ALU.max))
                    ch.link(nc.vector.tensor_tensor(den[:, 1, :, :], den[:, 1, :, :],
                                                    em[:, :, d, h].rearrange("p (a b) -> p a b", a=2), ALU.max))
                    ch.link(nc.vector.reciprocal(den[:, 2, :, :], den[:, 1, :, :]))
                    for t in range(TT):
                        num = out[:, b + t // 2, (t % 2) * 129:(t % 2) * 129 + 128]
                        r = den[:, 2, t // 2, t % 2:t % 2 + 1]
                        dst = hs[:, t, h * 128:(h + 1) * 128]
                        if d == 0:
                            ch.mark(nc.vector.tensor_scalar(dst, num, r, None, ALU.mult))
                        else:
                            ch.mark(nc.vector.scalar_tensor_tensor(out=dst, in0=num, scalar=r, in1=dst,
                                                                   op0=ALU.mult, op1=ALU.add))
                    ch.wait()
                    nc.vector.sem_inc(s_ev, 1)

                for u in range(len(units)):
                    weights(u)
                    if u >= 1:
                        finish(u - 1)
                finish(len(units) - 1)

            @block.gpsimd
            def _(pool):
                for n in range(4 * len(units)):
                    u, s = n // 4, n % 4
                    h, d = units[u]
                    pool.wait_ge(s_x, n + 1)
                    diagonal = dec[:, n % 2, s * P:(s + 1) * P]
                    nc.gpsimd.tensor_tensor(diagonal, diagonal, blk(g, C_UP if d == 0 else C_LO), ALU.mult)\
                        .then_inc(s_m, 1)

            @block.scalar
            def _(act):
                for d in range(2):
                    nc.scalar.activation(em[:, :, d, :], colg[:, :, 2 * d + 1, :], ACT.Exp, scale=-1.0)\
                        .then_inc(own_act, 1)
                act.wait_ge(own_act, 2)
                nc.scalar.sem_inc(s_em, 1)
                for n in range(4 * len(units)):
                    act.wait_ge(s_d, n + 1)
                    nc.scalar.activation(dec[:, n % 2, :], dec[:, n % 2, :], ACT.Exp).then_inc(s_x, 1)

            @block.tensor
            def _(pe):
                pe.wait_ge(s_v, 1)

                def scores(u):
                    h, d = units[u]
                    if u >= 2:
                        pe.wait_ge(s_d, 4 * (u - 1))
                    nc.tensor.matmul(gb[:, u % 2, :], sel[:, h, :], rowo[:, 4 + d, :], start=True, stop=True)\
                        .then_inc(s_gb, 1)
                    for s in range(TT):
                        n = 4 * u + s
                        if n >= 2:
                            pe.wait_ge(s_w, n - 1)
                        nc.tensor.matmul(raw[:, n % 2, :], kT[:, h, s * P:(s + 1) * P], qT[:, h, :],
                                         start=True, stop=True).then_inc(s_raw, 1)

                def values(u):
                    h, d = units[u]
                    pe.wait_ge(s_w, 4 * u + 4)
                    if u >= 2:
                        pe.wait_ge(s_ev, u - 1)
                    for t in range(TT):
                        ss = blocks[d][t]
                        for s in ss:
                            mm = nc.tensor.matmul(out[:, 2 * (u % 2) + t // 2, (t % 2) * 129:(t % 2) * 129 + 129],
                                                  wt[:, u % 2, s, t * P:(t + 1) * P], v1[:, s, h, :],
                                                  start=(s == ss[0]), stop=(s == ss[-1]))
                    mm.then_inc(s_o, 1)

                for u in range(len(units)):
                    scores(u)
                    values(u)


def ab_merge(g, proj, hs, head_row, cat):
    nc = g.nc
    with Phase(g, "abmerge") as ph:
        sq = ph.sb("square", [P, 512])
        sg = ph.sb("sigmoid", [P, TT, 512])
        ss = ph.sb("sums", [P, 3, TT * ML_H])
        own, s_ms, s_rt, s_sg = ph.sem("chain"), ph.sem("mean"), ph.sem("root"), ph.sem("sigmoid")
        with nc.Block() as block:
            @block.vector
            def _(dve):
                ch = Chain(dve, own)
                for t in range(TT):
                    x = hs[:, t, :]
                    ch.link(nc.vector.tensor_tensor(sq[:, :], x, x, ALU.mult))
                    ch.link(nc.vector.tensor_reduce(ss[:, 0, 4 * t:4 * t + 4],
                                                    sq[:, :].rearrange("p (h d) -> p h d", h=4), AX.X, ALU.add))
                nc.vector.tensor_scalar(ss[:, 1, :], ss[:, 0, :], 1.0 / ML_D, EPS, ALU.mult, ALU.add)\
                    .then_inc(s_ms, 1)
                dve.wait_ge(s_rt, 1)
                ch.link(nc.vector.reciprocal(ss[:, 0, :], ss[:, 2, :]))
                dve.wait_ge(s_sg, TT)
                for t in range(TT):
                    x = hs[:, t, :]
                    ch.link(nc.vector.tensor_tensor(x.rearrange("p (h d) -> p h d", h=4),
                                                    x.rearrange("p (h d) -> p h d", h=4),
                                                    rep(ss[:, 0, 4 * t:4 * t + 4], ML_D, 2), ALU.mult))
                    ch.link(nc.vector.tensor_tensor(x, x, head_row, ALU.mult))
                    ch.link(nc.vector.tensor_tensor(cat[:, t, 512:1024], x, sg[:, t, :], ALU.mult))

            @block.scalar
            def _(act):
                for t in range(TT):
                    nc.scalar.activation(sg[:, t, :], proj[:, t, 1536:2048], ACT.Sigmoid).then_inc(s_sg, 1)
                act.wait_ge(s_ms, 1)
                nc.scalar.activation(ss[:, 2, :], ss[:, 1, :], ACT.Sqrt).then_inc(s_rt, 1)


class Inverse:

    def __init__(self, g, ph):
        self.g, self.nc = g, g.nc
        self.L = [ph.sb(f"L{l}", [P, 4, P]) for l in range(2)]
        self.X = [ph.sb(f"X{l}", [P, 4, P]) for l in range(2)]
        self.Y = [ph.sb(f"Y{l}", [P, 4, P]) for l in range(2)]
        self.T = [ph.sb(f"T{l}", [P, 4, P]) for l in range(2)]
        self.Lo = [ph.sb(f"Lo{l}", [P, 4, P]) for l in range(2)]
        names = ("join", "t_ready", "t_copied", "y_ready", "x_ready", "y_new", "x_new")
        self.s = [{n: ph.sem(f"{n}{l}") for n in names} for l in range(2)]

    def pool(self, take, l_ready, d):
        nc, g = self.nc, self.g
        for k in range(LEVELS):
            mask = blk(g, C_LVL + LEVELS * d + k)
            for l in range(2):
                if k == 0:
                    take(l_ready[l])
                else:
                    take(self.s[l]["t_ready"])
                nc.gpsimd.tensor_tensor(self.Lo[l][:, :, :], self.L[l][:, :, :], rep(mask, 4), ALU.mult)\
                    .then_inc(self.s[l]["join"], 1)
        for l in range(2):
            take(self.s[l]["t_ready"])

    def act(self, take, banks):
        for k in range(LEVELS):
            for l in range(2):
                take(self.s[l]["t_ready"])
                self.nc.scalar.copy(self.T[l][:, :, :], banks[l][:, 0, :].rearrange("p (h c) -> p h c", h=4))\
                    .then_inc(self.s[l]["t_copied"], 1)

    def dve(self, take):
        nc, g = self.nc, self.g

        def add(l, k, dst, bank, ready, new):
            take(self.s[l][ready])
            old = rep(blk(g, C_ID), 4) if k == 0 else dst[:, :, :]
            nc.vector.tensor_tensor(dst[:, :, :], bank.rearrange("p (h c) -> p h c", h=4), old, ALU.add)\
                .then_inc(self.s[l][new], 1)

        def level(k, banks):
            for l in range(2):
                add(l, k, self.Y[l], banks[l][:, 1, :], "y_ready", "y_new")
                if k < LEVELS - 1:
                    add(l, k, self.X[l], banks[l][:, 2, :], "x_ready", "x_new")
        return level

    def pe(self, take, banks):
        nc, g = self.nc, self.g
        for k in range(LEVELS):
            for l in range(2):
                s = self.s[l]
                take(s["join"])
                if k:
                    take(s["y_new"])
                for h in range(4):
                    y = self.Y[l][:, h, :] if k else blk(g, C_ID)
                    mm = nc.tensor.matmul(banks[l][:, 0, h * P:(h + 1) * P], self.Lo[l][:, h, :], y,
                                          start=True, stop=True)
                mm.then_inc(s["t_ready"], 1)
            for l in range(2):
                s = self.s[l]
                take(s["t_copied"])
                if k:
                    take(s["x_new"])
                for h in range(4):
                    x = self.X[l][:, h, :] if k else blk(g, C_ID)
                    mm = nc.tensor.matmul(banks[l][:, 1, h * P:(h + 1) * P], x, self.T[l][:, h, :],
                                          start=True, stop=True)
                mm.then_inc(s["y_ready"], 1)
                if k < LEVELS - 1:
                    for h in range(4):
                        x = self.X[l][:, h, :] if k else blk(g, C_ID)
                        mm = nc.tensor.matmul(banks[l][:, 2, h * P:(h + 1) * P], self.T[l][:, h, :], x,
                                              start=True, stop=True)
                    mm.then_inc(s["x_ready"], 1)
        for l in range(2):
            take(self.s[l]["y_new"])


def rw_shift(g, xx):
    nc = g.nc
    with Phase(g, "rwshift") as ph:
        own = ph.sem("chain")
        with nc.Block() as block:
            @block.vector
            def _(dve):
                ch = Chain(dve, own)
                for kt in range(KT):
                    for s in range(2):
                        h = g.xT[:, kt, 256 * s:256 * s + 256]
                        x = xx[:, kt, 256 * s:256 * s + 256]
                        ch.mark(nc.vector.tensor_tensor(x[:, 1:255], h[:, 0:254], h[:, 2:256], ALU.add))
                        ch.mark(nc.vector.tensor_copy(x[:, 0:1], h[:, 1:2]))
                        ch.mark(nc.vector.tensor_copy(x[:, 255:256], h[:, 254:255]))
                ch.wait()
                for kt in range(KT):
                    ch.mark(nc.vector.scalar_tensor_tensor(out=xx[:, kt, :], in0=xx[:, kt, :], scalar=0.5,
                                                           in1=g.xT[:, kt, :], op0=ALU.mult, op1=ALU.subtract))
                ch.wait()


def rw_mix(g, name, xx, xs, mu):
    nc = g.nc
    with Phase(g, name) as ph:
        own = ph.sem("chain")
        with nc.Block() as block:
            @block.vector
            def _(dve):
                ch = Chain(dve, own)
                for kt in range(KT):
                    ch.mark(nc.vector.scalar_tensor_tensor(out=xs[:, kt, :], in0=xx[:, kt, :],
                                                           scalar=mu[:, kt:kt + 1], in1=g.xT[:, kt, :],
                                                           op0=ALU.mult, op1=ALU.add))
                ch.wait()


def rw_lora(g, name, w, xs, t0, outs, func):
    nc = g.nc
    n_tok = 512 - t0
    width = w.shape[2]
    with Phase(g, name) as ph:
        ws = ph.sb("w", [P, KT, width])
        ps = ph.ps("low", [P, 2, 512])
        s_ld, s_mm, own = ph.sem("loaded"), ph.sem("product"), ph.sem("chain")
        with nc.Block() as block:
            @block.sync
            def _(sync):
                sync.dma_start(ws[:, :, :], w).then_inc(s_ld, 16)

            @block.tensor
            def _(pe):
                pe.wait_ge(s_ld, 16)
                for i, (a, b, dst) in enumerate(outs):
                    for kt in range(KT):
                        mm = nc.tensor.matmul(ps[0:b - a, i, 0:n_tok], ws[:, kt, a:b], xs[:, kt, t0:512],
                                              start=(kt == 0), stop=(kt == KT - 1))
                    mm.then_inc(s_mm, 1)

            @block.scalar
            def _(act):
                for i, (a, b, dst) in enumerate(outs):
                    act.wait_ge(s_mm, i + 1)
                    nc.scalar.activation(dst, ps[0:b - a, i, 0:n_tok], func).then_inc(own, 1)
                act.wait_ge(own, len(outs))


def rw_kk(g, stage, kk, row):
    nc = g.nc
    with Phase(g, "rwkk") as ph:
        sq = ph.sb("square", [P, D])
        ss = ph.sb("sums", [P, 2, TT * RW_H])
        own, s_ss, s_rt = ph.sem("chain"), ph.sem("sum"), ph.sem("root")
        with nc.Block() as block:
            @block.vector
            def _(dve):
                ch = Chain(dve, own)
                for t in range(TT):
                    ch.link(nc.vector.tensor_tensor(kk[:, t, :], stage[:, t, :], row, ALU.mult))
                    ch.link(nc.vector.tensor_tensor(sq[:, :], kk[:, t, :], kk[:, t, :], ALU.mult))
                    ch.link(nc.vector.tensor_reduce(ss[:, 0, RW_H * t:RW_H * (t + 1)],
                                                    sq[:, :].rearrange("p (h d) -> p h d", h=RW_H), AX.X, ALU.add))
                nc.vector.sem_inc(s_ss, 1)
                dve.wait_ge(s_rt, 1)
                ch.link(nc.vector.tensor_scalar(ss[:, 1, :], ss[:, 1, :], 1e-12, None, ALU.max))
                ch.link(nc.vector.reciprocal(ss[:, 0, :], ss[:, 1, :]))
                for t in range(TT):
                    v = kk[:, t, :].rearrange("p (h d) -> p h d", h=RW_H)
                    ch.mark(nc.vector.tensor_tensor(v, v, rep(ss[:, 0, RW_H * t:RW_H * (t + 1)], RW_D, 2), ALU.mult))
                ch.wait()

            @block.scalar
            def _(act):
                act.wait_ge(s_ss, 1)
                nc.scalar.activation(ss[:, 1, :], ss[:, 0, :], ACT.Sqrt).then_inc(s_rt, 1)


def store(g, name, jobs):
    nc = g.nc
    with Phase(g, name) as ph:
        s = ph.sem("stored")
        with nc.Block() as block:
            @block.sync
            def _(sync):
                for dst, src in jobs:
                    sync.dma_start(dst, src).then_inc(s, 16)
                sync.wait_ge(s, 16 * len(jobs))


DECAY = math.exp(-0.5)


def rw_chunks(g, scr, low_w, low_a, w2, a2, rows, y, coef):
    nc = g.nc
    with Phase(g, "rwkv") as ph:
        ld = ph.sb("loaded", [P, 4, D])
        K_, V_, KK_, R_ = range(4)
        bt = ph.sb("B", [P, D])
        kt_ = ph.sb("K", [P, D])
        at = ph.sb("A", [P, D])
        rt = g.tmp
        tr = g.xT[:, :, :].rearrange("p a b -> p (a b)").rearrange("p (q a b) -> p q a b", q=4, a=KT)
        st = ph.sb("state", [P, KT, RW_D])
        pc = ph.sb("chunk_decay", [P, KT, 2])
        inv = Inverse(g, ph)
        mat = [ph.sb(f"mat{l}", [P, 3, 512]) for l in range(2)]
        rhs = [ph.sb(f"rhs{l}", [P, 256]) for l in range(2)]
        us = [ph.sb(f"U{l}", [P, 256]) for l in range(2)]
        banks = [ph.ps(f"lane{l}", [P, 4, 512]) for l in range(2)]
        n = lambda x: ph.sem(x)
        s_ld, s_free = n("loaded"), n("chunk_done")
        s_wl, s_al, s_lg, s_sg, s_cum, s_exp, s_cs = (n("w_logits"), n("a_logits"), n("logits"), n("sigmoids"),
                                                      n("cum"), n("exps"), n("cum_used"))
        s_til, s_tr, s_trc, s_tra, own = n("tilde"), n("turned"), n("turn_v"), n("turn_a"), n("chain")
        s_mat = [n(f"mat{l}") for l in range(2)]
        s_matc = [n(f"matc{l}") for l in range(2)]
        s_lready = [n(f"L{l}") for l in range(2)]
        s_rhs, s_rhsc, s_u, s_uc = ([n(f"{x}{l}") for l in range(2)] for x in ("rhs", "rhsc", "u", "uc"))
        s_y, s_yc = ([n(f"{x}{l}") for l in range(2)] for x in ("y", "yc"))
        s_act = n("act_chain")
        steps = [(0, t) for t in (0, 1, 2, 3)] + [(1, t) for t in (1, 0, 3, 2)]
        w2s, a2s = w2, a2
        with nc.Block() as block:
            @block.sync
            def _(sync):
                for i, (d, t) in enumerate(steps):
                    if i:
                        sync.wait_ge(s_free, i)
                    for q, name in enumerate(("k", "v", "kk", "r")):
                        if name == "r" and t < 2:
                            continue
                        src = scr[name][t - (2 if name == "r" else 0)]
                        sync.dma_start(ld[:, q, :], src).then_inc(s_ld, 16)

            @block.vector
            def _(dve):
                ch, take = Chain(dve, own), Take(dve)
                level = inv.dve(take)
                for i, (d, t) in enumerate(steps):
                    lat = t >= 2
                    if i in (0, 4):
                        ch.link(nc.vector.memset(st[:, :, :], 0.0))
                    take(s_wl)
                    for j in range(2):
                        ch.mark(nc.vector.tensor_tensor(at[:, j * 512:j * 512 + 512], banks[0][:, j, :],
                                                        rows["w0"][:, d, j * 512:j * 512 + 512], ALU.add))
                    take(s_al)
                    for j in range(2):
                        ch.mark(nc.vector.tensor_tensor(bt[:, j * 512:j * 512 + 512], banks[0][:, 2 + j, :],
                                                        rows["a0"][:, d, j * 512:j * 512 + 512], ALU.add))
                    ch.wait()
                    nc.vector.sem_inc(s_lg, 1)
                    take(s_sg, 2)
                    take(s_ld, 16 * (4 if lat else 3))
                    ch.link(nc.vector.scalar_tensor_tensor(out=kt_[:, :], in0=bt[:, :], scalar=-1.0, in1=rows["ka"],
                                                           op0=ALU.add, op1=ALU.mult))
                    ch.link(nc.vector.scalar_tensor_tensor(out=kt_[:, :], in0=kt_[:, :], scalar=1.0,
                                                           in1=ld[:, K_, :], op0=ALU.add, op1=ALU.mult))
                    ch.link(nc.vector.tensor_tensor(bt[:, :], bt[:, :], ld[:, KK_, :], ALU.mult))
                    if lat:
                        ch.link(nc.vector.tensor_tensor(rt[:, :], ld[:, R_, :], kt_[:, :], ALU.mult))
                        ch.link(nc.vector.tensor_tensor(rt[:, :], rt[:, :], rows["rk"], ALU.mult))
                        co = coef[:, d, t - 2, :]
                        ch.link(nc.vector.tensor_reduce(co, rt[:, :].rearrange("p (h d) -> p h d", h=RW_H),
                                                        AX.X, ALU.add))
                    take(s_cum)
                    take(s_exp, 3 if lat else 2)
                    for j in range(2):
                        sl = slice(j * 512, j * 512 + 512)
                        ch.mark(nc.vector.tensor_tensor(at[:, sl], banks[0][:, j, :], at[:, sl], ALU.subtract))
                    ch.wait()
                    nc.vector.sem_inc(s_cs, 1)
                    take(s_exp)
                    e_a, e_i, e_r = (tr[:, q, :, :].rearrange("p a b -> p (a b)") for q in range(3))
                    ch.mark(nc.vector.scalar_tensor_tensor(out=at[:, :], in0=e_a, scalar=-1.0, in1=ld[:, KK_, :],
                                                           op0=ALU.mult, op1=ALU.mult))
                    ch.mark(nc.vector.tensor_tensor(bt[:, :], bt[:, :], e_i, ALU.mult))
                    ch.mark(nc.vector.tensor_tensor(kt_[:, :], kt_[:, :], e_i, ALU.mult))
                    if lat:
                        ch.mark(nc.vector.tensor_tensor(rt[:, :], ld[:, R_, :], e_r, ALU.mult))
                    ch.wait()
                    nc.vector.sem_inc(s_til, 1)
                    nq = 4 if lat else 3
                    for q in range(nq):
                        take(s_tr)
                        nc.vector.tensor_copy(tr[:, q, 0:4, :], banks[0][:, q, :].rearrange("p (a b) -> p a b", a=4))\
                            .then_inc(s_trc, 1)
                    for r in range(2):
                        strict_lo, strict_up = (C_LOS, C_UPS) if d == 0 else (C_UPS, C_LOS)
                        incl_up = C_UP if d == 0 else C_LO
                        for l in range(2):
                            take(s_mat[l])
                            for q in range(4 if lat else 2):
                                m = (strict_lo, strict_up, incl_up, incl_up)[q]
                                dst = inv.L[l][:, :, :] if q == 0 else mat[l][:, q - 1, :].rearrange(
                                    "p (h c) -> p h c", h=4)
                                ins = nc.vector.tensor_tensor(dst, banks[l][:, q, :].rearrange("p (h c) -> p h c", h=4),
                                                              rep(blk(g, m), 4), ALU.mult)
                                ins.then_inc(s_lready[l] if q == 0 else s_matc[l], 1)
                        for k in range(LEVELS):
                            level(k, banks)
                        for l in range(2):
                            if lat:
                                take(s_y[l])
                                src = banks[l][:, 1, 0:256].rearrange("p (k c) -> p k c", k=4)
                                dst = y[:, t - 2, :].rearrange("p (k l c) -> p k l c", l=2, c=RW_D)[
                                    :, 4 * r:4 * r + 4, l, :]
                                if d == 0:
                                    nc.vector.tensor_copy(dst, src).then_inc(s_yc[l], 1)
                                else:
                                    nc.vector.tensor_tensor(dst, dst, src, ALU.add).then_inc(s_yc[l], 1)
                                take(s_yc[l])
                            take(s_y[l])
                            half = slice(64 * l, 64 * l + 64)
                            sv = st[half, 4 * r:4 * r + 4, :]
                            ch.link(nc.vector.tensor_tensor(sv, sv, banks[l][half, 2, 0:256].rearrange(
                                "p (a b) -> p a b", a=4), ALU.add))
                            nc.vector.tensor_tensor(sv, sv, rep(pc[half, 4 * r:4 * r + 4, 0], RW_D, 2), ALU.mult)\
                                .then_inc(s_yc[l], 1)
                            take(s_yc[l])
                    nc.vector.sem_inc(s_free, 1)

            @block.gpsimd
            def _(pool):
                take = Take(pool)
                for i, (d, t) in enumerate(steps):
                    for r in range(2):
                        inv.pool(take, s_lready, d)

            @block.scalar
            def _(act):
                ch, take = Chain(act, s_act), Take(act)
                flat = lambda q: tr[:, q, :, :].rearrange("p a b -> p (a b)")
                for i, (d, t) in enumerate(steps):
                    lat = t >= 2
                    take(s_lg)
                    nc.scalar.activation(at[:, :], at[:, :], ACT.Sigmoid).then_inc(s_sg, 1)
                    nc.scalar.activation(bt[:, :], bt[:, :], ACT.Sigmoid).then_inc(s_sg, 1)
                    take(s_cum)
                    two = banks[0][:, 0:2, :]
                    o2 = lambda q: flat(q).rearrange("p (a b) -> p a b", a=2)
                    nc.scalar.activation(o2(1), two, ACT.Exp, scale=DECAY).then_inc(s_exp, 1)
                    if lat:
                        nc.scalar.activation(o2(2), two, ACT.Exp, scale=-DECAY).then_inc(s_exp, 1)
                    nc.scalar.activation(pc[:, :, :], banks[0][:, 2, 0:16].rearrange("p (a b) -> p a b", b=2),
                                         ACT.Exp, scale=-DECAY).then_inc(s_exp, 1)
                    take(s_cs)
                    nc.scalar.activation(flat(0), at[:, :], ACT.Exp, scale=-DECAY).then_inc(s_exp, 1)
                    for q in range(4 if lat else 3):
                        take(s_tr)
                        nc.scalar.copy(tr[:, q, 4:8, :], banks[1][:, q, :].rearrange("p (a b) -> p a b", a=4))\
                            .then_inc(s_tra, 1)
                    for r in range(2):
                        inv.act(take, banks)
                        for l in range(2):
                            take(s_rhs[l])
                            nc.scalar.copy(rhs[l][:, :], banks[l][:, 3, 0:256]).then_inc(s_rhsc[l], 1)
                        for l in range(2):
                            take(s_u[l])
                            nc.scalar.copy(us[l][:, :], banks[l][:, 0, 0:256]).then_inc(s_uc[l], 1)

            @block.tensor
            def _(pe):
                take = Take(pe)
                for i, (d, t) in enumerate(steps):
                    lat = t >= 2
                    z = slice(64 * d, 64 * d + 64)
                    for which, (low, w, s) in enumerate(((low_w, w2s, s_wl), (low_a, a2s, s_al))):
                        for j in range(2):
                            mm = nc.tensor.matmul(banks[0][:, 2 * which + j, :], low[z, t * P:(t + 1) * P],
                                                  w[z, j * 512:j * 512 + 512], start=True, stop=True)
                        mm.then_inc(s, 1)
                    take(s_sg, 2)
                    tri = blk(g, C_UP if d == 0 else C_LO)
                    for j in range(2):
                        nc.tensor.matmul(banks[0][:, j, :], tri, at[:, j * 512:j * 512 + 512], start=True, stop=True)
                    for kt in range(KT):
                        mm = nc.tensor.matmul(banks[0][:, 2, 2 * kt:2 * kt + 2], at[:, kt * P:(kt + 1) * P],
                                              blk(g, C_ONE)[:, 0:2], start=True, stop=True)
                    mm.then_inc(s_cum, 1)
                    take(s_til)
                    srcs = (at, bt, kt_, rt)[:4 if lat else 3]
                    for q, src in enumerate(srcs):
                        for kt in range(KT):
                            mm = nc.tensor.transpose(banks[kt // 4][:, q, (kt % 4) * P:(kt % 4 + 1) * P],
                                                     src[:, kt * P:(kt + 1) * P], blk(g, C_ID))
                        mm.then_inc(s_tr, 1)
                    for q in range(len(srcs)):
                        take(s_trc)
                        take(s_tra)
                    A, B, K, R = range(4)
                    for r in range(2):
                        for l in range(2):
                            jobs = ((A, B), (K, A), (B, R), (K, R))[:4 if lat else 2]
                            for q, (lhs, rh) in enumerate(jobs):
                                for h in range(4):
                                    hh = 8 * r + 2 * h + l
                                    o = slice(64 * l, 64 * l + 64)
                                    mm = nc.tensor.matmul(banks[l][:, q, h * P:(h + 1) * P], tr[o, lhs, hh // 2, :],
                                                          tr[o, rh, hh // 2, :], start=True, stop=True)
                            mm.then_inc(s_mat[l], 1)
                        inv_masks = 3 if lat else 1
                        for l in range(2):
                            take(s_matc[l], inv_masks)
                        inv.pe(take, banks)
                        for l in range(2):
                            for h in range(4):
                                hh = 8 * r + 2 * h + l
                                o = slice(64 * l, 64 * l + 64)
                                nc.tensor.matmul(banks[l][:, 3, h * 64:h * 64 + 64], tr[o, A, hh // 2, :],
                                                 st[o, hh // 2, :], start=True, stop=False)
                                mm = nc.tensor.matmul(banks[l][:, 3, h * 64:h * 64 + 64],
                                                      mat[l][:, 0, h * P:(h + 1) * P],
                                                      ld[:, V_, hh * 64:hh * 64 + 64], start=False, stop=True)
                            mm.then_inc(s_rhs[l], 1)
                        for l in range(2):
                            take(s_rhsc[l])
                            for h in range(4):
                                mm = nc.tensor.matmul(banks[l][:, 0, h * 64:h * 64 + 64], inv.Y[l][:, h, :],
                                                      rhs[l][:, h * 64:h * 64 + 64], start=True, stop=True)
                            mm.then_inc(s_u[l], 1)
                        for l in range(2):
                            take(s_uc[l])
                            if lat:
                                for h in range(4):
                                    hh = 8 * r + 2 * h + l
                                    o = slice(64 * l, 64 * l + 64)
                                    dst = banks[l][:, 1, h * 64:h * 64 + 64]
                                    nc.tensor.matmul(dst, tr[o, R, hh // 2, :], st[o, hh // 2, :],
                                                     start=True, stop=False)
                                    nc.tensor.matmul(dst, mat[l][:, 1, h * P:(h + 1) * P],
                                                     us[l][:, h * 64:h * 64 + 64], start=False, stop=False)
                                    mm = nc.tensor.matmul(dst, mat[l][:, 2, h * P:(h + 1) * P],
                                                          ld[:, V_, hh * 64:hh * 64 + 64], start=False, stop=True)
                                mm.then_inc(s_y[l], 1)
                            for h in range(4):
                                hh = 8 * r + 2 * h + l
                                dst = banks[l][64 * l:64 * l + 64, 2, h * 64:h * 64 + 64]
                                nc.tensor.matmul(dst, bt[:, hh * 64:hh * 64 + 64], us[l][:, h * 64:h * 64 + 64],
                                                 start=True, stop=False)
                                mm = nc.tensor.matmul(dst, kt_[:, hh * 64:hh * 64 + 64],
                                                      ld[:, V_, hh * 64:hh * 64 + 64], start=False, stop=True)
                            mm.then_inc(s_y[l], 1)
                        for l in range(2):
                            take(s_yc[l], 2 if lat else 1)


def rw_readout(g, y, coef, v, rows, sg0, sg1, g2a, g2b, out):
    nc = g.nc
    with Phase(g, "rwread") as ph:
        sq = ph.sb("square", [P, D])
        st = ph.sb("stats", [P, 5, 2 * RW_H])
        ps = ph.ps("gate", [P, 4, 512])
        own, s_mm, s_var, s_rt = ph.sem("chain"), ph.sem("gate"), ph.sem("var"), ph.sem("root")
        with nc.Block() as block:
            @block.tensor
            def _(pe):
                for i in range(4):
                    t, j = i // 2, i % 2
                    nc.tensor.matmul(ps[:, i, :], sg0[:, t * P:(t + 1) * P], g2a[:, j * 512:j * 512 + 512],
                                     start=True, stop=False)
                    nc.tensor.matmul(ps[:, i, :], sg1[0:32, t * P:(t + 1) * P], g2b[0:32, j * 512:j * 512 + 512],
                                     start=False, stop=True).then_inc(s_mm, 1)

            @block.scalar
            def _(act):
                act.wait_ge(s_var, 1)
                nc.scalar.activation(st[:, 3, :], st[:, 2, :], ACT.Sqrt).then_inc(s_rt, 1)

            @block.vector
            def _(dve):
                ch = Chain(dve, own)
                heads = lambda a: a.rearrange("p (h d) -> p h d", h=RW_H)
                for t in range(2):
                    c = slice(RW_H * t, RW_H * (t + 1))
                    yt = y[:, t, :]
                    ch.link(nc.vector.tensor_reduce(st[:, 0, c], heads(yt), AX.X, ALU.add))
                    ch.link(nc.vector.tensor_scalar(st[:, 0, c], st[:, 0, c], 1.0 / RW_D, None, ALU.mult))
                    ch.link(nc.vector.tensor_tensor(heads(yt), heads(yt), rep(st[:, 0, c], RW_D, 2), ALU.subtract))
                    ch.link(nc.vector.tensor_tensor(sq[:, :], yt, yt, ALU.mult))
                    ch.link(nc.vector.tensor_reduce(st[:, 1, c], heads(sq[:, :]), AX.X, ALU.add))
                nc.vector.tensor_scalar(st[:, 2, :], st[:, 1, :], 1.0 / RW_D, GN_EPS, ALU.mult, ALU.add)\
                    .then_inc(s_var, 1)
                dve.wait_ge(s_rt, 1)
                ch.link(nc.vector.reciprocal(st[:, 4, :], st[:, 3, :]))
                for t in range(2):
                    c = slice(RW_H * t, RW_H * (t + 1))
                    yt = y[:, t, :]
                    ch.link(nc.vector.tensor_tensor(heads(yt), heads(yt), rep(st[:, 4, c], RW_D, 2), ALU.mult))
                    ch.link(nc.vector.tensor_tensor(yt, yt, rows["lw"], ALU.mult))
                    ch.link(nc.vector.tensor_tensor(yt, yt, rows["lb"], ALU.add))
                    ch.link(nc.vector.tensor_tensor(st[:, 0, c], coef[:, 0, t, :], coef[:, 1, t, :], ALU.add))
                    ch.link(nc.vector.tensor_tensor(heads(sq[:, :]), heads(v[:, t, :]), rep(st[:, 0, c], RW_D, 2),
                                                    ALU.mult))
                    ch.link(nc.vector.tensor_tensor(yt, yt, sq[:, :], ALU.add))
                    for j in range(2):
                        dve.wait_ge(s_mm, 2 * t + j + 1)
                        sl = slice(j * 512, j * 512 + 512)
                        ch.mark(nc.vector.tensor_tensor(out[:, t, sl], yt[:, sl], ps[:, 2 * t + j, :], ALU.mult))
                    ch.wait()


def gd_conv(g, feat, taps, bias):
    nc, ring = g.nc, g.ring
    F = feat.shape[1]
    with Phase(g, "gdconv") as ph:
        pad = ph.sb("padded", [P, 4, 259])
        acc = ph.sb("sum", [P, 4, 256])
        banks = ph.ps("bank", [P, 8, 512])
        s_z, s_pad, s_acc, s_out, own = (ph.sem("zero"), ph.sem("padded"), ph.sem("summed"), ph.sem("out"),
                                         ph.sem("chain"))
        done0 = ring.done
        with nc.Block() as block:
            @block.sync
            def _(sync):
                ring.issue(sync, F // 4)

            @block.gpsimd
            def _(pool):
                nc.gpsimd.memset(pad[:, :, 0:3], 0.0).then_inc(s_z, 1)

            @block.tensor
            def _(pe):
                for f in range(F):
                    if f % 4 == 0:
                        wv = ring.take(pe)
                    if f >= 8:
                        pe.wait_ge(s_pad, f - 7)
                    for kt in range(KT):
                        mm = nc.tensor.matmul(banks[:, f % 8, 0:256], wv[:, kt, (f % 4) * P:(f % 4 + 1) * P],
                                              g.xT[:, kt, 0:256], start=(kt == 0), stop=(kt == KT - 1))
                    ring.mark(mm)

            @block.scalar
            def _(act):
                act.wait_ge(s_z, 1)

                def silu(f):
                    act.wait_ge(s_acc, f + 1)
                    nc.scalar.activation(feat[:, f, :], acc[:, f % 4, :], ACT.Silu, bias=bias[:, f:f + 1])\
                        .then_inc(s_out, 1)

                for f in range(F):
                    act.wait_ge(ring.gemm_done, done0 + f + 1)
                    if f >= 4:
                        act.wait_ge(s_acc, f - 3)
                    nc.scalar.copy(pad[:, f % 4, 3:259], banks[:, f % 8, 0:256]).then_inc(s_pad, 1)
                    if f >= 2:
                        silu(f - 2)
                silu(F - 2)
                silu(F - 1)
                act.wait_ge(s_out, F)

            @block.vector
            def _(dve):
                ch = Chain(dve, own)
                for f in range(F):
                    dve.wait_ge(s_pad, f + 1)
                    if f >= 4:
                        dve.wait_ge(s_out, f - 3)
                    a = acc[:, f % 4, :]
                    ch.link(nc.vector.tensor_scalar(a, pad[:, f % 4, 0:256], taps[:, f, 0:1], None, ALU.mult))
                    for j in range(1, 4):
                        ins = nc.vector.scalar_tensor_tensor(out=a, in0=pad[:, f % 4, j:j + 256],
                                                             scalar=taps[:, f, j:j + 1], in1=a,
                                                             op0=ALU.mult, op1=ALU.add)
                        if j < 3:
                            ch.link(ins)
                        else:
                            ins.then_inc(s_acc, 1)


def gd_l2(g, feat):
    nc = g.nc
    N = 2 * GD_H
    with Phase(g, "gdl2") as ph:
        sq = ph.sb("square", [P, 4, 256])
        r = ph.sb("root", [P, 4, 256])
        ps = ph.ps("sum", [P, 4, 512])
        s_sq, s_mm, s_e, s_rt, s_f, own = (ph.sem("square"), ph.sem("sum"), ph.sem("eps"), ph.sem("root"),
                                           ph.sem("final"), ph.sem("chain"))
        with nc.Block() as block:
            @block.gpsimd
            def _(pool):
                for n in range(N):
                    if n >= 4:
                        pool.wait_ge(s_mm, n - 3)
                    nc.gpsimd.tensor_tensor(sq[:, n % 4, :], feat[:, n, :], feat[:, n, :], ALU.mult).then_inc(s_sq, 1)

            @block.tensor
            def _(pe):
                for n in range(N):
                    pe.wait_ge(s_sq, n + 1)
                    if n >= 4:
                        pe.wait_ge(s_e, n - 3)
                    nc.tensor.matmul(ps[:, n % 4, 0:256], blk(g, C_ONE), sq[:, n % 4, :], start=True, stop=True)\
                        .then_inc(s_mm, 1)

            @block.scalar
            def _(act):
                for n in range(N):
                    act.wait_ge(s_e, n + 1)
                    nc.scalar.activation(r[:, n % 4, :], r[:, n % 4, :], ACT.Sqrt).then_inc(s_rt, 1)

            @block.vector
            def _(dve):
                ch = Chain(dve, own)

                def end(n):
                    dve.wait_ge(s_rt, n + 1)
                    ch.link(nc.vector.reciprocal(r[:, n % 4, :], r[:, n % 4, :]))
                    sc = P ** -0.5 if n < GD_H else 1.0
                    nc.vector.scalar_tensor_tensor(out=feat[:, n, :], in0=feat[:, n, :], scalar=sc,
                                                   in1=r[:, n % 4, :], op0=ALU.mult, op1=ALU.mult).then_inc(s_f, 1)

                for n in range(N):
                    dve.wait_ge(s_mm, n + 1)
                    if n >= 4:
                        dve.wait_ge(s_f, n - 3)
                    nc.vector.tensor_scalar(r[:, n % 4, :], ps[:, n % 4, 0:256], EPS, None, ALU.add).then_inc(s_e, 1)
                    if n >= 2:
                        end(n - 2)
                end(N - 2)
                end(N - 1)
                dve.wait_ge(s_f, N)


def gd_gates(g, p2, rows, beta, dt, ga, cums):
    nc = g.nc
    with Phase(g, "gdgates") as ph:
        z = ph.sb("z", [P, 2, 24])
        az = ph.sb("az", [P, 2, 24])
        ea = ph.sb("ea", [P, 24])
        ps = ph.ps("cums", [P, 4, 24])
        own, s_z, s_a, s_ga, s_mm = ph.sem("chain"), ph.sem("abs"), ph.sem("act"), ph.sem("ga"), ph.sem("cums")
        with nc.Block() as block:
            @block.vector
            def _(dve):
                ch = Chain(dve, own)
                ch.mark(nc.vector.tensor_tensor(z[:, :, 0:8], p2[:, :, 1032:1040],
                                                rep(rows[:, 0:8], 2), ALU.add))
                ch.mark(nc.vector.tensor_tensor(z[:, :, 8:24], p2[:, :, 2064:2080], rep(rows[:, 8:24], 2), ALU.add))
                ch.wait()
                nc.vector.scalar_tensor_tensor(out=az[:, :, :], in0=z[:, :, :], scalar=-1.0, in1=z[:, :, :],
                                               op0=ALU.mult, op1=ALU.max).then_inc(s_z, 1)
                dve.wait_ge(s_a, 1)
                nc.vector.tensor_scalar(az[:, :, :], az[:, :, :], 1.0, None, ALU.add).then_inc(s_z, 1)
                dve.wait_ge(s_a, 2)
                ch.link(nc.vector.scalar_tensor_tensor(out=z[:, :, :], in0=z[:, :, :], scalar=0.0, in1=az[:, :, :],
                                                       op0=ALU.max, op1=ALU.add))
                ch.mark(nc.vector.tensor_copy(dt[:, :, :], z[:, :, 8:24]))
                dve.wait_ge(s_a, 3)
                nc.vector.scalar_tensor_tensor(out=ga[:, :, :], in0=z[:, :, :], scalar=-1.0, in1=rep(ea[:, :], 2),
                                               op0=ALU.mult, op1=ALU.mult).then_inc(s_ga, 1)
                dve.wait_ge(s_mm, 1)
                ch.link(nc.vector.tensor_copy(cums[:, :, :], ps[:, :, :]))

            @block.scalar
            def _(act):
                act.wait_ge(s_z, 1)
                nc.scalar.activation(az[:, :, :], az[:, :, :], ACT.Exp, scale=-1.0).then_inc(s_a, 1)
                act.wait_ge(s_z, 2)
                nc.scalar.activation(az[:, :, :], az[:, :, :], ACT.Ln).then_inc(s_a, 1)
                act.wait_ge(s_a, 2)
                nc.scalar.activation(ea[:, :], rows[:, 24:48], ACT.Exp).then_inc(s_a, 1)
                nc.scalar.activation(beta[:, :, :], p2[:, :, 1024:1032], ACT.Sigmoid).then_inc(s_a, 1)
                act.wait_ge(s_a, 4)

            @block.tensor
            def _(pe):
                pe.wait_ge(s_ga, 1)
                for t in range(2):
                    nc.tensor.matmul(ps[:, t, :], blk(g, C_UP), ga[:, t, :], start=True, stop=True)
                    mm = nc.tensor.matmul(ps[:, 2 + t, :], blk(g, C_ONE), ga[:, t, :], start=True, stop=True)
                mm.then_inc(s_mm, 1)


def gd_chunks(g, feat, ktok, vtok, beta, ga, cums, og):
    nc = g.nc
    with Phase(g, "gdn") as ph:
        inv = Inverse(g, ph)
        spare = g.xT[:, :, :].rearrange("p a (h c) -> p a h c", h=4)
        wide, eA, eT, rhs = ([spare[:, 2 * q + l, :, :] for l in range(2)] for q in range(4))
        us = [ph.sb(f"U{l}", [P, 4, P]) for l in range(2)]
        st = [g.tmp[:, 512 * l:512 * l + 512].rearrange("p (h c) -> p h c", h=4) for l in range(2)]
        ex = ph.sb("exps", [P, 3, 2, 8])
        nb = ph.sb("minus_beta", [P, 2, 8])
        banks = [ph.ps(f"lane{l}", [P, 4, 512]) for l in range(2)]
        own, s_c, s_ce = ph.sem("chain"), ph.sem("cols"), ph.sem("cols_exp")
        two = lambda x: [ph.sem(f"{x}{l}") for l in range(2)]
        s_wide, s_gb, s_dif, s_exp, s_msk, s_lready = (two(x) for x in ("wide", "gb", "dif", "exp", "msk", "Lr"))
        s_rhs, s_u, s_uc, s_o, s_oc, s_ks = (two(x) for x in ("rhs", "u", "uc", "o", "oc", "ks"))
        s_m = two("m")
        b4 = lambda l, q: banks[l][:, q, :].rearrange("p (h c) -> p h c", h=4)
        with nc.Block() as block:
            @block.vector
            def _(dve):
                ch, take = Chain(dve, own), Take(dve)
                level = inv.dve(take)
                ch.mark(nc.vector.tensor_tensor(ex[:, 1, :, :], cums[:, 2:4, 0:8], cums[:, 0:2, 0:8], ALU.subtract))
                ch.link(nc.vector.tensor_scalar(nb[:, :, :], beta[:, :, :], -1.0, None, ALU.mult))
                nc.vector.sem_inc(s_c, 1)
                take(s_ce, 2)
                ch.link(nc.vector.tensor_tensor(ex[:, 2, :, :], nb[:, :, :], ex[:, 0, :, :], ALU.mult))
                for i in range(2):
                    tok = slice(i * P, (i + 1) * P)
                    for l in range(2):
                        for h in range(4):
                            hh = 4 * l + h
                            ins = nc.vector.tensor_scalar(wide[l][:, h, :], blk(g, C_ONE), ga[:, i, hh:hh + 1],
                                                          None, ALU.mult)
                            ins.then_inc(s_wide[l], 1)
                    for l in range(2):
                        take(s_gb[l])
                        for h in range(4):
                            hh = 4 * l + h
                            gam = cums[:, i, hh:hh + 1]
                            G = banks[l][:, 0, h * P:(h + 1) * P]
                            nc.vector.tensor_scalar(eA[l][:, h, :], G, gam, 0.0, ALU.subtract, ALU.max)\
                                .then_inc(s_dif[l], 1)
                            nc.vector.tensor_scalar(eT[l][:, h, :], G, gam, 0.0, ALU.subtract, ALU.min)\
                                .then_inc(s_dif[l], 1)
                    for l in range(2):
                        take(s_msk[l], 2)
                        for h in range(4):
                            hh = 4 * l + h
                            nc.vector.scalar_tensor_tensor(out=inv.L[l][:, h, :], in0=banks[l][:, 1, h * P:(h + 1) * P],
                                                           scalar=nb[:, i, hh:hh + 1], in1=eA[l][:, h, :],
                                                           op0=ALU.mult, op1=ALU.mult).then_inc(s_lready[l], 1)
                        nc.vector.tensor_tensor(eT[l][:, :, :], b4(l, 2), eT[l][:, :, :], ALU.mult)\
                            .then_inc(s_m[l], 1)
                        for h in range(4):
                            hh = 4 * l + h
                            ch.mark(nc.vector.tensor_scalar(rhs[l][:, h, :], vtok[:, i, hh * P:(hh + 1) * P],
                                                            beta[:, i, hh:hh + 1], None, ALU.mult))
                        if i:
                            ch.wait()
                            take(s_ks[l])
                            for h in range(4):
                                hh = 4 * l + h
                                ch.mark(nc.vector.scalar_tensor_tensor(
                                    out=rhs[l][:, h, :], in0=banks[l][:, 3, h * P:(h + 1) * P],
                                    scalar=ex[:, 2, i, hh:hh + 1], in1=rhs[l][:, h, :], op0=ALU.mult, op1=ALU.add))
                        else:
                            for h in range(4):
                                hh = 4 * l + h
                                kv = ktok[:, 0, hh * P:(hh + 1) * P]
                                ch.mark(nc.vector.tensor_scalar(kv, kv, ex[:, 1, 0, hh:hh + 1], None, ALU.mult))
                        ch.wait()
                        nc.vector.sem_inc(s_rhs[l], 1)
                    for k in range(LEVELS):
                        level(k, banks)
                    for l in range(2):
                        take(s_o[l])
                        dst = og[:, i, l * 512:l * 512 + 512]
                        if i == 0:
                            nc.vector.tensor_copy(dst, banks[l][:, 1, :]).then_inc(s_oc[l], 1)
                            take(s_o[l])
                            nc.vector.tensor_copy(st[l][:, :, :], b4(l, 2)).then_inc(s_oc[l], 1)
                        else:
                            for h in range(4):
                                hh = 4 * l + h
                                ch.mark(nc.vector.tensor_scalar(og[:, i, hh * P:(hh + 1) * P],
                                                                banks[l][:, 3, h * P:(h + 1) * P],
                                                                ex[:, 0, i, hh:hh + 1], None, ALU.mult))
                            ch.wait()
                            ch.link(nc.vector.tensor_tensor(dst, dst, banks[l][:, 1, :], ALU.add))

            @block.gpsimd
            def _(pool):
                take = Take(pool)
                for i in range(2):
                    for l in range(2):
                        for buf, m in ((eA, C_LOS), (eT, C_UP)):
                            take(s_exp[l])
                            nc.gpsimd.tensor_tensor(buf[l][:, :, :], buf[l][:, :, :], rep(blk(g, m), 4), ALU.mult)\
                                .then_inc(s_msk[l], 1)
                    for l in range(2):
                        take(s_lready[l], 3)
                    inv.pool(take, s_lready, 0)

            @block.scalar
            def _(act):
                take = Take(act)
                take(s_c)
                nc.scalar.activation(ex[:, 0, :, :], cums[:, 0:2, 0:8], ACT.Exp).then_inc(s_ce, 1)
                nc.scalar.activation(ex[:, 1, :, :], ex[:, 1, :, :], ACT.Exp).then_inc(s_ce, 1)
                for i in range(2):
                    for l in range(2):
                        take(s_dif[l], 8)
                        nc.scalar.activation(eA[l][:, :, :], eA[l][:, :, :], ACT.Exp, scale=-1.0).then_inc(s_exp[l], 1)
                        nc.scalar.activation(eT[l][:, :, :], eT[l][:, :, :], ACT.Exp).then_inc(s_exp[l], 1)
                    inv.act(take, banks)
                    for l in range(2):
                        take(s_u[l])
                        nc.scalar.copy(us[l][:, :, :], b4(l, 0)).then_inc(s_uc[l], 1)

            @block.tensor
            def _(pe):
                take = Take(pe)
                for i in range(2):
                    tok = slice(i * P, (i + 1) * P)
                    for l in range(2):
                        if i:
                            take(s_oc[l], 2)
                        for h in range(4):
                            hh = 4 * l + h
                            take(s_wide[l])
                            cols = slice(h * P, (h + 1) * P)
                            nc.tensor.matmul(banks[l][:, 0, cols], wide[l][:, h, :], blk(g, C_UP), start=True, stop=True)
                            kT, qT = feat[:, 8 + hh, tok], feat[:, hh, tok]
                            nc.tensor.matmul(banks[l][:, 1, cols], kT, kT, start=True, stop=True)
                            mm = nc.tensor.matmul(banks[l][:, 2, cols], kT, qT, start=True, stop=True)
                        mm.then_inc(s_gb[l], 1)
                        if i:
                            for h in range(4):
                                mm = nc.tensor.matmul(banks[l][:, 3, h * P:(h + 1) * P], feat[:, 8 + 4 * l + h, tok],
                                                      st[l][:, h, :], start=True, stop=True)
                            mm.then_inc(s_ks[l], 1)
                    for l in range(2):
                        take(s_m[l])
                        take(s_rhs[l])
                    inv.pe(take, banks)
                    for l in range(2):
                        for h in range(4):
                            mm = nc.tensor.matmul(banks[l][:, 0, h * P:(h + 1) * P], inv.Y[l][:, h, :], rhs[l][:, h, :],
                                                  start=True, stop=True)
                        mm.then_inc(s_u[l], 1)
                    for l in range(2):
                        take(s_uc[l])
                        for h in range(4):
                            hh = 4 * l + h
                            cols = slice(h * P, (h + 1) * P)
                            if i:
                                nc.tensor.matmul(banks[l][:, 3, cols], feat[:, hh, tok], st[l][:, h, :],
                                                 start=True, stop=True)
                            mm = nc.tensor.matmul(banks[l][:, 1, cols], eT[l][:, h, :], us[l][:, h, :],
                                                  start=True, stop=True)
                        mm.then_inc(s_o[l], 1)
                        if i == 0:
                            for h in range(4):
                                hh = 4 * l + h
                                mm = nc.tensor.matmul(banks[l][:, 2, h * P:(h + 1) * P],
                                                      ktok[:, 0, hh * P:(hh + 1) * P], us[l][:, h, :],
                                                      start=True, stop=True)
                            mm.then_inc(s_o[l], 1)


def ssd(g, feat, xtok, dt, ga, cums, drow, ys):
    nc = g.nc
    with Phase(g, "ssd") as ph:
        cb = ph.sb("cb", [P, SS_G, 384])
        xd = ph.sb("xdt", [P, 2, D])
        wide = ph.sb("wide", [P, 4, 2, P])
        dec = ph.sb("decay", [P, 4, 384])
        ac = ph.sb("acum", [P, 2, SS_H])
        pcb = ph.ps("cb", [P, 2, 512])
        G = ph.ps("G", [P, 4, 512])
        out = ph.ps("out", [P, 2, 512])
        own, s_cb, s_cbc = ph.sem("chain"), ph.sem("cb"), ph.sem("cb_ready")
        s_w, s_g, s_d, s_e, s_wt, s_o, s_oc = (ph.sem(x) for x in ("wide", "G", "diff", "exp", "weights", "out", "oc"))
        with nc.Block() as block:
            @block.tensor
            def _(pe):
                for gr in range(SS_G):
                    B, C = feat[:, 32 + gr, :], feat[:, 34 + gr, :]
                    nc.tensor.matmul(pcb[:, gr, 0:256], B[:, 0:P], C, start=True, stop=True)
                    nc.tensor.matmul(pcb[:, gr, 256:384], B[:, P:256], C[:, P:256], start=True, stop=True)\
                        .then_inc(s_cb, 1)
                pe.wait_ge(s_cbc, 1)

                def rows(h):
                    pe.wait_ge(s_w, 2 * h + 2)
                    if h >= 4:
                        pe.wait_ge(s_d, 2 * (h - 3))
                    b = h % 4
                    nc.tensor.matmul(G[:, b, 0:P], wide[:, b, 0, :], blk(g, C_UP), start=True, stop=True)
                    nc.tensor.matmul(G[:, b, P:256], wide[:, b, 0, :], blk(g, C_ONE), start=True, stop=False)
                    nc.tensor.matmul(G[:, b, P:256], wide[:, b, 1, :], blk(g, C_UP), start=False, stop=True)\
                        .then_inc(s_g, 1)

                def values(h):
                    pe.wait_ge(s_wt, h + 1)
                    if h % 4 == 0 and h >= 8:
                        pe.wait_ge(s_oc, h // 4 - 1)
                    bank = out[:, (h // 4) % 2, :].rearrange("p (t h c) -> p t h c", t=2, h=4)
                    W = dec[:, h % 4, :]
                    x0, x1 = xd[:, 0, h * 64:h * 64 + 64], xd[:, 1, h * 64:h * 64 + 64]
                    nc.tensor.matmul(bank[:, 0, h % 4, :], W[:, 0:P], x0, start=True, stop=True)
                    nc.tensor.matmul(bank[:, 1, h % 4, :], W[:, P:256], x0, start=True, stop=False)
                    nc.tensor.matmul(bank[:, 1, h % 4, :], W[:, 256:384], x1, start=False, stop=True).then_inc(s_o, 1)

                for h in range(SS_H + 1):
                    if h < SS_H:
                        rows(h)
                    if h >= 1:
                        values(h - 1)

            @block.gpsimd
            def _(pool):
                for h in range(SS_H):
                    pool.wait_ge(s_e, h + 1)
                    nc.gpsimd.tensor_tensor(dec[:, h % 4, :], dec[:, h % 4, :], cb[:, h // 8, :], ALU.mult)\
                        .then_inc(s_wt, 1)

            @block.scalar
            def _(act):
                for h in range(SS_H):
                    act.wait_ge(s_d, 2 * h + 2)
                    nc.scalar.activation(dec[:, h % 4, :], dec[:, h % 4, :], ACT.Exp).then_inc(s_e, 1)

            @block.vector
            def _(dve):
                ch = Chain(dve, own)
                for gr in range(SS_G):
                    dve.wait_ge(s_cb, gr + 1)
                    ch.mark(nc.vector.tensor_tensor(cb[:, gr, 0:P], pcb[:, gr, 0:P], blk(g, C_UP), ALU.mult))
                    ch.mark(nc.vector.tensor_copy(cb[:, gr, P:256], pcb[:, gr, P:256]))
                    ch.mark(nc.vector.tensor_tensor(cb[:, gr, 256:384], pcb[:, gr, 256:384], blk(g, C_UP), ALU.mult))
                ch.mark(nc.vector.tensor_copy(ac[:, 0, :], cums[:, 0, 8:24]))
                ch.mark(nc.vector.tensor_tensor(ac[:, 1, :], cums[:, 1, 8:24], cums[:, 2, 8:24], ALU.add))
                for t in range(2):
                    v = xtok[:, t, :].rearrange("p (h c) -> p h c", h=SS_H)
                    ch.mark(nc.vector.tensor_tensor(xd[:, t, :].rearrange("p (h c) -> p h c", h=SS_H), v,
                                                    rep(dt[:, t, :], SS_P, 2), ALU.mult))
                    ch.mark(nc.vector.tensor_tensor(ys[:, t, :].rearrange("p (h c) -> p h c", h=SS_H), v,
                                                    rep(drow, SS_P, 2), ALU.mult))
                ch.wait()
                nc.vector.sem_inc(s_cbc, 1)

                def wides(h):
                    if h >= 4:
                        dve.wait_ge(s_g, h - 3)
                    for t in range(2):
                        nc.vector.tensor_scalar(wide[:, h % 4, t, :], blk(g, C_ONE), ga[:, t, 8 + h:9 + h], None,
                                                ALU.mult).then_inc(s_w, 1)

                def diff(h):
                    dve.wait_ge(s_g, h + 1)
                    if h >= 4:
                        dve.wait_ge(s_o, h - 3)
                    for t, a, b, c in ((0, 0, 256, 0), (1, 256, 384, P)):
                        nc.vector.tensor_scalar(dec[:, h % 4, a:b], G[:, h % 4, c:256], ac[:, t, h:h + 1], 0.0,
                                                ALU.subtract, ALU.min).then_inc(s_d, 1)

                def evac(q):
                    dve.wait_ge(s_o, 4 * q + 4)
                    v = ys[:, :, q * 256:q * 256 + 256]
                    nc.vector.tensor_tensor(v, v, out[:, q % 2, :].rearrange("p (t c) -> p t c", t=2), ALU.add)\
                        .then_inc(s_oc, 1)

                wides(0)
                for h in range(SS_H):
                    if h + 1 < SS_H:
                        wides(h + 1)
                    diff(h)
                    if h % 4 == 2 and h >= 6:
                        evac(h // 4 - 1)
                evac(3)
                dve.wait_ge(s_oc, 4)


def gd_merge(g, p2, og, ys, rows, mix):
    nc = g.nc
    with Phase(g, "gdmerge") as ph:
        sq = ph.sb("square", [P, D])
        sz = ph.sb("silu", [P, 2, 2, D])
        ss = ph.sb("sums", [P, 3, 2 * 10])
        own, s_sz, s_ms, s_rt = ph.sem("chain"), ph.sem("silu"), ph.sem("mean"), ph.sem("root")
        with nc.Block() as block:
            @block.scalar
            def _(act):
                for t in range(2):
                    for j in range(2):
                        nc.scalar.activation(sz[:, t, j, :], p2[:, t, 1040 * j:1040 * j + 1024], ACT.Silu)\
                            .then_inc(s_sz, 1)
                act.wait_ge(s_ms, 1)
                nc.scalar.activation(ss[:, 2, :], ss[:, 1, :], ACT.Sqrt).then_inc(s_rt, 1)

            @block.vector
            def _(dve):
                ch = Chain(dve, own)
                dve.wait_ge(s_sz, 4)
                for t in range(2):
                    o, y = og[:, t, :], ys[:, t, :]
                    ch.link(nc.vector.tensor_tensor(y, y, sz[:, t, 1, :], ALU.mult))
                    for x, n, c in ((o, 8, 10 * t), (y, 2, 10 * t + 8)):
                        ch.link(nc.vector.tensor_tensor(sq[:, :], x, x, ALU.mult))
                        ch.link(nc.vector.tensor_reduce(ss[:, 0, c:c + n], sq[:, :].rearrange("p (h d) -> p h d", h=n),
                                                        AX.X, ALU.add))
                        ch.link(nc.vector.tensor_scalar(ss[:, 1, c:c + n], ss[:, 0, c:c + n], n / D, EPS,
                                                        ALU.mult, ALU.add))
                nc.vector.sem_inc(s_ms, 1)
                dve.wait_ge(s_rt, 1)
                ch.link(nc.vector.reciprocal(ss[:, 0, :], ss[:, 2, :]))
                for t in range(2):
                    o, y = og[:, t, :], ys[:, t, :]
                    for x, n, c in ((o, 8, 10 * t), (y, 2, 10 * t + 8)):
                        v = x.rearrange("p (h d) -> p h d", h=n)
                        ch.link(nc.vector.tensor_tensor(v, v, rep(ss[:, 0, c:c + n], D // n, 2), ALU.mult))
                    ov = o.rearrange("p (h d) -> p h d", h=8)
                    ch.link(nc.vector.tensor_tensor(ov, ov, rep(rows["gn"], 8), ALU.mult))
                    ch.link(nc.vector.tensor_tensor(mix[:, t, 0:D], o, sz[:, t, 0, :], ALU.mult))
                    ch.link(nc.vector.tensor_tensor(mix[:, t, D:2 * D], y, rows["sn"], ALU.mult))


def gemm_rows(g, name, n_chunks, actT, row):
    nc, ring = g.nc, g.ring
    with Phase(g, name) as ph:
        banks = ph.ps("bank", [P, 4, 512])
        own, s_o = ph.sem("chain"), ph.sem("out")
        done0 = ring.done
        with nc.Block() as block:
            @block.sync
            def _(sync):
                ring.issue(sync, n_chunks)

            @block.tensor
            def _(pe):
                for n in range(n_chunks):
                    wv = ring.take(pe)
                    for j in range(4):
                        for i in range(4):
                            mm = nc.tensor.matmul(banks[:, i, :], actT[:, 4 * n + j, (i // 2) * P:(i // 2 + 1) * P],
                                                  wv[:, j, (i % 2) * 512:(i % 2) * 512 + 512],
                                                  start=(n + j == 0), stop=(n == n_chunks - 1 and j == 3))
                    ring.mark(mm)

            @block.vector
            def _(dve):
                ch = Chain(dve, own)
                dve.wait_ge(ring.gemm_done, done0 + n_chunks)
                for i in range(4):
                    residual(g, lambda t: row, 0)(ch, 2 + i // 2, (i % 2) * 512, 512, banks[:, i, :]).then_inc(s_o, 1)
                dve.wait_ge(s_o, 4)


def router(g, rw, rb, iota, bdown, gates, acc):
    nc = g.nc
    with Phase(g, "router") as ph:
        w = ph.sb("w", [P, KT, N_EXP])
        bd = ph.sb("bd", [N_EXP, D])
        lg = ph.sb("logits", [P, 2, N_EXP])
        top = ph.sb("top", [P, 2, 8])
        idx = ph.sb("idx", [P, 2, 8], U32)
        idf = ph.sb("idxf", [P, 2, 8])
        st = ph.sb("stats", [P, 2, 8])
        tmp = ph.sb("onehot", [P, N_EXP])
        gT = ph.sb("gatesT", [N_EXP, 2, P])
        pl = ph.ps("logits", [P, 2, 512])
        pt = ph.ps("gatesT", [P, 2, 512])
        pb = ph.ps("bias", [P, 4, 512])
        s_ld, s_l, s_t, s_e, s_g, s_gt, s_gc, s_b, own = (ph.sem(x) for x in (
            "loaded", "logits", "top", "exp", "gates", "gatesT", "gatesT_copied", "bias", "chain"))
        with nc.Block() as block:
            @block.sync
            def _(sync):
                sync.dma_start(w[:, :, :], rw.rearrange("(a p) n -> p a n", p=P)).then_inc(s_ld, 16)
                sync.dma_start(bd[:, :], bdown).then_inc(s_ld, 16)

            @block.tensor
            def _(pe):
                pe.wait_ge(s_ld, 32)
                for t in range(2):
                    for kt in range(KT):
                        mm = nc.tensor.matmul(pl[:, t, 0:N_EXP], g.xT[:, kt, t * P:(t + 1) * P], w[:, kt, :],
                                              start=(kt == 0), stop=(kt == KT - 1))
                    mm.then_inc(s_l, 1)
                for t in range(2):
                    pe.wait_ge(s_g, t + 1)
                    nc.tensor.transpose(pt[0:N_EXP, t, 0:P], gates[:, t, :], blk(g, C_ID)).then_inc(s_gt, 1)
                for t in range(2):
                    pe.wait_ge(s_gc, t + 1)
                    for j in range(2):
                        nc.tensor.matmul(pb[:, 2 * t + j, :], gT[:, t, :], bd[:, j * 512:j * 512 + 512],
                                         start=True, stop=True).then_inc(s_b, 1)

            @block.scalar
            def _(act):
                for t in range(2):
                    act.wait_ge(s_t, t + 1)
                    nc.scalar.activation(top[:, t, 0:4], top[:, t, 0:4], ACT.Exp, bias=st[:, t, 0:1])\
                        .then_inc(s_e, 1)

            @block.vector
            def _(dve):
                ch = Chain(dve, own)
                for t in range(2):
                    dve.wait_ge(s_l, t + 1)
                    ch.link(nc.vector.tensor_tensor(lg[:, t, :], pl[:, t, 0:N_EXP], rb, ALU.add))
                    ch.link(nc.vector.max(top[:, t, :], lg[:, t, :]))
                    ch.link(nc.vector.max_index(idx[:, t, :], top[:, t, :], lg[:, t, :]))
                    ch.link(nc.vector.tensor_copy(idf[:, t, :], idx[:, t, :]))
                    nc.vector.tensor_scalar(st[:, t, 0:1], top[:, t, 0:1], -1.0, None, ALU.mult).then_inc(s_t, 1)
                for t in range(2):
                    dve.wait_ge(s_e, t + 1)
                    ch.link(nc.vector.tensor_reduce(st[:, t, 1:2], top[:, t, 0:4], AX.X, ALU.add))
                    ch.link(nc.vector.reciprocal(st[:, t, 2:3], st[:, t, 1:2]))
                    ch.link(nc.vector.tensor_scalar(st[:, t, 4:8], top[:, t, 0:4], st[:, t, 2:3], None, ALU.mult))
                    for k in range(4):
                        dst = gates[:, t, :] if k == 0 else tmp[:, :]
                        ch.link(nc.vector.tensor_scalar(dst, iota, idf[:, t, k:k + 1], st[:, t, 4 + k:5 + k],
                                                        ALU.is_equal, ALU.mult))
                        if k:
                            ch.link(nc.vector.tensor_tensor(gates[:, t, :], gates[:, t, :], tmp[:, :], ALU.add))
                    nc.vector.sem_inc(s_g, 1)
                for t in range(2):
                    dve.wait_ge(s_gt, t + 1)
                    nc.vector.tensor_copy(gT[:, t, :], pt[0:N_EXP, t, 0:P]).then_inc(s_gc, 1)
                for i in range(4):
                    dve.wait_ge(s_b, i + 1)
                    ch.mark(nc.vector.tensor_copy(acc[:, i // 2, (i % 2) * 512:(i % 2) * 512 + 512], pb[:, i, :]))
                ch.wait()


EXP_CHUNKS = 6
EXP_FREED = (4, 4, 8, 8, 9, 10)
EXP_UNITS = 10


def experts(g, w_gu, w_down, bgu, gates, acc):
    nc, ring = g.nc, g.ring
    base, done0 = ring.used, ring.done
    assert SLOTS == 3 and ring.issued == base + SLOTS
    with Phase(g, "experts") as ph:
        hid = ph.sb("hidden", [P, KT, 256])
        bc = ph.sb("bias", [P, 16])
        gc = ph.sb("gates", [P, 2])
        gt = ph.sb("gate", [P, 2, 256])
        up = ph.sb("up", [P, 2, 256])
        sg = ph.sb("sigmoid", [P, 2, 256])
        pg = ph.ps("gu", [P, 4, 512])
        pd = ph.ps("down", [P, 4, 512])
        own, s_gt, s_up, s_sg, s_h, s_acc = (ph.sem(x) for x in ("chain", "gate", "up", "sigmoid", "hidden", "acc"))
        s_hp = ph.sem("half")

        def src(e, j):
            if j < 4:
                c = 1024 * (j % 2) + 512 * (j // 2)
                return w_gu[bass.ds(e, 1), :, c:c + 512].rearrange("e (a p) n -> p (e a) n", p=P)
            r = 512 * (j - 4)
            return w_down[bass.ds(e, 1), r:r + 512, :].rearrange("e (a p) n -> p (e a) n", p=P)

        def place(j):
            b = ring.buf[:, (base + j) % SLOTS, :]
            return b.rearrange("p (a b) -> p a b", a=8 if j % EXP_CHUNKS < 4 else 4)

        with nc.Block() as block:
            @block.sync
            def _(sync):
                def load(e, e_src, j):
                    sync.wait_ge(ring.gemm_done, e * EXP_UNITS + (done0 + EXP_FREED[j - 3]))
                    sync.dma_start(place(j), src(e_src, j % EXP_CHUNKS)).then_inc(ring.loaded[(base + j) % SLOTS], 16)

                with sync.Fori(0, N_EXP - 1) as e:
                    for j in range(3, 9):
                        load(e, e + (1 if j >= 6 else 0), j)
                for j in range(3, 6):
                    load(N_EXP - 1, N_EXP - 1, j)

            @block.tensor
            def _(pe):
                with pe.Fori(0, N_EXP) as e:
                    def arrived(j):
                        i = base + j
                        pe.wait_ge(ring.loaded[i % SLOTS], e * 32 + 16 * (i // SLOTS + 1))

                    for half in range(2):
                        arrived(2 * half)
                        arrived(2 * half + 1)
                        for j in range(4):
                            f = 4 * half + j
                            if f >= 4:
                                pe.wait_ge(s_up, e * 8 + (f - 3))
                            else:
                                pass
                            for q in range(2):
                                wv = place(2 * half + q)
                                for kt in range(KT):
                                    mm = nc.tensor.matmul(pg[:, f % 4, q * 256:q * 256 + 256],
                                                          wv[:, kt, j * P:(j + 1) * P], g.xT[:, kt, 0:256],
                                                          start=(kt == 0), stop=(kt == KT - 1))
                            mm.then_inc(ring.gemm_done, 1)
                    pe.wait_ge(s_acc, e * 4 + 4)
                    for half in range(2):
                        arrived(4 + half)
                        wv = place(4 + half)
                        for j in range(4):
                            f = 4 * half + j
                            pe.wait_ge(s_h, e * 8 + (f + 1))
                            for i in range(4):
                                mm = nc.tensor.matmul(pd[:, i, :], hid[:, f, (i // 2) * P:(i // 2 + 1) * P],
                                                      wv[:, j, (i % 2) * 512:(i % 2) * 512 + 512],
                                                      start=(f == 0), stop=(f == KT - 1))
                        mm.then_inc(ring.gemm_done, 1)

            @block.scalar
            def _(act):
                with act.Fori(0, N_EXP) as e:
                    for f in range(8):
                        act.wait_ge(s_gt, e * 8 + (f + 1))
                        nc.scalar.activation(sg[:, f % 2, :], gt[:, f % 2, :], ACT.Sigmoid, scale=SWI_ALPHA)\
                            .then_inc(s_sg, 1)

            @block.gpsimd
            def _(pool):
                with pool.Fori(0, N_EXP) as e:
                    for f in range(8):
                        pool.wait_ge(s_sg, e * 8 + (f + 1))
                        nc.gpsimd.tensor_tensor(sg[:, f % 2, :], sg[:, f % 2, :], gt[:, f % 2, :], ALU.mult)\
                            .then_inc(s_hp, 1)
                        pool.wait_ge(s_hp, e * 8 + (f + 1))
                        pool.wait_ge(s_up, e * 8 + (f + 1))
                        nc.gpsimd.tensor_tensor(hid[:, f, :], sg[:, f % 2, :], up[:, f % 2, :], ALU.mult)\
                            .then_inc(s_h, 1)

            @block.vector
            def _(dve):
                nc.vector.sem_inc(s_acc, 4)
                with dve.Fori(0, N_EXP) as e:
                    dve.wait_ge(s_acc, e * 4 + 4)
                    nc.vector.tensor_copy(bc[:, :], bgu[:, bass.ds(e * 16, 16)]).then_inc(own, 1)
                    nc.vector.tensor_copy(gc[:, :], gates[:, :, bass.ds(e, 1)].rearrange("p t o -> p (t o)"))\
                        .then_inc(own, 1)
                    dve.wait_ge(own, e * 10 + 2)
                    for f in range(8):
                        dve.wait_ge(ring.gemm_done, e * EXP_UNITS + (done0 + f + 1))
                        if f >= 2:
                            dve.wait_ge(s_h, e * 8 + (f - 1))
                        nc.vector.tensor_scalar(gt[:, f % 2, :], pg[:, f % 4, 0:256], bc[:, f:f + 1], SWI_LIMIT,
                                                ALU.add, ALU.min).then_inc(s_gt, 1)
                        nc.vector.tensor_scalar(up[:, f % 2, :], pg[:, f % 4, 256:512], bc[:, 8 + f:9 + f], SWI_LIMIT,
                                                ALU.add, ALU.min).then_inc(own, 1)
                        dve.wait_ge(own, e * 10 + (3 + f))
                        nc.vector.tensor_scalar(up[:, f % 2, :], up[:, f % 2, :], -SWI_LIMIT, 1.0,
                                                ALU.max, ALU.add).then_inc(s_up, 1)
                    dve.wait_ge(ring.gemm_done, e * EXP_UNITS + (done0 + EXP_UNITS))
                    for i in range(4):
                        a = acc[:, i // 2, (i % 2) * 512:(i % 2) * 512 + 512]
                        nc.vector.scalar_tensor_tensor(out=a, in0=pd[:, i, :], scalar=gc[:, i // 2:i // 2 + 1], in1=a,
                                                       op0=ALU.mult, op1=ALU.add).then_inc(s_acc, 1)
                dve.wait_ge(s_acc, 4 * N_EXP + 4)
    ring.used += EXP_CHUNKS * N_EXP
    ring.done += EXP_UNITS * N_EXP


def final(g, acc, gate_row, final_row, out):
    nc = g.nc
    with Phase(g, "final") as ph:
        sq = ph.sb("square", [P, D])
        ss = ph.sb("sums", [P, 4, 2])
        own, s_x, s_ss, s_ms, s_rt, s_y, s_out = (ph.sem(x) for x in ("chain", "x", "sum", "mean", "root", "y", "out"))
        with nc.Block() as block:
            @block.vector
            def _(dve):
                ch = Chain(dve, own)
                for t in range(2):
                    a = acc[:, t, :]
                    ch.link(nc.vector.tensor_tensor(a, a, gate_row, ALU.mult))
                    nc.vector.tensor_tensor(g.x[:, 2 + t, :], g.x[:, 2 + t, :], a, ALU.add).then_inc(s_x, 1)
                dve.wait_ge(s_ss, 2)
                nc.vector.tensor_scalar(ss[:, 1, :], ss[:, 0, :], 1.0 / D, EPS, ALU.mult, ALU.add).then_inc(s_ms, 1)
                dve.wait_ge(s_rt, 1)
                ch.link(nc.vector.reciprocal(ss[:, 3, :], ss[:, 2, :]))
                for t in range(2):
                    nc.vector.scalar_tensor_tensor(out=acc[:, t, :], in0=g.x[:, 2 + t, :], scalar=ss[:, 3, t:t + 1],
                                                   in1=final_row, op0=ALU.mult, op1=ALU.mult).then_inc(s_y, 1)

            @block.scalar
            def _(act):
                for t in range(2):
                    act.wait_ge(s_x, t + 1)
                    nc.scalar.activation(sq[:, :], g.x[:, 2 + t, :], ACT.Square, accum_out=ss[:, 0, t:t + 1])\
                        .then_inc(s_ss, 1)
                    act.wait_ge(s_ss, t + 1)
                act.wait_ge(s_ms, 1)
                nc.scalar.activation(ss[:, 2, :], ss[:, 1, :], ACT.Sqrt).then_inc(s_rt, 1)

            @block.sync
            def _(sync):
                for t in range(2):
                    sync.wait_ge(s_y, t + 1)
                    sync.dma_start(out[0, t * P:(t + 1) * P, :], acc[:, t, :]).then_inc(s_out, 16)
                sync.wait_ge(s_out, 32)


def load(g, name, jobs):
    nc = g.nc
    with Phase(g, name) as ph:
        s = ph.sem("loaded")
        with nc.Block() as block:
            @block.sync
            def _(sync):
                for dst, src in jobs:
                    sync.dma_start(dst, src).then_inc(s, 16)
                sync.wait_ge(s, 16 * len(jobs))


def copy_to(g, dst):
    def out(ch, t, c0, w, ps):
        return g.nc.vector.tensor_copy(dst(t, c0, w), ps)
    return out


def row(ap):
    return ap.partition_broadcast(P)


def layer0(g, a):
    nc = g.nc
    adaln(g, "ada0", a["cond_col"], a["adab_col"][0], g.mod)
    mod = lambda j, t: g.mod[:, 8 * j:8 * j + 8, 0 if t >= 2 else 1]
    norm_T(g, "norm0a", ALL_TILES, g.xT, lambda t: mod(1, t), lambda t: mod(0, t))
    with ExitStack() as outer:
        osb = lambda n, s, dt=F32: outer.enter_context(nc.sbuf_tensor(n, s, dt))
        pb = osb("projB", [P, TT, 2064])
        gates = osb("gates", [P, TT, 16])
        small = osb("small", [P, 16 + 64 + 64])
        cat = g.xT[:, :, :].rearrange("p a b -> p (a b)").rearrange("p (t c) -> p t c", t=TT)
        with ExitStack() as inner:
            isb = lambda n, s, dt=F32: inner.enter_context(nc.sbuf_tensor(n, s, dt))
            pa = isb("projA", [P, TT, 1536])
            rope = isb("rope", [P, 2, 2, ML_D])
            load(g, "ldab", [(small[:, 0:16], row(a["gate_b"])), (small[:, 16:80], row(a["qn"])),
                             (small[:, 80:144], row(a["kn"])), (rope[:, :, :, :], a["rope"])])
            gemm_tok(g, "projAB", widths(AB_W), lambda kt, t: g.xT[:, kt, t * P:(t + 1) * P], ALL_TILES,
                     copy_to(g, lambda t, c0, w: pa[:, t, c0:c0 + w] if c0 < 1536
                             else pb[:, t, c0 - 1536:c0 - 1536 + w]))
            ab_prepare(g, pa, pb, small, rope, gates)
            qT = isb("qaT", [P, 4, 512])
            kT = isb("kaT", [P, 4, 512])
            turn(g, "turnA", [(pa[:, t, o + p * P:o + (p + 1) * P], dst[:, p, t * P:(t + 1) * P])
                              for t in ALL_TILES for o, dst in ((0, qT), (512, kT)) for p in range(4)])
            attention(g, pa, qT, kT, cat, a["rpb_cols"], a["window"])
        with ExitStack() as inner:
            isb = lambda n, s, dt=F32: inner.enter_context(nc.sbuf_tensor(n, s, dt))
            qT = isb("qbT", [P, 4, 512])
            kT = isb("kbT", [P, 4, 512])
            hs = isb("hs", [P, TT, 512])
            rowg = isb("rowg", [4, 4, 512])
            rowo = isb("rowo", [4, 6, 512])
            colg = isb("colg", [P, TT, 4, ML_H])
            sel = isb("sel", [4, 4, P])
            head_row = isb("head_row", [P, 512])
            turn(g, "turnB", [(pb[:, t, o + h * P:o + (h + 1) * P], dst[:, h, t * P:(t + 1) * P])
                              for t in ALL_TILES for o, dst in ((0, qT), (512, kT)) for h in range(4)]
                 + [(gates[:, t, 4 * q:4 * q + 4], rowg[:, q, t * P:(t + 1) * P]) for t in ALL_TILES for q in range(4)])
            load(g, "ldsel", [(sel[:, :, :], a["sel"]), (head_row[:, :], row(a["headn"]))])
            mlstm_rows(g, rowg, rowo, None)
            turn_small(g, "turnC", [(rowo[0:4, q, t * P:(t + 1) * P], colg[:, t, q, :])
                                    for t in ALL_TILES for q in range(4)])
            mlstm(g, pb, qT, kT, rowo, colg, sel, hs)
            ab_merge(g, pb, hs, head_row[:, :], cat)
    with ExitStack() as outer:
        osb = lambda n, s, dt=F32: outer.enter_context(nc.sbuf_tensor(n, s, dt))
        rows = osb("gate_rows0", [P, 4, D])
        gate_rows(g, "rows0", [lambda kt, j=j, i=i: g.mod[:, 8 * j + kt, i:i + 1] for j, i in
                               ((2, 0), (2, 1), (5, 0), (5, 1))], rows)
        with ExitStack() as inner:
            catT = inner.enter_context(nc.sbuf_tensor("catT", [P, KT, 512], F32))
            turn(g, "turnD", [(cat[:, t, k * P:(k + 1) * P], catT[:, k, t * P:(t + 1) * P])
                              for t in ALL_TILES for k in range(KT)])
            gemm_tok(g, "about", widths(D), lambda kt, t: catT[:, kt, t * P:(t + 1) * P], ALL_TILES,
                     residual(g, lambda t: rows[:, 0 if t >= 2 else 1, :], 0))
        norm_T(g, "norm0m", ALL_TILES, g.xT, lambda t: mod(4, t), lambda t: mod(3, t))
        mlp(g, "mlp0", ALL_TILES, lambda t: rows[:, 2 if t >= 2 else 3, :])


def turn_small(g, name, jobs):
    nc = g.nc
    with Phase(g, name) as ph:
        ps = ph.ps("turned", [P, len(jobs), 4])
        s, own = ph.sem("turned"), ph.sem("chain")
        with nc.Block() as block:
            @block.tensor
            def _(pe):
                for i, (src, dst) in enumerate(jobs):
                    nc.tensor.transpose(ps[:, i, :], src, blk(g, C_ID)[0:4, 0:4]).then_inc(s, 1)

            @block.vector
            def _(dve):
                dve.wait_ge(s, len(jobs))
                for i, (src, dst) in enumerate(jobs):
                    nc.vector.tensor_copy(dst, ps[:, i, :]).then_inc(own, 1)
                dve.wait_ge(own, len(jobs))


def layer1(g, a):
    nc = g.nc
    adaln(g, "ada1", a["cond_col"], a["adab_col"][1], g.mod)
    mod = lambda j, t: g.mod[:, 8 * j:8 * j + 8, 0 if t >= 2 else 1]
    norm_T(g, "norm1a", ALL_TILES, g.xT, lambda t: mod(1, t), lambda t: mod(0, t))
    scr = {n: nc.dram_tensor(f"rw_{n}", [2 if n == "r" else 4, P, D], F32, kind="Internal").ap()
           for n in ("k", "v", "kk", "r")}
    with ExitStack() as outer:
        osb = lambda n, s, dt=F32: outer.enter_context(nc.sbuf_tensor(n, s, dt))
        low_w = osb("low_w", [P, 512])
        low_a = osb("low_a", [P, 512])
        sg0 = osb("sg0", [P, 256])
        sg1 = osb("sg1", [32, 256])
        y = osb("rw_y", [P, 2, D])
        coef = osb("coef", [P, 2, 2, RW_H])
        with ExitStack() as inner:
            isb = lambda n, s, dt=F32: inner.enter_context(nc.sbuf_tensor(n, s, dt))
            xx = isb("xx", [P, KT, 512])
            xs = isb("xs", [P, KT, 512])
            stage = isb("stage", [P, TT, D])
            mu = isb("mu", [P, 6, KT])
            kkrow = isb("kkrow", [P, D])
            load(g, "ldmu", [(mu[:, :, :], a["mu_col"]), (kkrow[:, :], row(a["k_k"]))])
            rw_shift(g, xx)
            lhs = lambda kt, t: xs[:, kt, t * P:(t + 1) * P]
            to_stage = copy_to(g, lambda t, c0, w: stage[:, t, c0:c0 + w])
            for n, m, tiles in (("k", 2, ALL_TILES), ("v", 3, ALL_TILES), ("r", 0, LAT_TILES)):
                rw_mix(g, f"mix_{n}", xx, xs, mu[:, m, :])
                gemm_tok(g, f"proj_{n}", widths(D), lhs, tiles, to_stage)
                store(g, f"store_{n}", [(scr[n][t - tiles[0]], stage[:, t, :]) for t in tiles])
                if n == "k":
                    kk = isb("kk", [P, TT, D])
                    rw_kk(g, stage, kk, kkrow[:, :])
                    store(g, "store_kk", [(scr["kk"][t], kk[:, t, :]) for t in tiles])
            rw_mix(g, "mix_w", xx, xs, mu[:, 1, :])
            rw_lora(g, "lora_w", a["w1"], xs, 0, [(0, 128, low_w[:, :])], ACT.Tanh)
            rw_mix(g, "mix_a", xx, xs, mu[:, 4, :])
            rw_lora(g, "lora_a", a["a1"], xs, 0, [(0, 128, low_a[:, :])], ACT.Copy)
            rw_mix(g, "mix_g", xx, xs, mu[:, 5, :])
            rw_lora(g, "lora_g", a["g1"], xs, 256, [(0, 128, sg0[:, :]), (128, 160, sg1[:, :])], ACT.Sigmoid)
        with ExitStack() as inner:
            isb = lambda n, s, dt=F32: inner.enter_context(nc.sbuf_tensor(n, s, dt))
            w2 = isb("w2", [P, D])
            a2 = isb("a2", [P, D])
            w0 = isb("w0", [P, 2, D])
            a0 = isb("a0", [P, 2, D])
            ka = isb("ka", [P, D])
            rk = isb("rk", [P, D])
            load(g, "ldrw", [(w2[:, :], a["w2"]), (a2[:, :], a["a2"])]
                 + [(w0[:, z, :], row(a["w0"][z])) for z in range(2)]
                 + [(a0[:, z, :], row(a["a0"][z])) for z in range(2)]
                 + [(ka[:, :], row(a["k_a"])), (rk[:, :], row(a["r_k"]))])
            rw_chunks(g, scr, low_w, low_a, w2, a2, {"w0": w0, "a0": a0, "ka": ka[:, :], "rk": rk[:, :]}, y, coef)
        rows = osb("gate_rows1", [P, 2, D])
        gate_rows(g, "rows1", [lambda kt, j=j: g.mod[:, 8 * j + kt, 0:1] for j in (2, 5)], rows)
        with ExitStack() as inner:
            isb = lambda n, s, dt=F32: inner.enter_context(nc.sbuf_tensor(n, s, dt))
            v = isb("v_lat", [P, 2, D])
            lw = isb("lw", [P, D])
            lb = isb("lb", [P, D])
            g2a = isb("g2a", [P, D])
            g2b = isb("g2b", [32, D])
            ro = isb("readout", [P, 2, D])
            roT = isb("readoutT", [P, KT, 256])
            load(g, "ldro", [(v[:, t, :], scr["v"][2 + t]) for t in range(2)]
                 + [(lw[:, :], row(a["lnx_w"])), (lb[:, :], row(a["lnx_b"])), (g2a[:, :], a["g2"][0:P, :]),
                    (g2b[:, :], a["g2"][P:G_LORA, :])])
            rw_readout(g, y, coef, v, {"lw": lw[:, :], "lb": lb[:, :]}, sg0, sg1, g2a, g2b, ro)
            turn(g, "turnE", [(ro[:, t, k * P:(k + 1) * P], roT[:, k, t * P:(t + 1) * P])
                              for t in range(2) for k in range(KT)])
            gemm_tok(g, "rwout", widths(D), lambda kt, t: roT[:, kt, (t - 2) * P:(t - 1) * P], LAT_TILES,
                     residual(g, lambda t: rows[:, 0, :], 0))
        norm_T(g, "norm1m", LAT_TILES, g.xT, lambda t: mod(4, t), lambda t: mod(3, t))
        mlp(g, "mlp1", LAT_TILES, lambda t: rows[:, 1, :])


def block2(g, a, out):
    nc = g.nc
    adaln(g, "ada2", a["cond2_col"], a["adab2_col"], g.mod)
    mod = lambda j, t: g.mod[:, 8 * j:8 * j + 8, 0]
    with ExitStack() as outer:
        osb = lambda n, s, dt=F32: outer.enter_context(nc.sbuf_tensor(n, s, dt))
        gains = osb("gains", [P, 2, KT])
        load(g, "ldgain", [(gains[:, :, :], a["norm_g_col"])])
        norm_T(g, "norm2a", LAT_TILES, g.xT, lambda t: mod(1, t), lambda t: mod(0, t), gains[:, 0, :], off=2)
        with ExitStack() as mid:
            msb = lambda n, s, dt=F32: mid.enter_context(nc.sbuf_tensor(n, s, dt))
            p2 = msb("proj2", [P, 2, 2080])
            og = msb("og", [P, 2, D])
            ys = msb("ys", [P, 2, D])
            gemm_tok(g, "proj2", widths(2064) + [16], lambda kt, t: g.xT[:, kt, (t - 2) * P:(t - 1) * P], LAT_TILES,
                     copy_to(g, lambda t, c0, w: p2[:, t - 2, c0:c0 + w]))
            with ExitStack() as inner:
                isb = lambda n, s, dt=F32: inner.enter_context(nc.sbuf_tensor(n, s, dt))
                feat = isb("feat", [P, 36, 256])
                taps = isb("taps", [P, 36, 4])
                cbias = isb("cbias", [P, 36])
                small = isb("small2", [P, 64])
                beta = isb("beta", [P, 2, 8])
                dt = isb("dt", [P, 2, SS_H])
                ga = isb("ga", [P, 2, 24])
                cums = isb("cums", [P, 4, 24])
                load(g, "ldconv", [(taps[:, :, :], a["taps_col"]), (cbias[:, :], a["cbias_col"]),
                                   (small[:, :], row(a["small2"]))])
                gd_conv(g, feat, taps, cbias)
                gd_l2(g, feat)
                gd_gates(g, p2, small, beta, dt, ga, cums)
                with ExitStack() as deep:
                    xtok = deep.enter_context(nc.sbuf_tensor("xtok", [P, 2, D], F32))
                    turn(g, "turnF", [(feat[:, 24 + f, t * P:(t + 1) * P], xtok[:, t, f * P:(f + 1) * P])
                                      for f in range(8) for t in range(2)])
                    ssd(g, feat, xtok, dt, ga, cums, small[:, 48:64], ys)
                with ExitStack() as deep:
                    ktok = deep.enter_context(nc.sbuf_tensor("ktok", [P, 2, D], F32))
                    vtok = deep.enter_context(nc.sbuf_tensor("vtok", [P, 2, D], F32))
                    turn(g, "turnG", [(feat[:, 8 + 8 * v + f, t * P:(t + 1) * P], dst[:, t, f * P:(f + 1) * P])
                                      for v, dst in enumerate((ktok, vtok)) for f in range(8) for t in range(2)])
                    gd_chunks(g, feat, ktok, vtok, beta, ga, cums, og)
            with ExitStack() as inner:
                isb = lambda n, s, dt=F32: inner.enter_context(nc.sbuf_tensor(n, s, dt))
                mix = isb("mix", [P, 2, 2 * D])
                gn = isb("gn", [P, P])
                sn = isb("sn", [P, D])
                load(g, "ldmix", [(gn[:, :], row(a["gdn_norm_g"])), (sn[:, :], row(a["ssd_norm_g"]))])
                gd_merge(g, p2, og, ys, {"gn": gn[:, :], "sn": sn[:, :]}, mix)
                mixT = isb("mixT", [P, 16, 256])
                turn(g, "turnH", [(mix[:, t, k * P:(k + 1) * P], mixT[:, k, t * P:(t + 1) * P])
                                  for t in range(2) for k in range(16)])
                rows = isb("gate_rows2", [P, 1, D])
                gate_rows(g, "rows2", [lambda kt: g.mod[:, 16 + kt, 0:1]], rows)
                gemm_rows(g, "mixout", 4, mixT, rows[:, 0, :])
        norm_T(g, "norm2m", LAT_TILES, g.xT, lambda t: mod(4, t), lambda t: mod(3, t), gains[:, 1, :], off=2)
        acc = osb("moe_acc", [P, 2, D])
        gates = osb("moe_gates", [P, 2, N_EXP])
        bgu = osb("bgu", [P, N_EXP * 16])
        rb = osb("rb", [P, 2 * N_EXP])
        rows = osb("rows3", [P, 1, D])
        fin = osb("final_g", [P, D])
        load(g, "ldmoe", [(bgu[:, :], a["bgu_col"]), (rb[:, :], row(a["rb_iota"])), (fin[:, :], row(a["final_g"]))])
        gate_rows(g, "rows3", [lambda kt: g.mod[:, 40 + kt, 0:1]], rows)
        router(g, a["router_w"], rb[:, 0:N_EXP], rb[:, N_EXP:], a["b_down"], gates, acc)
        experts(g, a["w_gu"], a["w_down"], bgu, gates, acc)
        final(g, acc, rows[:, 0, :], fin[:, :], out)


def program(nc, a, out, parts=(0, 1, 2), x_out=None):
    g = G()
    g.nc = nc
    g.const = nc.alloc_sbuf_tensor("const", [P, N_BLOCKS * P], F32)
    g.x = nc.alloc_sbuf_tensor("x", [P, TT, D], F32)
    g.xT = nc.alloc_sbuf_tensor("xT", [P, KT, 512], F32)
    g.tmp = nc.alloc_sbuf_tensor("tmp", [P, D], F32)
    g.mod = nc.alloc_sbuf_tensor("mod", [P, 48, 2], F32)
    g.ring = ring = Ring(nc)
    if 0 in parts:
        plan_cols(ring, a["ada_w"][0], 6 * D, 1)
        plan_cols(ring, a["ab_w_in"], AB_W, 4)
        plan_cols(ring, a["ab_w_out"], D, 4)
        plan_cols(ring, a["mlp_w1"][0], D_FF, 4)
        plan_rows(ring, a["mlp_w2"][0], 1)
    if 1 in parts:
        plan_cols(ring, a["ada_w"][1], 6 * D, 1)
        for i, u in ((1, 4), (2, 4), (0, 2)):
            plan_cols(ring, a["w_rkv"][i], D, u)
        plan_cols(ring, a["rw_w_o"], D, 2)
        plan_cols(ring, a["mlp_w1"][1], D_FF, 4)
        plan_rows(ring, a["mlp_w2"][1], 1)
    if 2 in parts:
        plan_cols(ring, a["ada_w2"], 6 * D, 1)
        plan_cols(ring, a["w_in2"][:, 3072:5136], 2064, 2)
        plan_cols(ring, a["w_in2"][:, 6672:6688], 16, 2)
        plan_cols(ring, a["w_in2"][:, 0:3072], 3072, 4)
        plan_cols(ring, a["w_in2"][:, 5136:6672], 1536, 4)
        plan_rows(ring, a["w_out2"], 1)
        wv = a["w_gu"][0].rearrange("(a p) n -> p a n", p=P)
        for c in (0, 1024, 512):
            ring.add(wv[:, :, c:c + 512], 0)
    xin = {t: a["ctx"][t * P:(t + 1) * P, :] if t < 2 else a["x"][(t - 2) * P:(t - 1) * P, :] for t in range(TT)}
    load(g, "ldx", [(g.const[:, :], a["const"])] + [(g.x[:, t, :], xin[t]) for t in range(TT)])
    if 0 in parts:
        layer0(g, a)
    if 1 in parts:
        layer1(g, a)
    if 2 in parts:
        block2(g, a, out)
    if x_out is not None:
        store(g, "stx", [(x_out[t], g.x[:, t, :]) for t in range(TT)])


def layout(i):
    def col(v, n=P):
        v = np.asarray(v)
        v = v.reshape(*v.shape[:-1], v.shape[-1] // n, n)
        return np.ascontiguousarray(np.moveaxis(v, -1, 0))

    f = np.asarray
    pad = np.zeros((NA_H, 15, 127), np.float32)
    pad[:, :, 48:79] = f(i["na_rpb"])[0]
    c = np.arange(GRID_W)
    rpb_cols = pad[:, 4:11][:, :, c[None, :] - c[:, None] + 63]
    sel = np.zeros((4, 4, P), np.float32)
    for h in range(4):
        sel[h, h, :] = 1.0
    z_r = lambda w: np.ascontiguousarray(f(w)[0].transpose(1, 0, 2).reshape(D, P).reshape(KT, P, P).transpose(1, 0, 2))
    conv = np.concatenate([f(i["gdn_conv_w_2"])[0], f(i["ssd_conv_w_2"])[0]], axis=1)
    b_gu = f(i["moe_b_gu_2"])[0]
    return {
        "x": f(i["x"])[0], "ctx": f(i["ctx"])[0],
        "cond_col": np.stack([col(f(i["c"])[0]), col(f(i["c_ctx"]))], axis=2),
        "cond2_col": np.stack([col(f(i["c_2"])[0])] * 2, axis=2),
        "adab_col": np.stack([col(f(i["ada_b"])[l]) for l in range(2)]), "adab2_col": col(f(i["ada_b_2"])[0]),
        "ada_w": f(i["ada_w"]), "ab_w_in": f(i["ab_w_in"])[0], "ab_w_out": f(i["ab_w_out"])[0],
        "mlp_w1": f(i["mlp_w1"]), "mlp_w2": f(i["mlp_w2"]),
        "gate_b": f(i["ab_gate_b"])[0], "qn": f(i["na_q_norm"])[0], "kn": f(i["na_k_norm"])[0],
        "rpb_cols": rpb_cols, "headn": f(i["ml_head_norm"])[0].reshape(-1),
        "mu_col": col(f(i["rw_mu"])[0]), "w_rkv": f(i["rw_w_rkv"])[0],
        "w1": z_r(i["rw_w1"]), "a1": z_r(i["rw_a1"]),
        "g1": np.ascontiguousarray(f(i["rw_g1"])[0].reshape(KT, P, G_LORA).transpose(1, 0, 2)),
        "w2": f(i["rw_w2"])[0].reshape(P, D), "a2": f(i["rw_a2"])[0].reshape(P, D),
        "g2": f(i["rw_g2"])[0], "w0": f(i["rw_w0"])[0], "a0": f(i["rw_a0"])[0],
        "k_k": f(i["rw_k_k"])[0], "k_a": f(i["rw_k_a"])[0], "r_k": f(i["rw_r_k"])[0],
        "lnx_w": f(i["rw_lnx_w"])[0], "lnx_b": f(i["rw_lnx_b"])[0], "rw_w_o": f(i["rw_w_o"])[0],
        "ada_w2": f(i["ada_w_2"])[0], "w_in2": f(i["w_in_2"])[0], "w_out2": f(i["w_out_2"])[0],
        "norm_g_col": np.stack([col(f(i["norm1_g_2"])[0]), col(f(i["norm2_g_2"])[0])], axis=1),
        "taps_col": np.ascontiguousarray(conv.reshape(4, 36, P).transpose(2, 1, 0)),
        "cbias_col": np.concatenate([np.zeros((P, 24), np.float32), col(f(i["ssd_conv_b_2"])[0])], axis=1),
        "small2": np.concatenate([f(i[n])[0] for n in ("gdn_dt_bias_2", "ssd_dt_bias_2", "gdn_a_log_2",
                                                         "ssd_a_log_2", "ssd_d_2")]),
        "gdn_norm_g": f(i["gdn_norm_g_2"])[0], "ssd_norm_g": f(i["ssd_norm_g_2"])[0],
        "router_w": f(i["router_w_2"])[0],
        "rb_iota": np.concatenate([f(i["router_b_2"])[0], np.arange(N_EXP, dtype=np.float32)]),
        "w_gu": f(i["moe_w_gu_2"])[0], "w_down": f(i["moe_w_down_2"])[0], "b_down": f(i["moe_b_down_2"])[0],
        "bgu_col": np.ascontiguousarray(b_gu.reshape(N_EXP * 16, P).T), "final_g": f(i["final_g_2"]),
        "const": const_table(), "rope": rope_table(), "window": window_table(), "sel": sel,
    }


def kernel(**inputs):
    import concourse.bacc as bacc
    from concourse.bass_utils import run_bass_kernel_spmd

    nc = bacc.Bacc("TRN2", target_bir_lowering=False, num_devices=1)
    arrays = {f"in_{k}": np.ascontiguousarray(v) for k, v in layout(inputs).items()}
    aps = {k[3:]: nc.dram_tensor(k, v.shape, F32, kind="ExternalInput").ap() for k, v in arrays.items()}
    out = nc.dram_tensor("out", (1, 256, D), F32, kind="ExternalOutput").ap()
    program(nc, aps, out)
    r = run_bass_kernel_spmd(nc, [arrays], core_ids=[0])
    return r.results[0]["out"]
```

```python
import math
from contextlib import ExitStack

import numpy as np

import concourse.bass as bass
from concourse import mybir

F32 = mybir.dt.float32
U32 = mybir.dt.uint32
I32 = mybir.dt.int32
BF16 = mybir.dt.bfloat16
F32R = mybir.dt.float32r
ALU = mybir.AluOpType
ACT = mybir.ActivationFunctionType
AX = mybir.AxisListType

P = 128
D = 1024
KT = D // P
TT = 4
CTX_TILES = (0, 1)
LAT_TILES = (2, 3)
ALL_TILES = (0, 1, 2, 3)
EPS = 1e-6
SLOTS = 3
SLOT = KT * 512

NA_H, NA_D = 8, 64
ML_H, ML_D = 4, 128
AB_W = 3 * 512 + 4 * 512 + 16
GRID_W, NA_KW, NA_KH = 64, 16, 8
GATE_CAP = 15.0
RW_H, RW_D = 16, 64
GN_EPS = 64e-5
G_LORA = 160
D_FF = 4096
GD_H = 8
SS_H, SS_P, SS_G = 16, 64, 2
CONV_CH_Q = 3072
CONV_CH_S = 1536
N_EXP, TOP_K = 32, 4
SWI_ALPHA, SWI_LIMIT = 1.702, 7.0
LEVELS = 7

C_ID, C_UP, C_UPS, C_LO, C_LOS, C_ONE = range(6)
C_LVL = 6
N_BLOCKS = 6 + 2 * LEVELS


def const_table():
    r, c = np.arange(P)[:, None], np.arange(P)[None, :]
    blocks = [r == c, r <= c, r < c, r >= c, r > c, r >= 0 * c]
    lower = []
    for level in range(LEVELS):
        b = 1 << level
        lower.append((r // (2 * b) == c // (2 * b)) & (r % (2 * b) >= b) & (c % (2 * b) < b))
    blocks += lower + [m.T for m in lower]
    return np.concatenate([np.broadcast_to(b, (P, P)) for b in blocks], axis=1).astype(np.float32)


def rope_table():
    pos = np.arange(256)
    inv = (np.float32(10000.0) ** (-np.arange(32, dtype=np.float32) / 32)).astype(np.float32)
    out = np.zeros((256, 2, ML_D), np.float32)
    for half, p in enumerate((pos // GRID_W, pos % GRID_W)):
        ang = p.astype(np.float32)[:, None] * inv
        o = 64 * half
        out[:, 0, o:o + 32] = out[:, 0, o + 32:o + 64] = np.cos(ang)
        out[:, 1, o:o + 32], out[:, 1, o + 32:o + 64] = -np.sin(ang), np.sin(ang)
    return np.ascontiguousarray(out.reshape(2, P, 2, ML_D).transpose(1, 0, 2, 3))


def window_table():
    c = np.arange(GRID_W)
    start = np.clip(c - NA_KW // 2, 0, GRID_W - NA_KW)[:, None]
    ok = (c[None, :] >= start) & (c[None, :] < start + NA_KW)
    return np.where(ok, 0.0, -1e30).astype(np.float32)


class Take:

    def __init__(self, eng):
        self.eng = eng
        self.n = {}

    def __call__(self, sem, k=1):
        self.n[sem.name] = self.n.get(sem.name, 0) + k
        self.eng.wait_ge(sem, self.n[sem.name])

    def skip_first(self, sem, first, k=1):
        seen = self.n.get("uses " + sem.name, 0)
        self.n["uses " + sem.name] = seen + 1
        if seen >= first:
            self(sem, k)


class Phase:

    def __init__(self, g, name):
        self.g, self.nc, self.name = g, g.nc, name
        self.stack = ExitStack()
        self.sems = []

    def __enter__(self):
        self.stack.__enter__()
        return self

    def sb(self, name, shape, dt=F32):
        return self.stack.enter_context(self.nc.sbuf_tensor(f"{self.name}_{name}", shape, dt))

    def ps(self, name, shape, dt=F32):
        return self.stack.enter_context(self.nc.psum_tensor(f"{self.name}_psum_{name}", shape, dt))

    def sem(self, name):
        s = self.nc.alloc_semaphore(f"{self.name}_{name}")
        self.sems.append(s)
        return s

    def __exit__(self, *a):
        if a[0] is None:
            self.nc.clear_and_free_semaphores(self.sems)
            self.nc.all_engine_barrier()
        return self.stack.__exit__(*a)


class Chain:

    def __init__(self, eng, sem):
        self.eng, self.sem, self.n = eng, sem, 0

    def mark(self, ins):
        self.n += 1
        ins.then_inc(self.sem, 1)

    def wait(self):
        if self.n:
            self.eng.wait_ge(self.sem, self.n)

    def link(self, ins):
        self.mark(ins)
        self.wait()


def rounded_alias(nc, t):
    return nc.alloc_sbuf_tensor_at(f"{t.name}_rounded", list(t.shape), F32R,
                                   offset=nc.sbuf_base - 4 * math.prod(t.shape[1:]))


class Ring:

    def __init__(self, nc):
        self.nc = nc
        self.buf = nc.alloc_sbuf_tensor("ring", [P, SLOTS, SLOT], F32)
        self.rounded = rounded_alias(nc, self.buf)
        self.loaded = [nc.alloc_semaphore(f"ring_loaded_{i}") for i in range(SLOTS)]
        self.gemm_done = nc.alloc_semaphore("gemm_done")
        self.plan, self.after = [], []
        self.issued = 0
        self.used = 0
        self.done = 0

    def add(self, src, units):
        self.plan.append(src)
        self.after.append((self.after[-1] if self.after else 0) + units)

    def view(self, i, rounded=False):
        a, b = self.plan[i].shape[1:]
        return (self.rounded if rounded else self.buf)[:, i % SLOTS, 0:a * b].rearrange("p (a b) -> p a b", a=a)

    def issue(self, sync, n):
        end = min(self.base_of_phase + n + SLOTS, len(self.plan))
        while self.issued < end:
            i = self.issued
            if i >= SLOTS:
                sync.wait_ge(self.gemm_done, self.after[i - SLOTS])
            sync.dma_start(self.view(i), self.plan[i]).then_inc(self.loaded[i % SLOTS], 16)
            self.issued += 1

    @property
    def base_of_phase(self):
        return self.used

    def take(self, pe):
        i = self.used
        pe.wait_ge(self.loaded[i % SLOTS], 16 * (i // SLOTS + 1))
        self.used += 1
        return self.view(i)

    def mark(self, ins):
        ins.then_inc(self.gemm_done, 1)
        self.done += 1


class G:
    pass


def blk(g, i):
    return g.const[:, i * P:(i + 1) * P]


def rep(ap, n, at=1):
    x = ap.unsqueeze(at)
    shape = list(x.shape)
    shape[at] = n
    return x.to_broadcast(shape)


class Split:

    def __init__(self, g, ph, depth, cut, free):
        self.g, self.depth, self.cut, self.free = g, depth, cut, free
        self.base = g.ring.used
        self.buf = ph.sb("w_high", [P, depth, SLOT // 4], F32R)
        self.s_high, self.s_low = ph.sem("w_high"), ph.sem("w_low")

    def views(self, k):
        ring = self.g.ring
        w, low = (self.cut(ring.view(self.base + k // 4, r), k) for r in (False, True))
        a, b = w.shape[1:]
        return w, low, self.buf[:, k % self.depth, 0:a * b].rearrange("p (a b) -> p a b", a=a)

    def high(self, act, k):
        ring, n = self.g.ring, self.base + k // 4
        act.wait_ge(ring.loaded[n % SLOTS], 16 * (n // SLOTS + 1))
        if k >= self.depth:
            act.wait_ge(ring.gemm_done, self.free(k))
        w, _, h = self.views(k)
        self.g.nc.scalar.copy(h, w).then_inc(self.s_high, 1)

    def low(self, dve, k):
        dve.wait_ge(self.s_high, k + 1)
        w, low, h = self.views(k)
        self.g.nc.vector.tensor_tensor(low, w, h.bitcast(F32), ALU.subtract).then_inc(self.s_low, 1)

    def parts(self, k):
        _, low, h = self.views(k)
        return h, low

    def take(self, pe, k):
        pe.wait_ge(self.s_low, k + 1)
        return self.parts(k)


class SplitActs:

    def __init__(self, g, ph, x, x_low, hi=None):
        self.g, self.x, self.x_low = g, x, x_low
        self.hi = ph.sb("x_high", list(x.shape), F32R) if hi is None else hi
        self.s_high, self.s_low = ph.sem("x_high"), ph.sem("x_low")

    def high(self, act, kt):
        self.g.nc.scalar.copy(self.hi[:, kt, :], self.x[:, kt, :]).then_inc(self.s_high, 1)

    def low(self, dve, kt):
        dve.wait_ge(self.s_high, kt + 1)
        x = self.x[:, kt, :]
        self.g.nc.vector.tensor_tensor(self.x_low[:, kt, :], x, self.hi[:, kt, :].bitcast(F32), ALU.subtract)\
            .then_inc(self.s_low, 1)

    def get(self, kt, sl):
        return self.hi[:, kt, sl], self.x_low[:, kt, sl]


def gemm_tok(g, name, chunks, acts, tiles, out, depth=8):
    nc, ring = g.nc, g.ring
    NT = len(tiles)
    QUARTERS = 4
    parts = QUARTERS * len(chunks)
    with Phase(g, name) as ph:
        banks = ph.ps("bank", [P, 8, 512])
        evac = ph.sem("evacuated")
        own = ph.sem("vector_chain")
        done0 = ring.done
        weights = Split(g, ph, depth, lambda v, k: v[:, 2 * (k % 4):2 * (k % 4) + 2, :],
                        lambda k: done0 + NT * ((k - depth) // QUARTERS + 1))
        xs = SplitActs(g, ph, *acts)
        with nc.Block() as block:
            @block.sync
            def _(sync):
                ring.issue(sync, len(chunks))

            @block.scalar
            def _(act):
                for kt in range(KT):
                    xs.high(act, kt)
                for k in range(parts):
                    weights.high(act, k)

            @block.tensor
            def _(pe):
                n = 0
                for c, w in enumerate(chunks):
                    ring.take(pe)
                    for i in range(NT):
                        tok = slice(i * P, (i + 1) * P)
                        if n >= 8:
                            pe.wait_ge(evac, n - 7)
                        for kt in range(KT):
                            k = QUARTERS * c + kt // 2
                            wh, wl = weights.take(pe, k) if i == 0 else weights.parts(k)
                            if c == 0 and i == 0:
                                pe.wait_ge(xs.s_low, kt + 1)
                            xh, xl = xs.get(kt, tok)
                            for k, (a, b) in enumerate(((xh, wh), (xh, wl), (xl, wh))):
                                mm = nc.tensor.matmul(banks[:, n % 8, 0:w], a, b[:, kt % 2, :],
                                                      start=(kt + k == 0), stop=(kt == KT - 1 and k == 2))
                        ring.mark(mm)
                        n += 1

            @block.vector
            def _(dve):
                ch = Chain(dve, own)
                for kt in range(KT):
                    xs.low(dve, kt)
                n, c0 = 0, 0
                ahead = min(depth, parts)
                for k in range(ahead):
                    weights.low(dve, k)
                for c, w in enumerate(chunks):
                    for i, t in enumerate(tiles):
                        dve.wait_ge(ring.gemm_done, done0 + n + 1)
                        out(ch, t, c0, w, banks[:, n % 8, 0:w]).then_inc(evac, 1)
                        n += 1
                    for k in range(ahead, min(parts, QUARTERS * (c + 1) + depth)):
                        weights.low(dve, k)
                    ahead = max(ahead, min(parts, QUARTERS * (c + 1) + depth))
                    c0 += w


def widths(n):
    m, rest = divmod(n, 512)
    return [512] * m if rest == 0 else [512] * (m - 1) + [(512 + rest) // 2] * 2


def plan_cols(ring, w, n_cols, units):
    wv = w.rearrange("(a p) n -> p a n", p=P)
    c = 0
    for wd in widths(n_cols):
        ring.add(wv[:, :, c:c + wd], units)
        c += wd


def plan_rows(ring, w, units):
    wv = w.rearrange("(a p) n -> p a n", p=P)
    for a in range(0, wv.shape[1], 4):
        ring.add(wv[:, a:a + 4, :], units)


def adaln(g, name, cond, bias, mod):
    nc, ring = g.nc, g.ring
    with Phase(g, name) as ph:
        c = ph.sb("cond", [P, KT, 2])
        sc = ph.sb("silu", [P, KT, 2])
        b = ph.sb("bias", [P, 48])
        row = ph.sb("row", [2, 12, 512])
        ps = ph.ps("mod", [P, 48, 2])
        pr = ph.ps("row", [2, 4, 512])
        s_in, s_silu, own = ph.sem("loaded"), ph.sem("silu"), ph.sem("chain")
        s_row, s_mod = ph.sem("row"), ph.sem("mod")
        with nc.Block() as block:
            done0 = ring.done

            @block.sync
            def _(sync):
                sync.dma_start(c[:, :, :], cond).then_inc(s_in, 16)
                sync.dma_start(b[:, :], bias).then_inc(s_in, 16)
                ring.issue(sync, 12)

            @block.scalar
            def _(act):
                act.wait_ge(s_in, 32)
                nc.scalar.activation(sc[:, :, :], c[:, :, :], ACT.Sigmoid).then_inc(own, 1)
                for n in range(12):
                    act.wait_ge(ring.gemm_done, done0 + n + 1)
                    nc.scalar.copy(row[:, n, :], pr[:, n % 4, :]).then_inc(s_row, 1)

            @block.vector
            def _(dve):
                dve.wait_ge(own, 1)
                dve.wait_ge(s_in, 32)
                nc.vector.tensor_tensor(sc[:, :, :], sc[:, :, :], c[:, :, :], ALU.mult).then_inc(s_silu, 1)
                dve.wait_ge(s_mod, 12)
                nc.vector.tensor_tensor(mod[:, :, :], ps[:, :, :], rep(b[:, :], 2, 2), ALU.add).then_inc(own, 1)
                dve.wait_ge(own, 2)

            @block.tensor
            def _(pe):
                def turn_row(n):
                    pe.wait_ge(s_row, n + 1)
                    for f in range(4):
                        mm = nc.tensor.transpose(ps[:, 4 * n + f, :], row[:, n, f * P:(f + 1) * P],
                                                 blk(g, C_ID)[0:2, 0:2])
                    mm.then_inc(s_mod, 1)

                pe.wait_ge(s_silu, 1)
                for n in range(12):
                    wv = ring.take(pe)
                    if n >= 4:
                        pe.wait_ge(s_row, n - 3)
                    for kt in range(KT):
                        mm = nc.tensor.matmul(pr[:, n % 4, :], sc[:, kt, :], wv[:, kt, :],
                                              start=(kt == 0), stop=(kt == KT - 1))
                    ring.mark(mm)
                    if n:
                        turn_row(n - 1)
                turn_row(11)


def gate_rows(g, name, cols, rows):
    nc = g.nc
    n_vec = len(cols)
    with Phase(g, name) as ph:
        wide = ph.sb("wide", [P, n_vec, KT, P])
        ps = ph.ps("rows", [P, 2 * n_vec, 512])
        s_w, s_mm, own = ph.sem("wide"), ph.sem("row"), ph.sem("chain")
        with nc.Block() as block:
            @block.vector
            def _(dve):
                for i in range(n_vec):
                    for kt in range(KT):
                        nc.vector.tensor_scalar(wide[:, i, kt, :], blk(g, C_ONE), cols[i](kt), None,
                                                ALU.mult).then_inc(s_w, 1)
                for i in range(2 * n_vec):
                    dve.wait_ge(s_mm, i + 1)
                    nc.vector.tensor_copy(rows[:, i // 2, (i % 2) * 512:(i % 2) * 512 + 512],
                                          ps[:, i, :]).then_inc(own, 1)
                dve.wait_ge(own, 2 * n_vec)

            @block.tensor
            def _(pe):
                for i in range(2 * n_vec):
                    for j in range(4):
                        kt = (i % 2) * 4 + j
                        pe.wait_ge(s_w, (i // 2) * KT + kt + 1)
                        mm = nc.tensor.matmul(ps[:, i, j * P:(j + 1) * P], wide[:, i // 2, kt, :], blk(g, C_ID),
                                              start=True, stop=True)
                    mm.then_inc(s_mm, 1)


def norm_T(g, name, tiles, dst, scale, shift, gain=None, off=0):
    nc = g.nc
    with Phase(g, name) as ph:
        sq = ph.sb("square", [P, D])
        xn = ph.sb("normed", [P, 2, D])
        ss = ph.sb("sums", [P, 4, TT])
        sp = ph.sb("scale1", [P, TT, KT])
        ps = ph.ps("turned", [P, 4, 512])
        s_ss, s_rt, s_ms = ph.sem("sum"), ph.sem("root"), ph.sem("mean")
        s_xn, s_tr, s_ev, own = ph.sem("normed"), ph.sem("turned"), ph.sem("evacuated"), ph.sem("chain")
        s_sc = ph.sem("act_chain")
        with nc.Block() as block:
            def drain(dve, i):
                t = tiles[i]
                for kt in range(KT):
                    dve.wait_ge(s_tr, 2 * i + kt // 4 + 1)
                    nc.vector.tensor_scalar(dst[:, kt, (t - off) * P:(t - off + 1) * P],
                                            ps[:, (2 * i + kt // 4) % 4, (kt % 4) * P:(kt % 4 + 1) * P],
                                            sp[:, i, kt:kt + 1], shift(t)[:, kt:kt + 1], ALU.mult, ALU.add)\
                        .then_inc(s_ev, 1)

            @block.scalar
            def _(act):
                for i, t in enumerate(tiles):
                    nc.scalar.activation(sq[:, :], g.x[:, t, :], ACT.Square, accum_out=ss[:, 0, i:i + 1])\
                        .then_inc(s_ss, 1)
                    act.wait_ge(s_ss, i + 1)
                act.wait_ge(s_ms, 1)
                nc.scalar.activation(ss[:, 2, 0:len(tiles)], ss[:, 1, 0:len(tiles)], ACT.Sqrt).then_inc(s_rt, 1)

            @block.vector
            def _(dve):
                ch = Chain(dve, own)
                n = len(tiles)
                for i, t in enumerate(tiles):
                    ch.link(nc.vector.tensor_scalar(sp[:, i, :], scale(t), 1.0, None, ALU.add))
                    if gain is not None:
                        ch.link(nc.vector.tensor_tensor(sp[:, i, :], sp[:, i, :], gain, ALU.mult))
                dve.wait_ge(s_ss, n)
                nc.vector.tensor_scalar(ss[:, 1, 0:n], ss[:, 0, 0:n], 1.0 / D, EPS, ALU.mult, ALU.add)\
                    .then_inc(s_ms, 1)
                dve.wait_ge(s_rt, 1)
                ch.link(nc.vector.reciprocal(ss[:, 3, 0:n], ss[:, 2, 0:n]))
                for i, t in enumerate(tiles):
                    if i >= 2:
                        dve.wait_ge(s_tr, 2 * (i - 1))
                    nc.vector.tensor_scalar(xn[:, i % 2, :], g.x[:, t, :], ss[:, 3, i:i + 1], None, ALU.mult)\
                        .then_inc(s_xn, 1)
                    if i >= 1:
                        drain(dve, i - 1)
                drain(dve, n - 1)
                dve.wait_ge(s_ev, KT * n)

            @block.tensor
            def _(pe):
                for i, t in enumerate(tiles):
                    pe.wait_ge(s_xn, i + 1)
                    if i >= 2:
                        pe.wait_ge(s_ev, KT * (i - 1))
                    for kt in range(KT):
                        mm = nc.tensor.transpose(ps[:, (2 * i + kt // 4) % 4, (kt % 4) * P:(kt % 4 + 1) * P],
                                                 xn[:, i % 2, kt * P:(kt + 1) * P], blk(g, C_ID))
                        if kt % 4 == 3:
                            mm.then_inc(s_tr, 1)


def turn(g, name, jobs, after=None):
    nc = g.nc
    with Phase(g, name) as ph:
        ps = ph.ps("turned", [P, 8, 512])
        s_tr, s_ev, s_ev2 = ph.sem("turned"), ph.sem("vector_evac"), ph.sem("scalar_evac")
        groups = [jobs[i:i + 4] for i in range(0, len(jobs), 4)]
        with nc.Block() as block:
            @block.tensor
            def _(pe):
                for n, grp in enumerate(groups):
                    if n >= 8:
                        pe.wait_ge((s_ev, s_ev2)[n % 2], sum(len(groups[m]) for m in range(n % 2, n - 7, 2)))
                    for j, (src, dst) in enumerate(grp):
                        mm = nc.tensor.transpose(ps[0:src.shape[1], n % 8, j * P:j * P + P], src, blk(g, C_ID))
                    mm.then_inc(s_tr, 1)

            def evacuate(eng, copy, s, parity):
                k = 0
                for n in range(parity, len(groups), 2):
                    eng.wait_ge(s_tr, n + 1)
                    for j, (src, dst) in enumerate(groups[n]):
                        copy(dst, ps[0:src.shape[1], n % 8, j * P:j * P + P]).then_inc(s, 1)
                        k += 1
                if k:
                    eng.wait_ge(s, k)

            @block.vector
            def _(dve):
                evacuate(dve, nc.vector.tensor_copy, s_ev, 0)

            @block.scalar
            def _(act):
                evacuate(act, nc.scalar.copy, s_ev2, 1)


def residual(g, rows, i):
    nc = g.nc

    def out(ch, t, c0, w, ps):
        k = ch.n % 2
        tmp = g.tmp[:, k * 512:k * 512 + w]
        ch.link(nc.vector.tensor_tensor(tmp, ps, rows(t)[:, c0:c0 + w], ALU.mult))
        return nc.vector.tensor_tensor(g.x[:, t, c0:c0 + w], g.x[:, t, c0:c0 + w], tmp, ALU.add)
    return out


def mlp(g, name, tiles, rows):
    nc, ring = g.nc, g.ring
    n_tok = len(tiles) * P
    t0 = tiles[0] * P
    FT = D_FF // P
    DEPTH = 2 if n_tok > 256 else 4
    with Phase(g, name) as ph:
        hid = ph.sb("hidden", [P, FT, n_tok])
        hid_low = rounded_alias(nc, hid)
        hid_high = ph.sb("hidden_high", [P, DEPTH, n_tok], F32R)
        relu = ph.sb("relu", [P, 2, n_tok])
        banks = ph.ps("bank", [P, 8, 512])
        s_relu, s_sq, own, s_own = ph.sem("relu"), ph.sem("squared"), ph.sem("chain"), ph.sem("evac")
        s_hh, s_hl = ph.sem("hidden_high"), ph.sem("hidden_low")
        n_out = 2 * len(tiles)
        done0 = ring.done
        weights = Split(g, ph, DEPTH, lambda v, k: v[:, :, (k % 4) * P:(k % 4 + 1) * P] if k < FT
                        else v[:, k % 4:k % 4 + 1, :], lambda k: done0 + k - DEPTH + 1)
        acts = SplitActs(g, ph, g.xT[:, :, t0:t0 + n_tok], g.xT_low[:, :, t0:t0 + n_tok])
        with nc.Block() as block:
            @block.sync
            def _(sync):
                ring.issue(sync, FT // 4 + FT // 4)

            @block.scalar
            def _(act):
                def hidden_high(f):
                    act.wait_ge(s_sq, f + 1)
                    if f >= DEPTH:
                        act.wait_ge(ring.gemm_done, done0 + FT + f - DEPTH + 1)
                    nc.scalar.copy(hid_high[:, f % DEPTH, :], hid[:, f, :]).then_inc(s_hh, 1)

                weights.high(act, 0)
                for kt in range(KT):
                    acts.high(act, kt)
                for k in range(1, DEPTH):
                    weights.high(act, k)
                for f in range(FT):
                    act.wait_ge(ring.gemm_done, done0 + f + 1)
                    if f >= 2:
                        act.wait_ge(s_sq, f - 1)
                    nc.scalar.activation(relu[:, f % 2, :], banks[:, f % 8, 0:n_tok], ACT.Relu).then_inc(s_relu, 1)
                    weights.high(act, f + DEPTH)
                    if FT - DEPTH <= f:
                        hidden_high(f - FT + DEPTH)
                for f in range(DEPTH, FT):
                    hidden_high(f)
                    weights.high(act, FT + f)

            @block.vector
            def _(dve):
                def hidden_low(f):
                    dve.wait_ge(s_hh, f + 1)
                    nc.vector.tensor_tensor(hid_low[:, f, :], hid[:, f, :], hid_high[:, f % DEPTH, :].bitcast(F32),
                                            ALU.subtract).then_inc(s_hl, 1)

                ch = Chain(dve, own)
                weights.low(dve, 0)
                for kt in range(KT):
                    acts.low(dve, kt)
                for k in range(1, DEPTH):
                    weights.low(dve, k)
                for f in range(FT):
                    dve.wait_ge(s_relu, f + 1)
                    nc.vector.tensor_tensor(hid[:, f, :], relu[:, f % 2, :], relu[:, f % 2, :], ALU.mult)\
                        .then_inc(s_sq, 1)
                    weights.low(dve, f + DEPTH)
                    if FT - DEPTH <= f:
                        hidden_low(f - FT + DEPTH)
                for f in range(DEPTH, FT):
                    hidden_low(f)
                    weights.low(dve, FT + f)
                dve.wait_ge(ring.gemm_done, done0 + 2 * FT)
                for i in range(n_out):
                    t, c0 = tiles[i // 2], (i % 2) * 512
                    residual(g, rows, 0)(ch, t, c0, 512, banks[:, i, :]).then_inc(s_own, 1)
                dve.wait_ge(s_own, n_out)

            @block.tensor
            def _(pe):
                for f in range(FT):
                    if f % 4 == 0:
                        ring.take(pe)
                    if f >= 8:
                        pe.wait_ge(s_relu, f - 7)
                    wh, wl = weights.take(pe, f)
                    for kt in range(KT):
                        if f == 0:
                            pe.wait_ge(acts.s_low, kt + 1)
                        xh, xl = acts.get(kt, slice(0, n_tok))
                        for k, (w, x) in enumerate(((wh, xh), (wh, xl), (wl, xh))):
                            mm = nc.tensor.matmul(banks[:, f % 8, 0:n_tok], w[:, kt, :], x,
                                                  start=(kt + k == 0), stop=(kt == KT - 1 and k == 2))
                    ring.mark(mm)
                pe.wait_ge(s_relu, FT)
                for f in range(FT):
                    if f % 4 == 0:
                        ring.take(pe)
                    wh, wl = weights.take(pe, FT + f)
                    pe.wait_ge(s_hl, f + 1)
                    for t in range(len(tiles)):
                        hh = hid_high[:, f % DEPTH, t * P:(t + 1) * P]
                        hl = hid_low[:, f, t * P:(t + 1) * P]
                        for k, (h, w) in enumerate(((hh, wh), (hh, wl), (hl, wh))):
                            for c in range(2):
                                mm = nc.tensor.matmul(banks[:, 2 * t + c, :], h, w[:, 0, c * 512:c * 512 + 512],
                                                      start=(f + k == 0), stop=(f == FT - 1 and k == 2))
                    ring.mark(mm)


def tok_bcast(g, name, loads):
    nc = g.nc
    with Phase(g, name) as ph:
        s = ph.sem("loaded")
        with nc.Block() as block:
            @block.sync
            def _(sync):
                for dst, src in loads:
                    sync.dma_start(dst, src.partition_broadcast(P) if len(src.shape) == 1 else src).then_inc(s, 16)
                sync.wait_ge(s, 16 * len(loads))


def ab_prepare(g, pa, pb, rows, rope, gates):
    nc = g.nc
    with Phase(g, "abprep") as ph:
        sq = ph.sb("square", [P, 2, 512])
        ss = ph.sb("sums", [P, 3, TT * 16])
        t1 = ph.sb("rope1", [P, 512])
        t2 = ph.sb("rope2", [P, 512])
        own = ph.sem("chain")
        s_ms, s_rt, s_g, s_t = ph.sem("mean"), ph.sem("root"), ph.sem("gates"), ph.sem("tanh")
        s_f, s_a = ph.sem("capped"), ph.sem("act_chain")
        with nc.Block() as block:
            @block.vector
            def _(dve):
                ch = Chain(dve, own)
                gate_bias = rows[:, 0:16]
                nc.vector.tensor_tensor(gates[:, :, :], pb[:, :, 2048:2064], rep(gate_bias, TT), ALU.add)\
                    .then_inc(s_g, 1)
                for t in range(TT):
                    for j in range(2):
                        x = pa[:, t, 512 * j:512 * j + 512]
                        ch.link(nc.vector.tensor_tensor(sq[:, j, :], x, x, ALU.mult))
                        o = (2 * t + j) * 8
                        ch.link(nc.vector.tensor_reduce(ss[:, 0, o:o + 8],
                                                        sq[:, j, :].rearrange("p (h d) -> p h d", h=8),
                                                        AX.X, ALU.add))
                nc.vector.tensor_scalar(ss[:, 1, :], ss[:, 0, :], 1.0 / NA_D, EPS, ALU.mult, ALU.add)\
                    .then_inc(s_ms, 1)
                dve.wait_ge(s_t, 1)
                nc.vector.tensor_scalar(gates[:, :, :], gates[:, :, :], GATE_CAP, None, ALU.mult).then_inc(s_f, 1)
                dve.wait_ge(s_rt, 1)
                ch.link(nc.vector.reciprocal(ss[:, 0, :], ss[:, 2, :]))
                for t in range(TT):
                    for j in range(2):
                        x = pa[:, t, 512 * j:512 * j + 512].rearrange("p (h d) -> p h d", h=8)
                        o = (2 * t + j) * 8
                        ch.link(nc.vector.tensor_tensor(x, x, rep(ss[:, 0, o:o + 8], NA_D, 2), ALU.mult))
                        ch.link(nc.vector.tensor_tensor(x, x, rep(rows[:, 16 + 64 * j:80 + 64 * j], 8), ALU.mult))
                    kb = pb[:, t, 512:1024]
                    ch.link(nc.vector.tensor_scalar(kb, kb, ML_D ** -0.5, None, ALU.mult))
                for t in LAT_TILES:
                    for o in (0, 512):
                        x = pb[:, t, o:o + 512]
                        x5 = x.rearrange("p (h a b c) -> p h a b c", h=4, a=2, b=2)
                        y5 = t2[:, :].rearrange("p (h a b c) -> p h a b c", h=4, a=2, b=2)
                        sn = rope[:, t - 2, 1, :].rearrange("p (a b c) -> p a b c", a=2, b=2)
                        ch.mark(nc.vector.tensor_tensor(t1[:, :].rearrange("p (h d) -> p h d", h=4),
                                                        x.rearrange("p (h d) -> p h d", h=4),
                                                        rep(rope[:, t - 2, 0, :], 4), ALU.mult))
                        for a in range(2):
                            for b in range(2):
                                ch.mark(nc.vector.tensor_tensor(y5[:, :, a, b, :], x5[:, :, a, 1 - b, :],
                                                                rep(sn[:, a, b, :], 4), ALU.mult))
                        ch.wait()
                        ch.link(nc.vector.tensor_tensor(x, t1[:, :], t2[:, :], ALU.add))

            @block.scalar
            def _(act):
                act.wait_ge(s_g, 1)
                nc.scalar.activation(gates[:, :, :], gates[:, :, :], ACT.Tanh, scale=1.0 / GATE_CAP).then_inc(s_t, 1)
                act.wait_ge(s_ms, 1)
                nc.scalar.activation(ss[:, 2, :], ss[:, 1, :], ACT.Sqrt).then_inc(s_rt, 1)
                act.wait_ge(s_f, 1)
                for o in (4, 12):
                    nc.scalar.activation(gates[:, :, o:o + 4], gates[:, :, o:o + 4], ACT.Sigmoid).then_inc(s_a, 1)
                act.wait_ge(s_a, 2)
                for o in (4, 12):
                    nc.scalar.activation(gates[:, :, o:o + 4], gates[:, :, o:o + 4], ACT.Ln).then_inc(s_a, 1)
                act.wait_ge(s_a, 4)


def attention(g, proj, qT, kT, cat, rpb_cols, window):
    nc = g.nc
    units = [(h, t) for h in range(NA_H) for t in ALL_TILES]
    scale = NA_D ** -0.5
    with Phase(g, "attn") as ph:
        bm = ph.sb("bias", [P, NA_H, 2, 256])
        win = ph.sb("window", [P, GRID_W])
        pr = ph.sb("probs", [P, 2, 512])
        pT = ph.sb("probsT", [P, 2, 512])
        st = ph.sb("stats", [P, 4, 2])
        S = ph.ps("scores", [P, 2, 512])
        T = ph.ps("turned", [P, 2, 512])
        O = ph.ps("out", [P, 2, 512])
        s_ld, s_bm, s_s, s_mx = ph.sem("loaded"), ph.sem("bias"), ph.sem("scores"), ph.sem("max")
        s_e, s_t, s_tc, s_o, s_ev, own = (ph.sem("exp"), ph.sem("turned"), ph.sem("copied"), ph.sem("out"),
                                          ph.sem("evacuated"), ph.sem("chain"))
        s_head = [ph.sem(f"loaded_head{h}") for h in range(NA_H)]
        keys = lambda t: 2 if t < 2 else 4
        with nc.Block() as block:
            @block.sync
            def _(sync):
                for half in range(2):
                    sync.dma_start(win[64 * half:64 * half + 64, :], window).then_inc(s_ld, 16)
                for h in range(NA_H):
                    for r in range(4):
                        src = rpb_cols[h, 3 - r:7 - r].rearrange("i c k -> c i k")
                        dst = bm[64 * (r % 2):64 * (r % 2) + 64, h, r // 2, :].rearrange("p (i c) -> p i c", i=4)
                        sync.dma_start(dst, src).then_inc(s_head[h], 16)

            @block.vector
            def _(dve):
                ch = Chain(dve, own)
                dve.wait_ge(s_ld, 16 * 2)

                def bias(h):
                    dve.wait_ge(s_head[h], 16 * 4)
                    v = bm[:, h, :, :].rearrange("p a (i c) -> p (a i) c", i=4)
                    nc.vector.scalar_tensor_tensor(out=v, in0=v, scalar=1.0 / scale, in1=rep(win[:, :], 8),
                                                   op0=ALU.mult, op1=ALU.add).then_inc(s_bm, 1)
                    dve.wait_ge(s_bm, h + 1)

                def top(u):
                    h, t = units[u]
                    b, n = u % 2, 128 * keys(t)
                    if t == 2:
                        bias(h)
                    dve.wait_ge(s_s, u + 1)
                    if t >= 2:
                        lat = S[:, b, 256:512]
                        ch.link(nc.vector.tensor_tensor(lat, lat, bm[:, h, t - 2, :], ALU.add))
                    ch.link(nc.vector.tensor_reduce(st[:, 0, b:b + 1], S[:, b, 0:n], AX.X, ALU.max))
                    nc.vector.tensor_scalar(st[:, 1, b:b + 1], st[:, 0, b:b + 1], -scale, None, ALU.mult)\
                        .then_inc(s_mx, 1)

                def turn_copy(u):
                    h, t = units[u]
                    b, n = u % 2, 128 * keys(t)
                    dve.wait_ge(s_t, u + 1)
                    nc.vector.tensor_copy(pT[:, b, 0:n], T[:, b, 0:n]).then_inc(s_tc, 1)

                def store(u):
                    h, t = units[u]
                    b = u % 2
                    dve.wait_ge(s_o, u + 1)
                    ch.link(nc.vector.reciprocal(st[:, 3, b:b + 1], st[:, 2, b:b + 1]))
                    nc.vector.tensor_scalar(cat[:, t, h * 64:h * 64 + 64], O[:, b, 0:64], st[:, 3, b:b + 1], None,
                                            ALU.mult).then_inc(s_ev, 1)

                for u in range(len(units) + 1):
                    if u < len(units):
                        top(u)
                    if u >= 1:
                        turn_copy(u - 1)
                        store(u - 1)
                dve.wait_ge(s_ev, len(units))

            @block.scalar
            def _(act):
                for u, (h, t) in enumerate(units):
                    b, n = u % 2, 128 * keys(t)
                    act.wait_ge(s_mx, u + 1)
                    if u >= 2:
                        act.wait_ge(s_t, u - 1)
                        act.wait_ge(s_ev, u - 1)
                    nc.scalar.activation(pr[:, b, 0:n], S[:, b, 0:n], ACT.Exp, bias=st[:, 1, b:b + 1], scale=scale,
                                         accum_out=st[:, 2, b:b + 1]).then_inc(s_e, 1)

            @block.tensor
            def _(pe):
                def scores(u):
                    h, t = units[u]
                    b, n, o = u % 2, 128 * keys(t), 64 * (h % 2)
                    if u >= 2:
                        pe.wait_ge(s_e, u - 1)
                    nc.tensor.matmul(S[:, b, 0:n], qT[o:o + 64, h // 2, t * P:(t + 1) * P],
                                     kT[o:o + 64, h // 2, 0:n], start=True, stop=True).then_inc(s_s, 1)

                scores(0)
                for u, (h, t) in enumerate(units):
                    b = u % 2
                    if u + 1 < len(units):
                        scores(u + 1)
                    pe.wait_ge(s_e, u + 1)
                    if u >= 2:
                        pe.wait_ge(s_tc, u - 1)
                    for k in range(keys(t)):
                        mm = nc.tensor.transpose(T[:, b, k * P:(k + 1) * P], pr[:, b, k * P:(k + 1) * P],
                                                 blk(g, C_ID))
                    mm.then_inc(s_t, 1)
                    pe.wait_ge(s_tc, u + 1)
                    if u >= 2:
                        pe.wait_ge(s_ev, u - 1)
                    for k in range(keys(t)):
                        mm = nc.tensor.matmul(O[:, b, 0:64], pT[:, b, k * P:(k + 1) * P],
                                              proj[:, k, 1024 + h * 64:1088 + h * 64],
                                              start=(k == 0), stop=(k == keys(t) - 1))
                    mm.then_inc(s_o, 1)


def mlstm_rows(g, rowg, rowo, cols):
    nc = g.nc
    with Phase(g, "mlrows") as ph:
        F = ph.sb("F", [4, 2, 512])
        Gm = ph.sb("G", [4, 2, 512])
        one = ph.sb("one", [4, 512])
        own = ph.sem("chain")
        with nc.Block() as block:
            @block.vector
            def _(dve):
                ch = Chain(dve, own)
                ch.link(nc.vector.memset(one[:, :], 1.0))

                def scan(dst, src, d, op):
                    if d == 0:
                        ch.link(nc.vector.tensor_tensor_scan(dst[:, 0, :], one[:, :], src, 0.0, ALU.mult, op))
                    else:
                        ch.link(nc.vector.tensor_tensor_scan(dst[:, 1, 0:256][:, ::-1], one[:, 0:256],
                                                             src[:, 0:256][:, ::-1], 0.0, ALU.mult, op))
                        ch.link(nc.vector.tensor_tensor_scan(dst[:, 1, 256:512][:, ::-1], one[:, 0:256],
                                                             src[:, 256:512][:, ::-1], dst[:, 1, 0:1],
                                                             ALU.mult, op))
                for d in range(2):
                    scan(F, rowg[:, 2 * d + 1, :], d, ALU.add)
                    ch.link(nc.vector.tensor_tensor(rowo[:, 2 * d, :], rowg[:, 2 * d, :], F[:, d, :], ALU.subtract))
                    scan(Gm, rowo[:, 2 * d, :], d, ALU.max)
                    ch.link(nc.vector.tensor_tensor(rowo[:, 2 * d + 1, :], F[:, d, :], Gm[:, d, :], ALU.add))
                    ch.link(nc.vector.tensor_scalar(rowo[:, 4 + d, :], Gm[:, d, :], -1.0, None, ALU.mult))


def mlstm(g, proj, qT, kT, rowo, colg, sel, hs):
    nc = g.nc
    blocks = {0: {t: [s for s in range(TT) if s <= t] for t in range(TT)},
              1: {0: [0, 1], 1: [1], 2: [0, 1, 2, 3], 3: [0, 1, 3]}}
    units = [(h, d) for h in range(ML_H) for d in range(2)]
    with Phase(g, "mlstm") as ph:
        v1 = ph.sb("v1", [P, TT, ML_H, 129])
        dec = ph.sb("decay", [P, 2, 512])
        wt = ph.sb("weights", [P, 2, TT, 512])
        em = ph.sb("expm", [P, TT, 2, ML_H])
        den = ph.sb("den", [P, 3, 2, 2])
        raw = ph.ps("raw", [P, 2, 512])
        gb = ph.ps("G", [P, 2, 512])
        out = ph.ps("out", [P, 4, 512])
        s_v, s_em, s_gb, s_raw, s_d, s_x = (ph.sem("v"), ph.sem("em"), ph.sem("Gb"), ph.sem("raw"),
                                            ph.sem("diff"), ph.sem("exp"))
        own_act = ph.sem("act_chain")
        s_m, s_w, s_o, s_ev, own = ph.sem("masked"), ph.sem("weights"), ph.sem("out"), ph.sem("evac"), ph.sem("chain")
        with nc.Block() as block:
            @block.vector
            def _(dve):
                ch = Chain(dve, own)
                for t in range(TT):
                    ch.mark(nc.vector.tensor_copy(v1[:, t, :, 0:128],
                                                  proj[:, t, 1024:1536].rearrange("p (h d) -> p h d", h=4)))
                ch.link(nc.vector.memset(v1[:, :, :, 128:129], 1.0))
                nc.vector.sem_inc(s_v, 1)

                def weights(u):
                    h, d = units[u]
                    for s in range(TT):
                        n = 4 * u + s
                        if s == 0:
                            dve.wait_ge(s_gb, u + 1)
                        if n >= 2:
                            dve.wait_ge(s_m, n - 1)
                        if n >= 2:
                            dve.wait_ge(s_w, n - 1)
                        nc.vector.tensor_scalar(dec[:, n % 2, :], gb[:, u % 2, :], colg[:, s, 2 * d, h:h + 1], 0.0,
                                                ALU.add, ALU.min).then_inc(s_d, 1)
                        if n >= 1:
                            product(n - 1)
                    product(4 * u + 3)

                done = set()

                def product(n):
                    if n in done:
                        return
                    done.add(n)
                    u, s = n // 4, n % 4
                    dve.wait_ge(s_m, n + 1)
                    dve.wait_ge(s_raw, n + 1)
                    if u >= 2:
                        dve.wait_ge(s_o, u - 1)
                    nc.vector.tensor_tensor(wt[:, u % 2, s, :], raw[:, n % 2, :], dec[:, n % 2, :], ALU.mult)\
                        .then_inc(s_w, 1)

                def finish(u):
                    h, d = units[u]
                    dve.wait_ge(s_o, u + 1)
                    if u == 0:
                        dve.wait_ge(s_em, 1)
                    b = 2 * (u % 2)
                    dn = out[:, b:b + 2, 0:258].rearrange("p b (t e) -> p b t e", e=129)[:, :, :, 128]
                    ch.link(nc.vector.tensor_copy(den[:, 0, :, :], dn))
                    ch.link(nc.vector.scalar_tensor_tensor(out=den[:, 1, :, :], in0=den[:, 0, :, :], scalar=-1.0,
                                                           in1=den[:, 0, :, :], op0=ALU.mult, op1=ALU.max))
                    ch.link(nc.vector.tensor_tensor(den[:, 1, :, :], den[:, 1, :, :],
                                                    em[:, :, d, h].rearrange("p (a b) -> p a b", a=2), ALU.max))
                    ch.link(nc.vector.reciprocal(den[:, 2, :, :], den[:, 1, :, :]))
                    for t in range(TT):
                        num = out[:, b + t // 2, (t % 2) * 129:(t % 2) * 129 + 128]
                        r = den[:, 2, t // 2, t % 2:t % 2 + 1]
                        dst = hs[:, t, h * 128:(h + 1) * 128]
                        if d == 0:
                            ch.mark(nc.vector.tensor_scalar(dst, num, r, None, ALU.mult))
                        else:
                            ch.mark(nc.vector.scalar_tensor_tensor(out=dst, in0=num, scalar=r, in1=dst,
                                                                   op0=ALU.mult, op1=ALU.add))
                    ch.wait()
                    nc.vector.sem_inc(s_ev, 1)

                for u in range(len(units)):
                    weights(u)
                    if u >= 1:
                        finish(u - 1)
                finish(len(units) - 1)

            @block.gpsimd
            def _(pool):
                for n in range(4 * len(units)):
                    u, s = n // 4, n % 4
                    h, d = units[u]
                    pool.wait_ge(s_x, n + 1)
                    diagonal = dec[:, n % 2, s * P:(s + 1) * P]
                    nc.gpsimd.tensor_tensor(diagonal, diagonal, blk(g, C_UP if d == 0 else C_LO), ALU.mult)\
                        .then_inc(s_m, 1)

            @block.scalar
            def _(act):
                for d in range(2):
                    nc.scalar.activation(em[:, :, d, :], colg[:, :, 2 * d + 1, :], ACT.Exp, scale=-1.0)\
                        .then_inc(own_act, 1)
                act.wait_ge(own_act, 2)
                nc.scalar.sem_inc(s_em, 1)
                for n in range(4 * len(units)):
                    act.wait_ge(s_d, n + 1)
                    nc.scalar.activation(dec[:, n % 2, :], dec[:, n % 2, :], ACT.Exp).then_inc(s_x, 1)

            @block.tensor
            def _(pe):
                pe.wait_ge(s_v, 1)

                def scores(u):
                    h, d = units[u]
                    if u >= 2:
                        pe.wait_ge(s_d, 4 * (u - 1))
                    nc.tensor.matmul(gb[:, u % 2, :], sel[:, h, :], rowo[:, 4 + d, :], start=True, stop=True)\
                        .then_inc(s_gb, 1)
                    for s in range(TT):
                        n = 4 * u + s
                        if n >= 2:
                            pe.wait_ge(s_w, n - 1)
                        nc.tensor.matmul(raw[:, n % 2, :], kT[:, h, s * P:(s + 1) * P], qT[:, h, :],
                                         start=True, stop=True).then_inc(s_raw, 1)

                def values(u):
                    h, d = units[u]
                    pe.wait_ge(s_w, 4 * u + 4)
                    if u >= 2:
                        pe.wait_ge(s_ev, u - 1)
                    for t in range(TT):
                        ss = blocks[d][t]
                        for s in ss:
                            mm = nc.tensor.matmul(out[:, 2 * (u % 2) + t // 2, (t % 2) * 129:(t % 2) * 129 + 129],
                                                  wt[:, u % 2, s, t * P:(t + 1) * P], v1[:, s, h, :],
                                                  start=(s == ss[0]), stop=(s == ss[-1]))
                    mm.then_inc(s_o, 1)

                for u in range(len(units)):
                    scores(u)
                    values(u)


def ab_merge(g, proj, hs, head_row, cat):
    nc = g.nc
    with Phase(g, "abmerge") as ph:
        sq = ph.sb("square", [P, 512])
        sg = ph.sb("sigmoid", [P, TT, 512])
        ss = ph.sb("sums", [P, 3, TT * ML_H])
        own, s_ms, s_rt, s_sg = ph.sem("chain"), ph.sem("mean"), ph.sem("root"), ph.sem("sigmoid")
        with nc.Block() as block:
            @block.vector
            def _(dve):
                ch = Chain(dve, own)
                for t in range(TT):
                    x = hs[:, t, :]
                    ch.link(nc.vector.tensor_tensor(sq[:, :], x, x, ALU.mult))
                    ch.link(nc.vector.tensor_reduce(ss[:, 0, 4 * t:4 * t + 4],
                                                    sq[:, :].rearrange("p (h d) -> p h d", h=4), AX.X, ALU.add))
                nc.vector.tensor_scalar(ss[:, 1, :], ss[:, 0, :], 1.0 / ML_D, EPS, ALU.mult, ALU.add)\
                    .then_inc(s_ms, 1)
                dve.wait_ge(s_rt, 1)
                ch.link(nc.vector.reciprocal(ss[:, 0, :], ss[:, 2, :]))
                dve.wait_ge(s_sg, TT)
                for t in range(TT):
                    x = hs[:, t, :]
                    ch.link(nc.vector.tensor_tensor(x.rearrange("p (h d) -> p h d", h=4),
                                                    x.rearrange("p (h d) -> p h d", h=4),
                                                    rep(ss[:, 0, 4 * t:4 * t + 4], ML_D, 2), ALU.mult))
                    ch.link(nc.vector.tensor_tensor(x, x, head_row, ALU.mult))
                    ch.link(nc.vector.tensor_tensor(cat[:, t, 512:1024], x, sg[:, t, :], ALU.mult))

            @block.scalar
            def _(act):
                for t in range(TT):
                    nc.scalar.activation(sg[:, t, :], proj[:, t, 1536:2048], ACT.Sigmoid).then_inc(s_sg, 1)
                act.wait_ge(s_ms, 1)
                nc.scalar.activation(ss[:, 2, :], ss[:, 1, :], ACT.Sqrt).then_inc(s_rt, 1)


class Inverse:

    def __init__(self, g, ph):
        self.g, self.nc = g, g.nc
        self.L = [ph.sb(f"L{l}", [P, 4, P]) for l in range(2)]
        self.X = [ph.sb(f"X{l}", [P, 4, P]) for l in range(2)]
        self.Y = [ph.sb(f"Y{l}", [P, 4, P]) for l in range(2)]
        self.T = [ph.sb(f"T{l}", [P, 4, P]) for l in range(2)]
        self.Lo = [ph.sb(f"Lo{l}", [P, 4, P]) for l in range(2)]
        names = ("join", "t_ready", "t_copied", "y_ready", "x_ready", "y_new", "x_new")
        self.s = [{n: ph.sem(f"{n}{l}") for n in names} for l in range(2)]

    def pool(self, take, l_ready, d):
        nc, g = self.nc, self.g
        for k in range(LEVELS):
            mask = blk(g, C_LVL + LEVELS * d + k)
            for l in range(2):
                if k == 0:
                    take(l_ready[l])
                else:
                    take(self.s[l]["t_ready"])
                nc.gpsimd.tensor_tensor(self.Lo[l][:, :, :], self.L[l][:, :, :], rep(mask, 4), ALU.mult)\
                    .then_inc(self.s[l]["join"], 1)
                if k == 0:
                    take(self.s[l]["join"])
                    nc.gpsimd.tensor_tensor(self.X[l][:, :, :], self.Lo[l][:, :, :], rep(blk(g, C_ID), 4), ALU.add)\
                        .then_inc(self.s[l]["x_new"], 1)
                    take(self.s[l]["x_new"])
                    take.n[self.s[l]["join"].name] += LEVELS - 1
                    take.n[self.s[l]["x_new"].name] += LEVELS - 2
        for l in range(2):
            take(self.s[l]["t_ready"])

    def act(self, take, banks):
        for k in range(1, LEVELS):
            for l in range(2):
                take(self.s[l]["t_ready"], 2 if k == 1 else 1)
                self.nc.scalar.copy(self.T[l][:, :, :], banks[l][:, 0, :].rearrange("p (h c) -> p h c", h=4))\
                    .then_inc(self.s[l]["t_copied"], 1)

    def dve(self, take):
        nc, g = self.nc, self.g

        def add(l, k, dst, bank, ready, new):
            take(self.s[l][ready])
            old = rep(blk(g, C_ID), 4) if k == 0 else dst[:, :, :]
            nc.vector.tensor_tensor(dst[:, :, :], bank.rearrange("p (h c) -> p h c", h=4), old, ALU.add)\
                .then_inc(self.s[l][new], 1)

        def level(k, banks):
            for l in range(2):
                if k == 0:
                    add(l, k, self.Y[l], banks[l][:, 0, :], "t_ready", "y_new")
                    take.n[self.s[l]["t_ready"].name] += LEVELS - 1
                    continue
                add(l, k, self.Y[l], banks[l][:, 1, :], "y_ready", "y_new")
                if k < LEVELS - 1:
                    add(l, k, self.X[l], banks[l][:, 2, :], "x_ready", "x_new")
        return level

    def pe(self, take, banks):
        nc, g = self.nc, self.g
        for k in range(LEVELS):
            for l in range(2):
                s = self.s[l]
                take(s["join"])
                if k:
                    take(s["y_new"])
                for h in range(4):
                    y = self.Y[l][:, h, :] if k else blk(g, C_ID)
                    mm = nc.tensor.matmul(banks[l][:, 0, h * P:(h + 1) * P], self.Lo[l][:, h, :], y,
                                          start=True, stop=True)
                mm.then_inc(s["t_ready"], 1)
            for l in range(2):
                s = self.s[l]
                if k == 0:
                    continue
                take(s["t_copied"])
                take(s["x_new"])
                for h in range(4):
                    x = self.X[l][:, h, :]
                    mm = nc.tensor.matmul(banks[l][:, 1, h * P:(h + 1) * P], x, self.T[l][:, h, :],
                                          start=True, stop=True)
                mm.then_inc(s["y_ready"], 1)
                if k < LEVELS - 1:
                    for h in range(4):
                        x = self.X[l][:, h, :]
                        mm = nc.tensor.matmul(banks[l][:, 2, h * P:(h + 1) * P], self.T[l][:, h, :], x,
                                              start=True, stop=True)
                    mm.then_inc(s["x_ready"], 1)
        for l in range(2):
            take(self.s[l]["y_new"])


def rw_shift(g, xx):
    nc = g.nc
    with Phase(g, "rwshift") as ph:
        own = ph.sem("chain")
        with nc.Block() as block:
            @block.vector
            def _(dve):
                ch = Chain(dve, own)
                for kt in range(KT):
                    for s in range(2):
                        h = g.xT[:, kt, 256 * s:256 * s + 256]
                        x = xx[:, kt, 256 * s:256 * s + 256]
                        ch.mark(nc.vector.tensor_tensor(x[:, 1:255], h[:, 0:254], h[:, 2:256], ALU.add))
                        ch.mark(nc.vector.tensor_copy(x[:, 0:1], h[:, 1:2]))
                        ch.mark(nc.vector.tensor_copy(x[:, 255:256], h[:, 254:255]))
                ch.wait()
                for kt in range(KT):
                    ch.mark(nc.vector.scalar_tensor_tensor(out=xx[:, kt, :], in0=xx[:, kt, :], scalar=0.5,
                                                           in1=g.xT[:, kt, :], op0=ALU.mult, op1=ALU.subtract))
                ch.wait()


def rw_mix(g, name, xx, xs, mu):
    nc = g.nc
    with Phase(g, name) as ph:
        own = ph.sem("chain")
        with nc.Block() as block:
            @block.vector
            def _(dve):
                ch = Chain(dve, own)
                for kt in range(KT):
                    ch.mark(nc.vector.scalar_tensor_tensor(out=xs[:, kt, :], in0=xx[:, kt, :],
                                                           scalar=mu[:, kt:kt + 1], in1=g.xT[:, kt, :],
                                                           op0=ALU.mult, op1=ALU.add))
                ch.wait()


def rw_lora(g, name, w, xs, t0, outs, func):
    nc = g.nc
    n_tok = 512 - t0
    width = w.shape[2]
    with Phase(g, name) as ph:
        ws = ph.sb("w", [P, KT, width])
        ps = ph.ps("low", [P, 2, 512])
        s_ld, s_mm, own = ph.sem("loaded"), ph.sem("product"), ph.sem("chain")
        with nc.Block() as block:
            @block.sync
            def _(sync):
                sync.dma_start(ws[:, :, :], w).then_inc(s_ld, 16)

            @block.tensor
            def _(pe):
                pe.wait_ge(s_ld, 16)
                for i, (a, b, dst) in enumerate(outs):
                    for kt in range(KT):
                        mm = nc.tensor.matmul(ps[0:b - a, i, 0:n_tok], ws[:, kt, a:b], xs[:, kt, t0:512],
                                              start=(kt == 0), stop=(kt == KT - 1))
                    mm.then_inc(s_mm, 1)

            @block.scalar
            def _(act):
                for i, (a, b, dst) in enumerate(outs):
                    act.wait_ge(s_mm, i + 1)
                    nc.scalar.activation(dst, ps[0:b - a, i, 0:n_tok], func).then_inc(own, 1)
                act.wait_ge(own, len(outs))


def rw_kk(g, stage, kk, row):
    nc = g.nc
    with Phase(g, "rwkk") as ph:
        sq = ph.sb("square", [P, D])
        ss = ph.sb("sums", [P, 2, TT * RW_H])
        own, s_ss, s_rt = ph.sem("chain"), ph.sem("sum"), ph.sem("root")
        with nc.Block() as block:
            @block.vector
            def _(dve):
                ch = Chain(dve, own)
                for t in range(TT):
                    ch.link(nc.vector.tensor_tensor(kk[:, t, :], stage[:, t, :], row, ALU.mult))
                    ch.link(nc.vector.tensor_tensor(sq[:, :], kk[:, t, :], kk[:, t, :], ALU.mult))
                    ch.link(nc.vector.tensor_reduce(ss[:, 0, RW_H * t:RW_H * (t + 1)],
                                                    sq[:, :].rearrange("p (h d) -> p h d", h=RW_H), AX.X, ALU.add))
                nc.vector.sem_inc(s_ss, 1)
                dve.wait_ge(s_rt, 1)
                ch.link(nc.vector.tensor_scalar(ss[:, 1, :], ss[:, 1, :], 1e-12, None, ALU.max))
                ch.link(nc.vector.reciprocal(ss[:, 0, :], ss[:, 1, :]))
                for t in range(TT):
                    v = kk[:, t, :].rearrange("p (h d) -> p h d", h=RW_H)
                    ch.mark(nc.vector.tensor_tensor(v, v, rep(ss[:, 0, RW_H * t:RW_H * (t + 1)], RW_D, 2), ALU.mult))
                ch.wait()

            @block.scalar
            def _(act):
                act.wait_ge(s_ss, 1)
                nc.scalar.activation(ss[:, 1, :], ss[:, 0, :], ACT.Sqrt).then_inc(s_rt, 1)


def store(g, name, jobs):
    nc = g.nc
    with Phase(g, name) as ph:
        s = ph.sem("stored")
        with nc.Block() as block:
            @block.sync
            def _(sync):
                for dst, src in jobs:
                    sync.dma_start(dst, src).then_inc(s, 16)
                sync.wait_ge(s, 16 * len(jobs))


DECAY = math.exp(-0.5)


def rw_chunks(g, scr, low_w, low_a, w2, a2, rows, y, coef):
    nc = g.nc
    with Phase(g, "rwkv") as ph:
        ld = ph.sb("loaded", [P, 4, D])
        K_, V_, KK_, R_ = range(4)
        bt = ph.sb("B", [P, D])
        kt_ = ph.sb("K", [P, D])
        at = ph.sb("A", [P, D])
        rt = g.tmp
        tr = g.xT[:, :, :].rearrange("p a b -> p (a b)").rearrange("p (q a b) -> p q a b", q=4, a=KT)
        st = ph.sb("state", [P, KT, RW_D])
        pc = ph.sb("chunk_decay", [P, KT, 2])
        inv = Inverse(g, ph)
        mat = [ph.sb(f"mat{l}", [P, 3, 512]) for l in range(2)]
        rhs = [ph.sb(f"rhs{l}", [P, 256]) for l in range(2)]
        us = [ph.sb(f"U{l}", [P, 256]) for l in range(2)]
        banks = [ph.ps(f"lane{l}", [P, 4, 512]) for l in range(2)]
        n = lambda x: ph.sem(x)
        s_ld, s_free = n("loaded"), n("chunk_done")
        s_wl, s_al, s_lg, s_sg, s_cum, s_exp, s_cs = (n("w_logits"), n("a_logits"), n("logits"), n("sigmoids"),
                                                      n("cum"), n("exps"), n("cum_used"))
        s_til, s_tr, s_trc, s_tra, own = n("tilde"), n("turned"), n("turn_v"), n("turn_a"), n("chain")
        s_mat = [n(f"mat{l}") for l in range(2)]
        s_matc = [n(f"matc{l}") for l in range(2)]
        s_lready = [n(f"L{l}") for l in range(2)]
        s_rhs, s_rhsc, s_u, s_uc = ([n(f"{x}{l}") for l in range(2)] for x in ("rhs", "rhsc", "u", "uc"))
        s_y, s_yc = ([n(f"{x}{l}") for l in range(2)] for x in ("y", "yc"))
        s_act = n("act_chain")
        steps = [(0, t) for t in (0, 1, 2, 3)] + [(1, t) for t in (1, 0, 3, 2)]
        w2s, a2s = w2, a2
        with nc.Block() as block:
            @block.sync
            def _(sync):
                for i, (d, t) in enumerate(steps):
                    if i:
                        sync.wait_ge(s_free, i)
                    for q, name in enumerate(("k", "v", "kk", "r")):
                        if name == "r" and t < 2:
                            continue
                        src = scr[name][t - (2 if name == "r" else 0)]
                        sync.dma_start(ld[:, q, :], src).then_inc(s_ld, 16)

            @block.vector
            def _(dve):
                ch, take = Chain(dve, own), Take(dve)
                level = inv.dve(take)
                for i, (d, t) in enumerate(steps):
                    lat = t >= 2
                    if i in (0, 4):
                        ch.link(nc.vector.memset(st[:, :, :], 0.0))
                    take(s_wl)
                    for j in range(2):
                        ch.mark(nc.vector.tensor_tensor(at[:, j * 512:j * 512 + 512], banks[0][:, j, :],
                                                        rows["w0"][:, d, j * 512:j * 512 + 512], ALU.add))
                    take(s_al)
                    for j in range(2):
                        ch.mark(nc.vector.tensor_tensor(bt[:, j * 512:j * 512 + 512], banks[0][:, 2 + j, :],
                                                        rows["a0"][:, d, j * 512:j * 512 + 512], ALU.add))
                    ch.wait()
                    nc.vector.sem_inc(s_lg, 1)
                    take(s_sg, 2)
                    take(s_ld, 16 * (4 if lat else 3))
                    ch.link(nc.vector.scalar_tensor_tensor(out=kt_[:, :], in0=bt[:, :], scalar=-1.0, in1=rows["ka"],
                                                           op0=ALU.add, op1=ALU.mult))
                    ch.link(nc.vector.scalar_tensor_tensor(out=kt_[:, :], in0=kt_[:, :], scalar=1.0,
                                                           in1=ld[:, K_, :], op0=ALU.add, op1=ALU.mult))
                    ch.link(nc.vector.tensor_tensor(bt[:, :], bt[:, :], ld[:, KK_, :], ALU.mult))
                    if lat:
                        ch.link(nc.vector.tensor_tensor(rt[:, :], ld[:, R_, :], kt_[:, :], ALU.mult))
                        ch.link(nc.vector.tensor_tensor(rt[:, :], rt[:, :], rows["rk"], ALU.mult))
                        co = coef[:, d, t - 2, :]
                        ch.link(nc.vector.tensor_reduce(co, rt[:, :].rearrange("p (h d) -> p h d", h=RW_H),
                                                        AX.X, ALU.add))
                    take(s_cum)
                    take(s_exp, 3 if lat else 2)
                    for j in range(2):
                        sl = slice(j * 512, j * 512 + 512)
                        ch.mark(nc.vector.tensor_tensor(at[:, sl], banks[0][:, j, :], at[:, sl], ALU.subtract))
                    ch.wait()
                    nc.vector.sem_inc(s_cs, 1)
                    take(s_exp)
                    e_a, e_i, e_r = (tr[:, q, :, :].rearrange("p a b -> p (a b)") for q in range(3))
                    ch.mark(nc.vector.scalar_tensor_tensor(out=at[:, :], in0=e_a, scalar=-1.0, in1=ld[:, KK_, :],
                                                           op0=ALU.mult, op1=ALU.mult))
                    ch.mark(nc.vector.tensor_tensor(bt[:, :], bt[:, :], e_i, ALU.mult))
                    ch.mark(nc.vector.tensor_tensor(kt_[:, :], kt_[:, :], e_i, ALU.mult))
                    if lat:
                        ch.mark(nc.vector.tensor_tensor(rt[:, :], ld[:, R_, :], e_r, ALU.mult))
                    ch.wait()
                    nc.vector.sem_inc(s_til, 1)
                    nq = 4 if lat else 3
                    for q in range(nq):
                        take(s_tr)
                        nc.vector.tensor_copy(tr[:, q, 0:4, :], banks[0][:, q, :].rearrange("p (a b) -> p a b", a=4))\
                            .then_inc(s_trc, 1)
                    for r in range(2):
                        strict_lo, strict_up = (C_LOS, C_UPS) if d == 0 else (C_UPS, C_LOS)
                        incl_up = C_UP if d == 0 else C_LO
                        for l in range(2):
                            take(s_mat[l])
                            for q in range(4 if lat else 2):
                                m = (strict_lo, strict_up, incl_up, incl_up)[q]
                                dst = inv.L[l][:, :, :] if q == 0 else mat[l][:, q - 1, :].rearrange(
                                    "p (h c) -> p h c", h=4)
                                ins = nc.vector.tensor_tensor(dst, banks[l][:, q, :].rearrange("p (h c) -> p h c", h=4),
                                                              rep(blk(g, m), 4), ALU.mult)
                                ins.then_inc(s_lready[l] if q == 0 else s_matc[l], 1)
                        for k in range(LEVELS):
                            level(k, banks)
                        for l in range(2):
                            if lat:
                                take(s_y[l])
                                src = banks[l][:, 1, 0:256].rearrange("p (k c) -> p k c", k=4)
                                dst = y[:, t - 2, :].rearrange("p (k l c) -> p k l c", l=2, c=RW_D)[
                                    :, 4 * r:4 * r + 4, l, :]
                                if d == 0:
                                    nc.vector.tensor_copy(dst, src).then_inc(s_yc[l], 1)
                                else:
                                    nc.vector.tensor_tensor(dst, dst, src, ALU.add).then_inc(s_yc[l], 1)
                                take(s_yc[l])
                            take(s_y[l])
                            half = slice(64 * l, 64 * l + 64)
                            sv = st[half, 4 * r:4 * r + 4, :]
                            ch.link(nc.vector.tensor_tensor(sv, sv, banks[l][half, 2, 0:256].rearrange(
                                "p (a b) -> p a b", a=4), ALU.add))
                            nc.vector.tensor_tensor(sv, sv, rep(pc[half, 4 * r:4 * r + 4, 0], RW_D, 2), ALU.mult)\
                                .then_inc(s_yc[l], 1)
                            take(s_yc[l])
                    nc.vector.sem_inc(s_free, 1)

            @block.gpsimd
            def _(pool):
                take = Take(pool)
                for i, (d, t) in enumerate(steps):
                    for r in range(2):
                        inv.pool(take, s_lready, d)

            @block.scalar
            def _(act):
                ch, take = Chain(act, s_act), Take(act)
                flat = lambda q: tr[:, q, :, :].rearrange("p a b -> p (a b)")
                for i, (d, t) in enumerate(steps):
                    lat = t >= 2
                    take(s_lg)
                    nc.scalar.activation(at[:, :], at[:, :], ACT.Sigmoid).then_inc(s_sg, 1)
                    nc.scalar.activation(bt[:, :], bt[:, :], ACT.Sigmoid).then_inc(s_sg, 1)
                    take(s_cum)
                    two = banks[0][:, 0:2, :]
                    o2 = lambda q: flat(q).rearrange("p (a b) -> p a b", a=2)
                    nc.scalar.activation(o2(1), two, ACT.Exp, scale=DECAY).then_inc(s_exp, 1)
                    if lat:
                        nc.scalar.activation(o2(2), two, ACT.Exp, scale=-DECAY).then_inc(s_exp, 1)
                    nc.scalar.activation(pc[:, :, :], banks[0][:, 2, 0:16].rearrange("p (a b) -> p a b", b=2),
                                         ACT.Exp, scale=-DECAY).then_inc(s_exp, 1)
                    take(s_cs)
                    nc.scalar.activation(flat(0), at[:, :], ACT.Exp, scale=-DECAY).then_inc(s_exp, 1)
                    for q in range(4 if lat else 3):
                        take(s_tr)
                        nc.scalar.copy(tr[:, q, 4:8, :], banks[1][:, q, :].rearrange("p (a b) -> p a b", a=4))\
                            .then_inc(s_tra, 1)
                    for r in range(2):
                        inv.act(take, banks)
                        for l in range(2):
                            take(s_rhs[l])
                            nc.scalar.copy(rhs[l][:, :], banks[l][:, 3, 0:256]).then_inc(s_rhsc[l], 1)
                        for l in range(2):
                            take(s_u[l])
                            nc.scalar.copy(us[l][:, :], banks[l][:, 0, 0:256]).then_inc(s_uc[l], 1)

            @block.tensor
            def _(pe):
                take = Take(pe)
                for i, (d, t) in enumerate(steps):
                    lat = t >= 2
                    z = slice(64 * d, 64 * d + 64)
                    for which, (low, w, s) in enumerate(((low_w, w2s, s_wl), (low_a, a2s, s_al))):
                        for j in range(2):
                            mm = nc.tensor.matmul(banks[0][:, 2 * which + j, :], low[z, t * P:(t + 1) * P],
                                                  w[z, j * 512:j * 512 + 512], start=True, stop=True)
                        mm.then_inc(s, 1)
                    take(s_sg, 2)
                    tri = blk(g, C_UP if d == 0 else C_LO)
                    for j in range(2):
                        nc.tensor.matmul(banks[0][:, j, :], tri, at[:, j * 512:j * 512 + 512], start=True, stop=True)
                    for kt in range(KT):
                        mm = nc.tensor.matmul(banks[0][:, 2, 2 * kt:2 * kt + 2], at[:, kt * P:(kt + 1) * P],
                                              blk(g, C_ONE)[:, 0:2], start=True, stop=True)
                    mm.then_inc(s_cum, 1)
                    take(s_til)
                    srcs = (at, bt, kt_, rt)[:4 if lat else 3]
                    for q, src in enumerate(srcs):
                        for kt in range(KT):
                            mm = nc.tensor.transpose(banks[kt // 4][:, q, (kt % 4) * P:(kt % 4 + 1) * P],
                                                     src[:, kt * P:(kt + 1) * P], blk(g, C_ID))
                        mm.then_inc(s_tr, 1)
                    for q in range(len(srcs)):
                        take(s_trc)
                        take(s_tra)
                    A, B, K, R = range(4)
                    for r in range(2):
                        for l in range(2):
                            jobs = ((A, B), (K, A), (B, R), (K, R))[:4 if lat else 2]
                            for q, (lhs, rh) in enumerate(jobs):
                                for h in range(4):
                                    hh = 8 * r + 2 * h + l
                                    o = slice(64 * l, 64 * l + 64)
                                    mm = nc.tensor.matmul(banks[l][:, q, h * P:(h + 1) * P], tr[o, lhs, hh // 2, :],
                                                          tr[o, rh, hh // 2, :], start=True, stop=True)
                            mm.then_inc(s_mat[l], 1)
                        inv_masks = 3 if lat else 1
                        for l in range(2):
                            take(s_matc[l], inv_masks)
                        inv.pe(take, banks)
                        for l in range(2):
                            for h in range(4):
                                hh = 8 * r + 2 * h + l
                                o = slice(64 * l, 64 * l + 64)
                                nc.tensor.matmul(banks[l][:, 3, h * 64:h * 64 + 64], tr[o, A, hh // 2, :],
                                                 st[o, hh // 2, :], start=True, stop=False)
                                mm = nc.tensor.matmul(banks[l][:, 3, h * 64:h * 64 + 64],
                                                      mat[l][:, 0, h * P:(h + 1) * P],
                                                      ld[:, V_, hh * 64:hh * 64 + 64], start=False, stop=True)
                            mm.then_inc(s_rhs[l], 1)
                        for l in range(2):
                            take(s_rhsc[l])
                            for h in range(4):
                                mm = nc.tensor.matmul(banks[l][:, 0, h * 64:h * 64 + 64], inv.Y[l][:, h, :],
                                                      rhs[l][:, h * 64:h * 64 + 64], start=True, stop=True)
                            mm.then_inc(s_u[l], 1)
                        for l in range(2):
                            take(s_uc[l])
                            if lat:
                                for h in range(4):
                                    hh = 8 * r + 2 * h + l
                                    o = slice(64 * l, 64 * l + 64)
                                    dst = banks[l][:, 1, h * 64:h * 64 + 64]
                                    nc.tensor.matmul(dst, tr[o, R, hh // 2, :], st[o, hh // 2, :],
                                                     start=True, stop=False)
                                    nc.tensor.matmul(dst, mat[l][:, 1, h * P:(h + 1) * P],
                                                     us[l][:, h * 64:h * 64 + 64], start=False, stop=False)
                                    mm = nc.tensor.matmul(dst, mat[l][:, 2, h * P:(h + 1) * P],
                                                          ld[:, V_, hh * 64:hh * 64 + 64], start=False, stop=True)
                                mm.then_inc(s_y[l], 1)
                            for h in range(4):
                                hh = 8 * r + 2 * h + l
                                dst = banks[l][64 * l:64 * l + 64, 2, h * 64:h * 64 + 64]
                                nc.tensor.matmul(dst, bt[:, hh * 64:hh * 64 + 64], us[l][:, h * 64:h * 64 + 64],
                                                 start=True, stop=False)
                                mm = nc.tensor.matmul(dst, kt_[:, hh * 64:hh * 64 + 64],
                                                      ld[:, V_, hh * 64:hh * 64 + 64], start=False, stop=True)
                            mm.then_inc(s_y[l], 1)
                        for l in range(2):
                            take(s_yc[l], 2 if lat else 1)


def rw_readout(g, y, coef, v, rows, sg0, sg1, g2a, g2b, out):
    nc = g.nc
    with Phase(g, "rwread") as ph:
        sq = ph.sb("square", [P, D])
        st = ph.sb("stats", [P, 5, 2 * RW_H])
        ps = ph.ps("gate", [P, 4, 512])
        own, s_mm, s_var, s_rt = ph.sem("chain"), ph.sem("gate"), ph.sem("var"), ph.sem("root")
        with nc.Block() as block:
            @block.tensor
            def _(pe):
                for i in range(4):
                    t, j = i // 2, i % 2
                    nc.tensor.matmul(ps[:, i, :], sg0[:, t * P:(t + 1) * P], g2a[:, j * 512:j * 512 + 512],
                                     start=True, stop=False)
                    nc.tensor.matmul(ps[:, i, :], sg1[0:32, t * P:(t + 1) * P], g2b[0:32, j * 512:j * 512 + 512],
                                     start=False, stop=True).then_inc(s_mm, 1)

            @block.scalar
            def _(act):
                act.wait_ge(s_var, 1)
                nc.scalar.activation(st[:, 3, :], st[:, 2, :], ACT.Sqrt).then_inc(s_rt, 1)

            @block.vector
            def _(dve):
                ch = Chain(dve, own)
                heads = lambda a: a.rearrange("p (h d) -> p h d", h=RW_H)
                for t in range(2):
                    c = slice(RW_H * t, RW_H * (t + 1))
                    yt = y[:, t, :]
                    ch.link(nc.vector.tensor_reduce(st[:, 0, c], heads(yt), AX.X, ALU.add))
                    ch.link(nc.vector.tensor_scalar(st[:, 0, c], st[:, 0, c], 1.0 / RW_D, None, ALU.mult))
                    ch.link(nc.vector.tensor_tensor(heads(yt), heads(yt), rep(st[:, 0, c], RW_D, 2), ALU.subtract))
                    ch.link(nc.vector.tensor_tensor(sq[:, :], yt, yt, ALU.mult))
                    ch.link(nc.vector.tensor_reduce(st[:, 1, c], heads(sq[:, :]), AX.X, ALU.add))
                nc.vector.tensor_scalar(st[:, 2, :], st[:, 1, :], 1.0 / RW_D, GN_EPS, ALU.mult, ALU.add)\
                    .then_inc(s_var, 1)
                dve.wait_ge(s_rt, 1)
                ch.link(nc.vector.reciprocal(st[:, 4, :], st[:, 3, :]))
                for t in range(2):
                    c = slice(RW_H * t, RW_H * (t + 1))
                    yt = y[:, t, :]
                    ch.link(nc.vector.tensor_tensor(heads(yt), heads(yt), rep(st[:, 4, c], RW_D, 2), ALU.mult))
                    ch.link(nc.vector.tensor_tensor(yt, yt, rows["lw"], ALU.mult))
                    ch.link(nc.vector.tensor_tensor(yt, yt, rows["lb"], ALU.add))
                    ch.link(nc.vector.tensor_tensor(st[:, 0, c], coef[:, 0, t, :], coef[:, 1, t, :], ALU.add))
                    ch.link(nc.vector.tensor_tensor(heads(sq[:, :]), heads(v[:, t, :]), rep(st[:, 0, c], RW_D, 2),
                                                    ALU.mult))
                    ch.link(nc.vector.tensor_tensor(yt, yt, sq[:, :], ALU.add))
                    for j in range(2):
                        dve.wait_ge(s_mm, 2 * t + j + 1)
                        sl = slice(j * 512, j * 512 + 512)
                        ch.mark(nc.vector.tensor_tensor(out[:, t, sl], yt[:, sl], ps[:, 2 * t + j, :], ALU.mult))
                    ch.wait()


def gd_conv(g, feat, taps, bias, x_high, x_low):
    nc, ring = g.nc, g.ring
    F = feat.shape[1]
    with Phase(g, "gdconv") as ph:
        pad = ph.sb("padded", [P, 4, 259])
        acc = ph.sb("sum", [P, 4, 256])
        banks = ph.ps("bank", [P, 8, 512])
        s_z, s_pad, s_acc, s_out, own = (ph.sem("zero"), ph.sem("padded"), ph.sem("summed"), ph.sem("out"),
                                         ph.sem("chain"))
        done0 = ring.done
        DEPTH = 4
        weights = Split(g, ph, DEPTH, lambda v, k: v[:, :, (k % 4) * P:(k % 4 + 1) * P],
                        lambda k: done0 + k - DEPTH + 1)
        with nc.Block() as block:
            @block.sync
            def _(sync):
                ring.issue(sync, F // 4)

            @block.gpsimd
            def _(pool):
                nc.gpsimd.memset(pad[:, :, 0:3], 0.0).then_inc(s_z, 1)

            @block.tensor
            def _(pe):
                for f in range(F):
                    if f % 4 == 0:
                        ring.take(pe)
                    if f >= 8:
                        pe.wait_ge(s_pad, f - 7)
                    wh, wl = weights.take(pe, f)
                    for kt in range(KT):
                        xh, xl = x_high[:, kt, :], x_low[:, kt, :]
                        for k, (w, x) in enumerate(((wh, xh), (wh, xl), (wl, xh))):
                            mm = nc.tensor.matmul(banks[:, f % 8, 0:256], w[:, kt, :], x,
                                                  start=(kt + k == 0), stop=(kt == KT - 1 and k == 2))
                    ring.mark(mm)

            @block.scalar
            def _(act):
                act.wait_ge(s_z, 1)

                def silu(f):
                    act.wait_ge(s_acc, f + 1)
                    nc.scalar.activation(feat[:, f, :], acc[:, f % 4, :], ACT.Silu, bias=bias[:, f:f + 1])\
                        .then_inc(s_out, 1)

                for k in range(DEPTH):
                    weights.high(act, k)
                for f in range(F):
                    act.wait_ge(ring.gemm_done, done0 + f + 1)
                    if f >= 4:
                        act.wait_ge(s_acc, f - 3)
                    nc.scalar.copy(pad[:, f % 4, 3:259], banks[:, f % 8, 0:256]).then_inc(s_pad, 1)
                    if f + DEPTH < F:
                        weights.high(act, f + DEPTH)
                    if f >= 2:
                        silu(f - 2)
                silu(F - 2)
                silu(F - 1)
                act.wait_ge(s_out, F)

            @block.vector
            def _(dve):
                ch = Chain(dve, own)
                for k in range(DEPTH):
                    weights.low(dve, k)
                for f in range(F):
                    dve.wait_ge(s_pad, f + 1)
                    if f + DEPTH < F:
                        weights.low(dve, f + DEPTH)
                    if f >= 4:
                        dve.wait_ge(s_out, f - 3)
                    a = acc[:, f % 4, :]
                    ch.link(nc.vector.tensor_scalar(a, pad[:, f % 4, 0:256], taps[:, f, 0:1], None, ALU.mult))
                    for j in range(1, 4):
                        ins = nc.vector.scalar_tensor_tensor(out=a, in0=pad[:, f % 4, j:j + 256],
                                                             scalar=taps[:, f, j:j + 1], in1=a,
                                                             op0=ALU.mult, op1=ALU.add)
                        if j < 3:
                            ch.link(ins)
                        else:
                            ins.then_inc(s_acc, 1)


def gd_l2(g, feat):
    nc = g.nc
    N = 2 * GD_H
    with Phase(g, "gdl2") as ph:
        sq = ph.sb("square", [P, 4, 256])
        r = ph.sb("root", [P, 4, 256])
        ps = ph.ps("sum", [P, 4, 512])
        s_sq, s_mm, s_e, s_rt, s_f, own = (ph.sem("square"), ph.sem("sum"), ph.sem("eps"), ph.sem("root"),
                                           ph.sem("final"), ph.sem("chain"))
        with nc.Block() as block:
            @block.gpsimd
            def _(pool):
                for n in range(N):
                    if n >= 4:
                        pool.wait_ge(s_mm, n - 3)
                    nc.gpsimd.tensor_tensor(sq[:, n % 4, :], feat[:, n, :], feat[:, n, :], ALU.mult).then_inc(s_sq, 1)

            @block.tensor
            def _(pe):
                for n in range(N):
                    pe.wait_ge(s_sq, n + 1)
                    if n >= 4:
                        pe.wait_ge(s_e, n - 3)
                    nc.tensor.matmul(ps[:, n % 4, 0:256], blk(g, C_ONE), sq[:, n % 4, :], start=True, stop=True)\
                        .then_inc(s_mm, 1)

            @block.scalar
            def _(act):
                for n in range(N):
                    act.wait_ge(s_e, n + 1)
                    nc.scalar.activation(r[:, n % 4, :], r[:, n % 4, :], ACT.Sqrt).then_inc(s_rt, 1)

            @block.vector
            def _(dve):
                ch = Chain(dve, own)

                def end(n):
                    dve.wait_ge(s_rt, n + 1)
                    ch.link(nc.vector.reciprocal(r[:, n % 4, :], r[:, n % 4, :]))
                    sc = P ** -0.5 if n < GD_H else 1.0
                    nc.vector.scalar_tensor_tensor(out=feat[:, n, :], in0=feat[:, n, :], scalar=sc,
                                                   in1=r[:, n % 4, :], op0=ALU.mult, op1=ALU.mult).then_inc(s_f, 1)

                for n in range(N):
                    dve.wait_ge(s_mm, n + 1)
                    if n >= 4:
                        dve.wait_ge(s_f, n - 3)
                    nc.vector.tensor_scalar(r[:, n % 4, :], ps[:, n % 4, 0:256], EPS, None, ALU.add).then_inc(s_e, 1)
                    if n >= 2:
                        end(n - 2)
                end(N - 2)
                end(N - 1)
                dve.wait_ge(s_f, N)


def gd_gates(g, p2, rows, beta, dt, ga, cums):
    nc = g.nc
    with Phase(g, "gdgates") as ph:
        z = ph.sb("z", [P, 2, 24])
        az = ph.sb("az", [P, 2, 24])
        ea = ph.sb("ea", [P, 24])
        ps = ph.ps("cums", [P, 4, 24])
        own, s_z, s_a, s_ga, s_mm = ph.sem("chain"), ph.sem("abs"), ph.sem("act"), ph.sem("ga"), ph.sem("cums")
        with nc.Block() as block:
            @block.vector
            def _(dve):
                ch = Chain(dve, own)
                ch.mark(nc.vector.tensor_tensor(z[:, :, 0:8], p2[:, :, 1032:1040],
                                                rep(rows[:, 0:8], 2), ALU.add))
                ch.mark(nc.vector.tensor_tensor(z[:, :, 8:24], p2[:, :, 2064:2080], rep(rows[:, 8:24], 2), ALU.add))
                ch.wait()
                nc.vector.scalar_tensor_tensor(out=az[:, :, :], in0=z[:, :, :], scalar=-1.0, in1=z[:, :, :],
                                               op0=ALU.mult, op1=ALU.max).then_inc(s_z, 1)
                dve.wait_ge(s_a, 1)
                nc.vector.tensor_scalar(az[:, :, :], az[:, :, :], 1.0, None, ALU.add).then_inc(s_z, 1)
                dve.wait_ge(s_a, 2)
                ch.link(nc.vector.scalar_tensor_tensor(out=z[:, :, :], in0=z[:, :, :], scalar=0.0, in1=az[:, :, :],
                                                       op0=ALU.max, op1=ALU.add))
                ch.mark(nc.vector.tensor_copy(dt[:, :, :], z[:, :, 8:24]))
                dve.wait_ge(s_a, 3)
                nc.vector.scalar_tensor_tensor(out=ga[:, :, :], in0=z[:, :, :], scalar=-1.0, in1=rep(ea[:, :], 2),
                                               op0=ALU.mult, op1=ALU.mult).then_inc(s_ga, 1)
                dve.wait_ge(s_mm, 1)
                ch.link(nc.vector.tensor_copy(cums[:, :, :], ps[:, :, :]))

            @block.scalar
            def _(act):
                act.wait_ge(s_z, 1)
                nc.scalar.activation(az[:, :, :], az[:, :, :], ACT.Exp, scale=-1.0).then_inc(s_a, 1)
                act.wait_ge(s_z, 2)
                nc.scalar.activation(az[:, :, :], az[:, :, :], ACT.Ln).then_inc(s_a, 1)
                act.wait_ge(s_a, 2)
                nc.scalar.activation(ea[:, :], rows[:, 24:48], ACT.Exp).then_inc(s_a, 1)
                nc.scalar.activation(beta[:, :, :], p2[:, :, 1024:1032], ACT.Sigmoid).then_inc(s_a, 1)
                act.wait_ge(s_a, 4)

            @block.tensor
            def _(pe):
                pe.wait_ge(s_ga, 1)
                for t in range(2):
                    nc.tensor.matmul(ps[:, t, :], blk(g, C_UP), ga[:, t, :], start=True, stop=True)
                    mm = nc.tensor.matmul(ps[:, 2 + t, :], blk(g, C_ONE), ga[:, t, :], start=True, stop=True)
                mm.then_inc(s_mm, 1)


def gd_chunks(g, feat, ktok, vtok, beta, ga, cums, og):
    nc = g.nc
    with Phase(g, "gdn") as ph:
        inv = Inverse(g, ph)
        spare = g.xT[:, :, :].rearrange("p a (h c) -> p a h c", h=4)
        wide, eA, eT, rhs = ([spare[:, 2 * q + l, :, :] for l in range(2)] for q in range(4))
        us = [ph.sb(f"U{l}", [P, 4, P]) for l in range(2)]
        st = [g.tmp[:, 512 * l:512 * l + 512].rearrange("p (h c) -> p h c", h=4) for l in range(2)]
        ex = ph.sb("exps", [P, 3, 2, 8])
        nb = ph.sb("minus_beta", [P, 2, 8])
        banks = [ph.ps(f"lane{l}", [P, 4, 512]) for l in range(2)]
        own, s_c, s_ce = ph.sem("chain"), ph.sem("cols"), ph.sem("cols_exp")
        two = lambda x: [ph.sem(f"{x}{l}") for l in range(2)]
        s_wide, s_gb, s_dif, s_exp, s_msk, s_lready = (two(x) for x in ("wide", "gb", "dif", "exp", "msk", "Lr"))
        s_rhs, s_u, s_uc, s_o, s_oc, s_ks = (two(x) for x in ("rhs", "u", "uc", "o", "oc", "ks"))
        s_m = two("m")
        b4 = lambda l, q: banks[l][:, q, :].rearrange("p (h c) -> p h c", h=4)
        with nc.Block() as block:
            @block.vector
            def _(dve):
                ch, take = Chain(dve, own), Take(dve)
                level = inv.dve(take)
                ch.mark(nc.vector.tensor_tensor(ex[:, 1, :, :], cums[:, 2:4, 0:8], cums[:, 0:2, 0:8], ALU.subtract))
                ch.link(nc.vector.tensor_scalar(nb[:, :, :], beta[:, :, :], -1.0, None, ALU.mult))
                nc.vector.sem_inc(s_c, 1)
                take(s_ce, 2)
                ch.link(nc.vector.tensor_tensor(ex[:, 2, :, :], nb[:, :, :], ex[:, 0, :, :], ALU.mult))
                for i in range(2):
                    tok = slice(i * P, (i + 1) * P)
                    for l in range(2):
                        for h in range(4):
                            hh = 4 * l + h
                            ins = nc.vector.tensor_scalar(wide[l][:, h, :], blk(g, C_ONE), ga[:, i, hh:hh + 1],
                                                          None, ALU.mult)
                            ins.then_inc(s_wide[l], 1)
                    for l in range(2):
                        take(s_gb[l])
                        for h in range(4):
                            hh = 4 * l + h
                            gam = cums[:, i, hh:hh + 1]
                            G = banks[l][:, 0, h * P:(h + 1) * P]
                            nc.vector.tensor_scalar(eA[l][:, h, :], G, gam, 0.0, ALU.subtract, ALU.max)\
                                .then_inc(s_dif[l], 1)
                            nc.vector.tensor_scalar(eT[l][:, h, :], G, gam, 0.0, ALU.subtract, ALU.min)\
                                .then_inc(s_dif[l], 1)
                    for l in range(2):
                        take(s_msk[l], 2)
                        for h in range(4):
                            hh = 4 * l + h
                            nc.vector.scalar_tensor_tensor(out=inv.L[l][:, h, :], in0=banks[l][:, 1, h * P:(h + 1) * P],
                                                           scalar=nb[:, i, hh:hh + 1], in1=eA[l][:, h, :],
                                                           op0=ALU.mult, op1=ALU.mult).then_inc(s_lready[l], 1)
                        nc.vector.tensor_tensor(eT[l][:, :, :], b4(l, 2), eT[l][:, :, :], ALU.mult)\
                            .then_inc(s_m[l], 1)
                        for h in range(4):
                            hh = 4 * l + h
                            ch.mark(nc.vector.tensor_scalar(rhs[l][:, h, :], vtok[:, i, hh * P:(hh + 1) * P],
                                                            beta[:, i, hh:hh + 1], None, ALU.mult))
                        if i:
                            ch.wait()
                            take(s_ks[l])
                            for h in range(4):
                                hh = 4 * l + h
                                ch.mark(nc.vector.scalar_tensor_tensor(
                                    out=rhs[l][:, h, :], in0=banks[l][:, 3, h * P:(h + 1) * P],
                                    scalar=ex[:, 2, i, hh:hh + 1], in1=rhs[l][:, h, :], op0=ALU.mult, op1=ALU.add))
                        else:
                            for h in range(4):
                                hh = 4 * l + h
                                kv = ktok[:, 0, hh * P:(hh + 1) * P]
                                ch.mark(nc.vector.tensor_scalar(kv, kv, ex[:, 1, 0, hh:hh + 1], None, ALU.mult))
                        ch.wait()
                        nc.vector.sem_inc(s_rhs[l], 1)
                    for k in range(LEVELS):
                        level(k, banks)
                    for l in range(2):
                        take(s_o[l])
                        dst = og[:, i, l * 512:l * 512 + 512]
                        if i == 0:
                            nc.vector.tensor_copy(dst, banks[l][:, 1, :]).then_inc(s_oc[l], 1)
                            take(s_o[l])
                            nc.vector.tensor_copy(st[l][:, :, :], b4(l, 2)).then_inc(s_oc[l], 1)
                        else:
                            for h in range(4):
                                hh = 4 * l + h
                                ch.mark(nc.vector.tensor_scalar(og[:, i, hh * P:(hh + 1) * P],
                                                                banks[l][:, 3, h * P:(h + 1) * P],
                                                                ex[:, 0, i, hh:hh + 1], None, ALU.mult))
                            ch.wait()
                            ch.link(nc.vector.tensor_tensor(dst, dst, banks[l][:, 1, :], ALU.add))

            @block.gpsimd
            def _(pool):
                take = Take(pool)
                for i in range(2):
                    for l in range(2):
                        for buf, m in ((eA, C_LOS), (eT, C_UP)):
                            take(s_exp[l])
                            nc.gpsimd.tensor_tensor(buf[l][:, :, :], buf[l][:, :, :], rep(blk(g, m), 4), ALU.mult)\
                                .then_inc(s_msk[l], 1)
                    for l in range(2):
                        take(s_lready[l], 3)
                    inv.pool(take, s_lready, 0)

            @block.scalar
            def _(act):
                take = Take(act)
                take(s_c)
                nc.scalar.activation(ex[:, 0, :, :], cums[:, 0:2, 0:8], ACT.Exp).then_inc(s_ce, 1)
                nc.scalar.activation(ex[:, 1, :, :], ex[:, 1, :, :], ACT.Exp).then_inc(s_ce, 1)
                for i in range(2):
                    for l in range(2):
                        take(s_dif[l], 8)
                        nc.scalar.activation(eA[l][:, :, :], eA[l][:, :, :], ACT.Exp, scale=-1.0).then_inc(s_exp[l], 1)
                        nc.scalar.activation(eT[l][:, :, :], eT[l][:, :, :], ACT.Exp).then_inc(s_exp[l], 1)
                    inv.act(take, banks)
                    for l in range(2):
                        take(s_u[l])
                        nc.scalar.copy(us[l][:, :, :], b4(l, 0)).then_inc(s_uc[l], 1)

            @block.tensor
            def _(pe):
                take = Take(pe)
                for i in range(2):
                    tok = slice(i * P, (i + 1) * P)
                    for l in range(2):
                        if i:
                            take(s_oc[l], 2)
                        for h in range(4):
                            hh = 4 * l + h
                            take(s_wide[l])
                            cols = slice(h * P, (h + 1) * P)
                            nc.tensor.matmul(banks[l][:, 0, cols], wide[l][:, h, :], blk(g, C_UP), start=True, stop=True)
                            kT, qT = feat[:, 8 + hh, tok], feat[:, hh, tok]
                            nc.tensor.matmul(banks[l][:, 1, cols], kT, kT, start=True, stop=True)
                            mm = nc.tensor.matmul(banks[l][:, 2, cols], kT, qT, start=True, stop=True)
                        mm.then_inc(s_gb[l], 1)
                        if i:
                            for h in range(4):
                                mm = nc.tensor.matmul(banks[l][:, 3, h * P:(h + 1) * P], feat[:, 8 + 4 * l + h, tok],
                                                      st[l][:, h, :], start=True, stop=True)
                            mm.then_inc(s_ks[l], 1)
                    for l in range(2):
                        take(s_m[l])
                        take(s_rhs[l])
                    inv.pe(take, banks)
                    for l in range(2):
                        for h in range(4):
                            mm = nc.tensor.matmul(banks[l][:, 0, h * P:(h + 1) * P], inv.Y[l][:, h, :], rhs[l][:, h, :],
                                                  start=True, stop=True)
                        mm.then_inc(s_u[l], 1)
                    for l in range(2):
                        take(s_uc[l])
                        for h in range(4):
                            hh = 4 * l + h
                            cols = slice(h * P, (h + 1) * P)
                            if i:
                                nc.tensor.matmul(banks[l][:, 3, cols], feat[:, hh, tok], st[l][:, h, :],
                                                 start=True, stop=True)
                            mm = nc.tensor.matmul(banks[l][:, 1, cols], eT[l][:, h, :], us[l][:, h, :],
                                                  start=True, stop=True)
                        mm.then_inc(s_o[l], 1)
                        if i == 0:
                            for h in range(4):
                                hh = 4 * l + h
                                mm = nc.tensor.matmul(banks[l][:, 2, h * P:(h + 1) * P],
                                                      ktok[:, 0, hh * P:(hh + 1) * P], us[l][:, h, :],
                                                      start=True, stop=True)
                            mm.then_inc(s_o[l], 1)


def ssd(g, feat, xtok, dt, ga, cums, drow, ys):
    nc = g.nc
    with Phase(g, "ssd") as ph:
        cb = ph.sb("cb", [P, SS_G, 384])
        xd = ph.sb("xdt", [P, 2, D])
        wide = ph.sb("wide", [P, 4, 2, P])
        dec = ph.sb("decay", [P, 4, 384])
        ac = ph.sb("acum", [P, 2, SS_H])
        pcb = ph.ps("cb", [P, 2, 512])
        G = ph.ps("G", [P, 4, 512])
        out = ph.ps("out", [P, 2, 512])
        own, s_cb, s_cbc = ph.sem("chain"), ph.sem("cb"), ph.sem("cb_ready")
        s_w, s_g, s_d, s_e, s_wt, s_o, s_oc = (ph.sem(x) for x in ("wide", "G", "diff", "exp", "weights", "out", "oc"))
        with nc.Block() as block:
            @block.tensor
            def _(pe):
                for gr in range(SS_G):
                    B, C = feat[:, 32 + gr, :], feat[:, 34 + gr, :]
                    nc.tensor.matmul(pcb[:, gr, 0:256], B[:, 0:P], C, start=True, stop=True)
                    nc.tensor.matmul(pcb[:, gr, 256:384], B[:, P:256], C[:, P:256], start=True, stop=True)\
                        .then_inc(s_cb, 1)
                pe.wait_ge(s_cbc, 1)

                def rows(h):
                    pe.wait_ge(s_w, 2 * h + 2)
                    if h >= 4:
                        pe.wait_ge(s_d, 2 * (h - 3))
                    b = h % 4
                    nc.tensor.matmul(G[:, b, 0:P], wide[:, b, 0, :], blk(g, C_UP), start=True, stop=True)
                    nc.tensor.matmul(G[:, b, P:256], wide[:, b, 0, :], blk(g, C_ONE), start=True, stop=False)
                    nc.tensor.matmul(G[:, b, P:256], wide[:, b, 1, :], blk(g, C_UP), start=False, stop=True)\
                        .then_inc(s_g, 1)

                def values(h):
                    pe.wait_ge(s_wt, h + 1)
                    if h % 4 == 0 and h >= 8:
                        pe.wait_ge(s_oc, h // 4 - 1)
                    bank = out[:, (h // 4) % 2, :].rearrange("p (t h c) -> p t h c", t=2, h=4)
                    W = dec[:, h % 4, :]
                    x0, x1 = xd[:, 0, h * 64:h * 64 + 64], xd[:, 1, h * 64:h * 64 + 64]
                    nc.tensor.matmul(bank[:, 0, h % 4, :], W[:, 0:P], x0, start=True, stop=True)
                    nc.tensor.matmul(bank[:, 1, h % 4, :], W[:, P:256], x0, start=True, stop=False)
                    nc.tensor.matmul(bank[:, 1, h % 4, :], W[:, 256:384], x1, start=False, stop=True).then_inc(s_o, 1)

                for h in range(SS_H + 1):
                    if h < SS_H:
                        rows(h)
                    if h >= 1:
                        values(h - 1)

            @block.gpsimd
            def _(pool):
                for h in range(SS_H):
                    pool.wait_ge(s_e, h + 1)
                    nc.gpsimd.tensor_tensor(dec[:, h % 4, :], dec[:, h % 4, :], cb[:, h // 8, :], ALU.mult)\
                        .then_inc(s_wt, 1)

            @block.scalar
            def _(act):
                for h in range(SS_H):
                    act.wait_ge(s_d, 2 * h + 2)
                    nc.scalar.activation(dec[:, h % 4, :], dec[:, h % 4, :], ACT.Exp).then_inc(s_e, 1)

            @block.vector
            def _(dve):
                ch = Chain(dve, own)
                for gr in range(SS_G):
                    dve.wait_ge(s_cb, gr + 1)
                    ch.mark(nc.vector.tensor_tensor(cb[:, gr, 0:P], pcb[:, gr, 0:P], blk(g, C_UP), ALU.mult))
                    ch.mark(nc.vector.tensor_copy(cb[:, gr, P:256], pcb[:, gr, P:256]))
                    ch.mark(nc.vector.tensor_tensor(cb[:, gr, 256:384], pcb[:, gr, 256:384], blk(g, C_UP), ALU.mult))
                ch.mark(nc.vector.tensor_copy(ac[:, 0, :], cums[:, 0, 8:24]))
                ch.mark(nc.vector.tensor_tensor(ac[:, 1, :], cums[:, 1, 8:24], cums[:, 2, 8:24], ALU.add))
                for t in range(2):
                    v = xtok[:, t, :].rearrange("p (h c) -> p h c", h=SS_H)
                    ch.mark(nc.vector.tensor_tensor(xd[:, t, :].rearrange("p (h c) -> p h c", h=SS_H), v,
                                                    rep(dt[:, t, :], SS_P, 2), ALU.mult))
                    ch.mark(nc.vector.tensor_tensor(ys[:, t, :].rearrange("p (h c) -> p h c", h=SS_H), v,
                                                    rep(drow, SS_P, 2), ALU.mult))
                ch.wait()
                nc.vector.sem_inc(s_cbc, 1)

                def wides(h):
                    if h >= 4:
                        dve.wait_ge(s_g, h - 3)
                    for t in range(2):
                        nc.vector.tensor_scalar(wide[:, h % 4, t, :], blk(g, C_ONE), ga[:, t, 8 + h:9 + h], None,
                                                ALU.mult).then_inc(s_w, 1)

                def diff(h):
                    dve.wait_ge(s_g, h + 1)
                    if h >= 4:
                        dve.wait_ge(s_o, h - 3)
                    for t, a, b, c in ((0, 0, 256, 0), (1, 256, 384, P)):
                        nc.vector.tensor_scalar(dec[:, h % 4, a:b], G[:, h % 4, c:256], ac[:, t, h:h + 1], 0.0,
                                                ALU.subtract, ALU.min).then_inc(s_d, 1)

                def evac(q):
                    dve.wait_ge(s_o, 4 * q + 4)
                    v = ys[:, :, q * 256:q * 256 + 256]
                    nc.vector.tensor_tensor(v, v, out[:, q % 2, :].rearrange("p (t c) -> p t c", t=2), ALU.add)\
                        .then_inc(s_oc, 1)

                wides(0)
                for h in range(SS_H):
                    if h + 1 < SS_H:
                        wides(h + 1)
                    diff(h)
                    if h % 4 == 2 and h >= 6:
                        evac(h // 4 - 1)
                evac(3)
                dve.wait_ge(s_oc, 4)


def gd_merge(g, p2, og, ys, rows, mix):
    nc = g.nc
    with Phase(g, "gdmerge") as ph:
        sq = ph.sb("square", [P, D])
        sz = ph.sb("silu", [P, 2, 2, D])
        ss = ph.sb("sums", [P, 3, 2 * 10])
        own, s_sz, s_ms, s_rt = ph.sem("chain"), ph.sem("silu"), ph.sem("mean"), ph.sem("root")
        with nc.Block() as block:
            @block.scalar
            def _(act):
                for t in range(2):
                    for j in range(2):
                        nc.scalar.activation(sz[:, t, j, :], p2[:, t, 1040 * j:1040 * j + 1024], ACT.Silu)\
                            .then_inc(s_sz, 1)
                act.wait_ge(s_ms, 1)
                nc.scalar.activation(ss[:, 2, :], ss[:, 1, :], ACT.Sqrt).then_inc(s_rt, 1)

            @block.vector
            def _(dve):
                ch = Chain(dve, own)
                dve.wait_ge(s_sz, 4)
                for t in range(2):
                    o, y = og[:, t, :], ys[:, t, :]
                    ch.link(nc.vector.tensor_tensor(y, y, sz[:, t, 1, :], ALU.mult))
                    for x, n, c in ((o, 8, 10 * t), (y, 2, 10 * t + 8)):
                        ch.link(nc.vector.tensor_tensor(sq[:, :], x, x, ALU.mult))
                        ch.link(nc.vector.tensor_reduce(ss[:, 0, c:c + n], sq[:, :].rearrange("p (h d) -> p h d", h=n),
                                                        AX.X, ALU.add))
                        ch.link(nc.vector.tensor_scalar(ss[:, 1, c:c + n], ss[:, 0, c:c + n], n / D, EPS,
                                                        ALU.mult, ALU.add))
                nc.vector.sem_inc(s_ms, 1)
                dve.wait_ge(s_rt, 1)
                ch.link(nc.vector.reciprocal(ss[:, 0, :], ss[:, 2, :]))
                for t in range(2):
                    o, y = og[:, t, :], ys[:, t, :]
                    for x, n, c in ((o, 8, 10 * t), (y, 2, 10 * t + 8)):
                        v = x.rearrange("p (h d) -> p h d", h=n)
                        ch.link(nc.vector.tensor_tensor(v, v, rep(ss[:, 0, c:c + n], D // n, 2), ALU.mult))
                    ov = o.rearrange("p (h d) -> p h d", h=8)
                    ch.link(nc.vector.tensor_tensor(ov, ov, rep(rows["gn"], 8), ALU.mult))
                    ch.link(nc.vector.tensor_tensor(mix[:, t, 0:D], o, sz[:, t, 0, :], ALU.mult))
                    ch.link(nc.vector.tensor_tensor(mix[:, t, D:2 * D], y, rows["sn"], ALU.mult))


def gemm_rows(g, name, n_chunks, actT, row):
    nc, ring = g.nc, g.ring
    with Phase(g, name) as ph:
        banks = ph.ps("bank", [P, 4, 512])
        own, s_o = ph.sem("chain"), ph.sem("out")
        done0 = ring.done
        with nc.Block() as block:
            @block.sync
            def _(sync):
                ring.issue(sync, n_chunks)

            @block.tensor
            def _(pe):
                for n in range(n_chunks):
                    wv = ring.take(pe)
                    for j in range(4):
                        for i in range(4):
                            mm = nc.tensor.matmul(banks[:, i, :], actT[:, 4 * n + j, (i // 2) * P:(i // 2 + 1) * P],
                                                  wv[:, j, (i % 2) * 512:(i % 2) * 512 + 512],
                                                  start=(n + j == 0), stop=(n == n_chunks - 1 and j == 3))
                    ring.mark(mm)

            @block.vector
            def _(dve):
                ch = Chain(dve, own)
                dve.wait_ge(ring.gemm_done, done0 + n_chunks)
                for i in range(4):
                    residual(g, lambda t: row, 0)(ch, 2 + i // 2, (i % 2) * 512, 512, banks[:, i, :]).then_inc(s_o, 1)
                dve.wait_ge(s_o, 4)


N_PAIR = 256 * TOP_K
N_SLOT = N_PAIR + P
N_ITEM = N_EXP + (N_PAIR - 1) // (P + 1) + 1


def router(g, rw, rb, iota, bdown, acc, rank, topg, XgT, table, S, gsel, bgu, b16, pick):
    nc = g.nc
    with Phase(g, "router") as ph:
        w = ph.sb("w", [P, KT, N_EXP])
        bd = ph.sb("bd", [N_EXP, D])
        lg = ph.sb("logits", [P, 2, N_EXP])
        top = ph.sb("top", [P, 2, 8])
        idx = ph.sb("idx", [P, 2, 8], U32)
        idf = ph.sb("idxf", [P, 2, 8])
        st = ph.sb("stats", [P, 2, 4])
        hot = ph.sb("onehot", [P, 2, TOP_K, N_EXP])
        hotb = ph.sb("onehot_base", [P, 2, TOP_K, N_EXP])
        gates = ph.sb("gates", [P, 2, N_EXP])
        mask = ph.sb("mask", [P, 2, N_EXP])
        base = ph.sb("base", [P, 2, N_EXP])
        gT = ph.sb("gatesT", [N_EXP, 2, P])
        cnt = ph.sb("counts", [N_EXP, 2, P])
        prev = ph.sb("previous", [1, 3, N_EXP])
        le = ph.sb("item_expert", [1, 2, N_ITEM, N_EXP])
        item = ph.sb("items", [1, 4, N_ITEM])
        htok = ph.sb("tokens", [P, 2, D])
        pl = ph.ps("logits", [P, 2, 512])
        pt = ph.ps("small", [P, 2, 512])
        pb = ph.ps("wide", [P, 4, 512])
        s_ld, s_l, s_t, s_e, s_g, s_gt, s_gc, s_b, own = (ph.sem(x) for x in (
            "loaded", "logits", "top", "exp", "gates", "gatesT", "gatesT_copied", "bias", "chain"))
        b32 = ph.sb("bias_rest", [96, 2048])
        s_pad, s_ldb, s_pc = ph.sem("padding"), ph.sem("biases_loaded"), ph.sem("pool_chain")
        s_tok, s_tokc, s_m, s_cnt, s_cntc, s_base, s_S, s_xg, s_xgc, s_bc = (ph.sem(x) for x in (
            "tokens", "tokens_copied", "mask", "counts", "counts_copied", "base", "slots", "gathered",
            "gathered_copied", "bias_copied"))
        with nc.Block() as block:
            @block.sync
            def _(sync):
                sync.dma_start(w[:, :, :], rw.rearrange("(a p) n -> p a n", p=P)).then_inc(s_ld, 16)
                sync.dma_start(bd[:, :], bdown).then_inc(s_ld, 16)
                for q in range(3):
                    sync.dma_start(b32[32 * q:32 * q + 32, :], bgu).then_inc(s_ldb, 16)

            @block.tensor
            def _(pe):
                pe.wait_ge(s_ld, 32)
                for t in range(2):
                    for kt in range(KT):
                        mm = nc.tensor.matmul(pl[:, t, 0:N_EXP], g.xT[:, kt, t * P:(t + 1) * P], w[:, kt, :],
                                              start=(kt == 0), stop=(kt == KT - 1))
                    mm.then_inc(s_l, 1)
                for t in range(2):
                    for kt in range(KT):
                        mm = nc.tensor.transpose(pb[:, 2 * t + kt // 4, (kt % 4) * P:(kt % 4 + 1) * P],
                                                 g.xT[:, kt, t * P:(t + 1) * P], blk(g, C_ID))
                        if kt % 4 == 3:
                            mm.then_inc(s_tok, 1)
                pe.wait_ge(s_m, 1)
                for t in range(2):
                    nc.tensor.matmul(pt[0:N_EXP, 0, 0:P], mask[:, t, :], blk(g, C_ONE), start=(t == 0), stop=(t == 1))
                for t in range(2):
                    mm = nc.tensor.matmul(pt[:, 1, 0:N_EXP], blk(g, C_ONE), mask[:, t, :],
                                          start=(t == 0), stop=(t == 1))
                mm.then_inc(s_cnt, 1)
                pe.wait_ge(s_cntc, 1)
                for t in range(2):
                    nc.tensor.matmul(pl[:, t, 0:N_EXP], cnt[:, 0, :], blk(g, C_UPS)[0:N_EXP, 0:N_EXP],
                                     start=True, stop=False)
                    if t:
                        nc.tensor.matmul(pl[:, t, 0:N_EXP], blk(g, C_ONE), mask[:, 0, :], start=False, stop=False)
                    nc.tensor.matmul(pl[:, t, 0:N_EXP], blk(g, C_UPS), mask[:, t, :], start=False, stop=True)
                nc.tensor.matmul(pt[:, 1, 0:N_EXP], cnt[:, 1, :], blk(g, C_UPS)[0:N_EXP, 0:N_EXP],
                                 start=True, stop=True).then_inc(s_base, 1)
                pe.wait_ge(s_S, 1)
                pe.wait_ge(s_tokc, 4)
                for kt in range(KT):
                    for sh in range(2):
                        n = 2 * kt + sh
                        if n >= 4:
                            pe.wait_ge(s_xgc, n - 3)
                        for t in range(2):
                            mm = nc.tensor.matmul(pb[:, n % 4, :], htok[:, t, kt * P:(kt + 1) * P],
                                                  S[:, t, sh * 512:(sh + 1) * 512], start=(t == 0), stop=(t == 1))
                        mm.then_inc(s_xg, 1)
                pe.wait_ge(s_xgc, 2 * KT)
                for t in range(2):
                    pe.wait_ge(s_g, t + 1)
                    nc.tensor.transpose(pl[0:N_EXP, t, 0:P], gates[:, t, :], blk(g, C_ID)).then_inc(s_gt, 1)
                for t in range(2):
                    pe.wait_ge(s_gc, t + 1)
                    for j in range(2):
                        nc.tensor.matmul(pb[:, 2 * t + j, :], gT[:, t, :], bd[:, j * 512:j * 512 + 512],
                                         start=True, stop=True).then_inc(s_b, 1)

            @block.scalar
            def _(act):
                for t in range(2):
                    act.wait_ge(s_t, t + 1)
                    nc.scalar.activation(top[:, t, 0:4], top[:, t, 0:4], ACT.Exp, bias=st[:, t, 0:1])\
                        .then_inc(s_e, 1)
                for n in range(4):
                    act.wait_ge(s_tok, n + 1)
                    nc.scalar.copy(htok[:, n // 2, (n % 2) * 512:(n % 2) * 512 + 512], pb[:, n, :]).then_inc(s_tokc, 1)
                for n in range(2 * KT):
                    act.wait_ge(s_xg, n + 1)
                    nc.scalar.copy(XgT[:, n // 2, (n % 2) * 512:(n % 2) * 512 + 512], pb[:, n % 4, :])\
                        .then_inc(s_xgc, 1)
                for i in range(4):
                    act.wait_ge(s_b, i + 1)
                    nc.scalar.copy(acc[:, i // 2, (i % 2) * 512:(i % 2) * 512 + 512], pb[:, i, :]).then_inc(s_bc, 1)
                act.wait_ge(s_bc, 4)

            @block.gpsimd
            def _(pool):
                nc.gpsimd.memset(XgT[:, :, N_PAIR:], 0.0).then_inc(s_pad, 1)
                pool.wait_ge(s_pad, 1)
                pool.wait_ge(s_ldb, 48)
                ch = Chain(pool, s_pc)
                v = nc.gpsimd
                for q in range(3):
                    rows = slice(32 * q, 32 * q + 32)
                    ch.link(v.tensor_copy(pick[rows, :], blk(g, C_ID)[rows, rows]))
                ch.link(v.tensor_copy(b16[:, :], b32[:, :]))
                for q in (1, 2):
                    rows = slice(32 * q, 32 * q + 32)
                    for k in range(q):
                        ch.link(v.tensor_tensor(b32[rows, :], b32[rows, :], b16[rows, :], ALU.subtract))
                        ch.link(v.tensor_copy(b16[rows, :], b32[rows, :]))

            @block.vector
            def _(dve):
                ch = Chain(dve, own)
                v = nc.vector
                for t in range(2):
                    dve.wait_ge(s_l, t + 1)
                    ch.link(v.tensor_tensor(lg[:, t, :], pl[:, t, 0:N_EXP], rb, ALU.add))
                    ch.link(v.max(top[:, t, :], lg[:, t, :]))
                    ch.link(v.max_index(idx[:, t, :], top[:, t, :], lg[:, t, :]))
                    v.tensor_scalar(st[:, t, 0:1], top[:, t, 0:1], -1.0, None, ALU.mult).then_inc(s_t, 1)
                    ch.link(v.tensor_copy(idf[:, t, :], idx[:, t, :]))
                    for k in range(TOP_K):
                        ch.mark(v.tensor_scalar(hot[:, t, k, :], iota[:, 0:N_EXP], idf[:, t, k:k + 1], None,
                                                ALU.is_equal))
                ch.wait()
                v.tensor_reduce(mask[:, :, :], hot[:, :, :, :].rearrange("p t k e -> p t e k"), AX.X, ALU.add)\
                    .then_inc(s_m, 1)
                dve.wait_ge(s_cnt, 1)
                ch.mark(v.tensor_scalar(cnt[:, 1, :], pt[0:N_EXP, 0, 0:P], float(P), 1.0, ALU.is_gt, ALU.add))
                ch.mark(v.memset(prev[:, :, 0:1], 0.0))
                ch.mark(v.tensor_copy(prev[0:1, 0, 1:N_EXP], pt[0:1, 1, 0:N_EXP - 1]))
                ch.mark(v.tensor_scalar(prev[0:1, 1, 1:N_EXP], pt[0:1, 1, 0:N_EXP - 1], float(P), 1.0,
                                        ALU.is_gt, ALU.add))
                ch.mark(v.tensor_scalar(item[0:1, 3, 0:1], pt[0:1, 1, N_EXP - 1:N_EXP], float(P), None, ALU.is_gt))
                ch.wait()
                v.tensor_copy(cnt[:, 0, :], pt[0:N_EXP, 0, 0:P]).then_inc(s_cntc, 1)
                dve.wait_ge(s_base, 1)
                ch.mark(v.tensor_copy(base[:, :, :], pl[:, :, 0:N_EXP]))
                ch.link(v.tensor_copy(prev[0:1, 2, :], pt[0:1, 1, 0:N_EXP]))
                ch.link(v.tensor_tensor(hotb[:, :, :, :], hot[:, :, :, :], rep(base[:, :, :], TOP_K, 2), ALU.mult))
                ch.link(v.tensor_reduce(rank, hotb[:, :, :, :], AX.X, ALU.add))
                for t in range(2):
                    ch.link(v.tensor_scalar(S[:, t, :], iota, rank[:, t, 0:1], None, ALU.is_equal))
                    for k in range(1, TOP_K):
                        ch.link(v.scalar_tensor_tensor(out=S[:, t, :], in0=iota, scalar=rank[:, t, k:k + 1],
                                                       in1=S[:, t, :], op0=ALU.is_equal, op1=ALU.add))
                v.sem_inc(s_S, 1)
                for t in range(2):
                    dve.wait_ge(s_e, t + 1)
                    ch.link(v.tensor_reduce(st[:, t, 1:2], top[:, t, 0:4], AX.X, ALU.add))
                    ch.link(v.reciprocal(st[:, t, 2:3], st[:, t, 1:2]))
                    ch.link(v.tensor_scalar(topg[:, t, :], top[:, t, 0:4], st[:, t, 2:3], None, ALU.mult))
                    ch.link(v.tensor_scalar(gates[:, t, :], hot[:, t, 0, :], topg[:, t, 0:1], None, ALU.mult))
                    for k in range(1, TOP_K):
                        ch.link(v.scalar_tensor_tensor(out=gates[:, t, :], in0=hot[:, t, k, :],
                                                       scalar=topg[:, t, k:k + 1], in1=gates[:, t, :],
                                                       op0=ALU.mult, op1=ALU.add))
                    v.sem_inc(s_g, 1)
                it = rep(iota[0:1, 0:N_ITEM], N_EXP, 2)
                ch.link(v.tensor_tensor(le[0:1, 0, :, :], rep(prev[0:1, 2, :], N_ITEM, 1), it, ALU.is_le))
                ch.link(v.tensor_reduce(item[0:1, 0, :], le[0:1, 0, :, :], AX.X, ALU.add))
                ch.mark(v.tensor_scalar(table[0:1, 0:N_ITEM], item[0:1, 0, :], 1.0, None, ALU.subtract))
                for q in range(2):
                    ch.link(v.tensor_tensor(le[0:1, 1, :, :], le[0:1, 0, :, :], rep(prev[0:1, q, :], N_ITEM, 1),
                                            ALU.mult))
                    ch.link(v.tensor_reduce(item[0:1, 1 + q, :], le[0:1, 1, :, :], AX.X, ALU.add))
                ch.link(v.tensor_tensor(item[0:1, 2, :], iota[0:1, 0:N_ITEM], item[0:1, 2, :], ALU.subtract))
                ch.mark(v.scalar_tensor_tensor(out=table[0:1, N_ITEM:2 * N_ITEM], in0=item[0:1, 2, :],
                                               scalar=float(P), in1=item[0:1, 1, :], op0=ALU.mult, op1=ALU.add))
                ch.mark(v.tensor_tensor(table[0:1, 2 * N_ITEM:2 * N_ITEM + 1], prev[0:1, 2, N_EXP - 1:N_EXP],
                                        item[0:1, 3, 0:1], ALU.add))
                for t in range(2):
                    dve.wait_ge(s_gt, t + 1)
                    v.tensor_copy(gT[:, t, :], pl[0:N_EXP, t, 0:P]).then_inc(s_gc, 1)
                for t in range(2):
                    ch.link(v.tensor_scalar(gsel[:, t, :], iota, rank[:, t, 0:1], topg[:, t, 0:1],
                                            ALU.is_equal, ALU.mult))
                    for k in range(1, TOP_K):
                        ch.link(v.tensor_scalar(g.tmp[:, :], iota, rank[:, t, k:k + 1], topg[:, t, k:k + 1],
                                                ALU.is_equal, ALU.mult))
                        ch.link(v.tensor_tensor(gsel[:, t, :], gsel[:, t, :], g.tmp[:, :], ALU.add))
                ch.wait()


EXP_CHUNKS = 6


def experts(g, w_gu, w_down, b16, pick, XgT, table, y_dram):
    nc, ring = g.nc, g.ring
    base, done0 = ring.used, ring.done
    C = EXP_CHUNKS
    assert SLOTS == 3 and ring.issued == base + SLOTS
    with Phase(g, "experts") as ph:
        xe = ph.sb("x", [P, 2, KT, P], F32R)
        hidT = ph.sb("hiddenT", [P, 2, KT, P], F32R)
        gt = ph.sb("gate", [P, 2, 512])
        up = ph.sb("up", [P, 2, 512])
        sg = ph.sb("sigmoid", [P, 2, 512])
        y = g.tmp
        pe_pick = ph.sb("picked", [96, P], BF16)
        w_high = [g.xT_low[:, :, :].rearrange("p a b -> p (a b)"),
                  ph.sb("w_high1", [P, SLOT], F32R)[:, :], ph.sb("w_high2", [P, SLOT], F32R)[:, :]]
        pg = ph.ps("gu", [P, 4, 512])
        pd = ph.ps("down", [P, 2, 512])
        pt = ph.ps("hiddenT", [P, 2, 512])
        own, s_gt, s_up, s_sg, s_h, s_t, s_tc, s_tl, s_y, s_pk, s_xh, s_xl, s_st, s_end, s_hi, s_lo, s_lp = (ph.sem(x) for x in (
            "chain", "gate", "up", "sigmoid", "hidden", "turned", "turned_high", "turned_low", "y", "picked",
            "x_high", "x_low", "stored", "end", "high", "low", "low_pool"))

        s_used = ph.sem("first_half_used")
        s_ld2 = [ph.sem(f"second_half_loaded_{n}") for n in range(SLOTS)]

        def src(e, j):
            if j < 4:
                c = 1024 * (j % 2) + 512 * (j // 2)
                return w_gu[bass.ds(e, 1), :, c:c + 512].rearrange("e (a p) n -> p (e a) n", p=P)
            r = 512 * (j - 4)
            return w_down[bass.ds(e, 1), r:r + 512, :].rearrange("e (a p) n -> p (e a) n", p=P)

        def flat(j):
            return ring.buf[:, (base + j) % SLOTS, :]

        def flat_low(j):
            return ring.rounded[:, (base + j) % SLOTS, :]

        def shaped(w, j):
            return w.rearrange("p (a b) -> p a b", a=8 if j % C < 4 else 4)

        def parts(j):
            return shaped(w_high[j % 3], j), shaped(flat_low(j), j)

        def half(j, x, h):
            n = 4 if j % C < 4 else 2
            return x[:, h * n:(h + 1) * n, :]

        def last_item(eng):
            return eng.value_load(table[0:1, 2 * N_ITEM:2 * N_ITEM + 1], min_val=N_EXP - 1, max_val=N_ITEM - 1)

        def expert_of(eng, i):
            return eng.value_load(table[0:1, bass.ds(i, 1)], min_val=0, max_val=N_EXP - 1)

        def slot_of(eng, i):
            return eng.value_load(table[0:1, bass.ds(i + N_ITEM, 1)], min_val=0, max_val=N_PAIR)

        PARTS, DVE_PARTS, POOL_PARTS = 4, (0, 2, 3), (1,)

        def part(p):
            return slice(p * SLOT // PARTS, (p + 1) * SLOT // PARTS)

        def low(eng, i, j, ps, sem):
            for p in ps:
                eng.wait_ge(s_hi, i * PARTS * C + (PARTS * j + p + 1))
                eng.tensor_tensor(flat_low(j)[:, part(p)], flat(j)[:, part(p)], w_high[j % 3][:, part(p)].bitcast(F32), ALU.subtract)\
                    .then_inc(sem, 1)

        with nc.Block() as block:
            @block.sync
            def _(sync):
                def load(i, e, j):
                    sync.wait_ge(s_used, i * C + (j - 2))
                    sync.dma_start(half(j, shaped(flat(j), j), 0), half(j, src(e, j % C), 0))\
                        .then_inc(ring.loaded[(base + j) % SLOTS], 16)
                    sync.wait_ge(ring.gemm_done, i * C + (done0 + j - 2))
                    sync.dma_start(half(j, shaped(flat(j), j), 1), half(j, src(e, j % C), 1))\
                        .then_inc(s_ld2[j % SLOTS], 16)

                for n in range(SLOTS):
                    sync.sem_inc(s_ld2[n], 16)
                last = last_item(sync)
                with sync.Fori(0, last) as i:
                    e = expert_of(sync, i)
                    for j in range(3, 6):
                        load(i, e, j)
                    e = expert_of(sync, i + 1)
                    for j in range(6, 9):
                        load(i, e, j)
                for j in range(3, 6):
                    load(last, N_EXP - 1, j)

            @block.gpsimd
            def _(pool):
                def picked(i):
                    e = expert_of(pool, i)
                    nc.gpsimd.tensor_copy(pe_pick[:, :], pick[:, bass.ds(e, 1)].to_broadcast([96, P]))\
                        .then_inc(s_pk, 1)

                def item(i, more):
                    for j in (2, 3, 4, 5):
                        low(pool, i, j, POOL_PARTS, s_lp)
                    if more:
                        low(pool, i, 6, POOL_PARTS, s_lp)
                        picked(i + 1)
                        low(pool, i, 7, POOL_PARTS, s_lp)

                picked(0)
                low(pool, 0, 0, POOL_PARTS, s_lp)
                low(pool, 0, 1, POOL_PARTS, s_lp)
                last = last_item(pool)
                with pool.Fori(0, last) as i:
                    item(i, True)
                item(last, False)

            @block.tensor
            def _(pe):
                pe.sem_inc(s_t, 2)
                with pe.Fori(0, last_item(pe) + 1) as i:
                    def split(j, p):
                        if p in DVE_PARTS:
                            pe.wait_ge(s_lo, i * len(DVE_PARTS) * C + (len(DVE_PARTS) * j + DVE_PARTS.index(p) + 1))
                        else:
                            pe.wait_ge(s_lp, i * C + (j + 1))

                    def gate_or_up(j):
                        h, q = j // 2, j % 2
                        c = 1024 * q + 512 * h
                        nc.tensor.matmul(pg[:, j, :], pe_pick[:, :], b16[:, c:c + 512], start=True, stop=False)
                        for kt in range(KT):
                            if kt % 2 == 0:
                                split(j, kt // 2)
                            wh, wl = (w[:, kt, :] for w in parts(j))
                            xh, xl = (xe[:, p, kt, :] for p in range(2))
                            nc.tensor.matmul(pg[:, j, :], xh, wh, start=False, stop=False)
                            nc.tensor.matmul(pg[:, j, :], xh, wl, start=False, stop=False)
                            mm = nc.tensor.matmul(pg[:, j, :], xl, wh, start=False, stop=(kt == KT - 1))
                            if kt == KT // 2 - 1:
                                mm.then_inc(s_used, 1)
                        mm.then_inc(ring.gemm_done, 1)

                    def turn_hidden(h):
                        pe.wait_ge(s_h, i * 2 + (h + 3))
                        for j in range(4):
                            mm = nc.tensor.transpose(pt[:, h, j * P:(j + 1) * P], up[:, h, j * P:(j + 1) * P],
                                                     blk(g, C_ID))
                        mm.then_inc(s_t, 1)

                    def down(h):
                        pe.wait_ge(s_tl, i * 2 + (h + 1))
                        for j in range(4):
                            split(4 + h, j)
                            f = 4 * h + j
                            wh, wl = (w[:, j, :] for w in parts(4 + h))
                            xh, xl = (hidT[:, p, f, :] for p in range(2))
                            for k, (x, w) in enumerate(((xh, wh), (xh, wl), (xl, wh))):
                                for c in range(2):
                                    mm = nc.tensor.matmul(pd[:, c, :], x, w[:, c * 512:c * 512 + 512],
                                                          start=(f == 0 and k == 0), stop=(f == KT - 1 and k == 2))
                            if j == 1:
                                mm.then_inc(s_used, 1)
                        mm.then_inc(ring.gemm_done, 1)

                    pe.wait_ge(s_pk, i + 1)
                    pe.wait_ge(s_xl, i + 1)
                    pe.wait_ge(s_up, i * 2 + 1)
                    gate_or_up(0)
                    gate_or_up(1)
                    pe.wait_ge(s_up, i * 2 + 2)
                    gate_or_up(2)
                    turn_hidden(0)
                    gate_or_up(3)
                    pe.wait_ge(s_y, i * 2 + 2)
                    down(0)
                    turn_hidden(1)
                    down(1)

            @block.scalar
            def _(act):
                def high(i, j):
                    n = base + j
                    act.wait_ge(ring.loaded[n % SLOTS], i * 32 + 16 * (n // SLOTS + 1))
                    for p in range(PARTS):
                        if p == PARTS // 2:
                            act.wait_ge(s_ld2[j % SLOTS], i * 32 + 16 * (j // SLOTS + 1))
                        nc.scalar.copy(w_high[j % 3][:, part(p)], flat(j)[:, part(p)]).then_inc(s_hi, 1)

                def tokens(i):
                    s0 = slot_of(act, i)
                    nc.scalar.copy(xe[:, 0, :, :], XgT[:, :, bass.ds(s0, P)]).then_inc(s_xh, 1)

                def sigmoid(i, h):
                    act.wait_ge(s_gt, i * 2 + (h + 1))
                    nc.scalar.activation(sg[:, h, :], gt[:, h, :], ACT.Sigmoid, scale=SWI_ALPHA).then_inc(s_sg, 1)

                def turned(i, h):
                    act.wait_ge(s_t, i * 2 + (h + 3))
                    nc.scalar.copy(hidT[:, 0, 4 * h:4 * h + 4, :].rearrange("p a b -> p (a b)"), pt[:, h, :])\
                        .then_inc(s_tc, 1)

                def item(i, more):
                    s0 = slot_of(act, i)
                    high(i, 2)
                    sigmoid(i, 0)
                    high(i, 3)
                    turned(i, 0)
                    high(i, 4)
                    sigmoid(i, 1)
                    high(i, 5)
                    turned(i, 1)
                    if more:
                        tokens(i + 1)
                        high(i, 6)
                        high(i, 7)
                    act.wait_ge(ring.gemm_done, i * C + (done0 + C))
                    act.wait_ge(s_st, i * 16 + 16)
                    for c in range(2):
                        nc.scalar.copy(y[:, c * 512:c * 512 + 512], pd[:, c, :]).then_inc(s_y, 1)
                    act.wait_ge(s_y, i * 2 + 4)
                    act.dma_start(y_dram[bass.ds(s0, P), :], y[:, :]).then_inc(s_st, 16)

                nc.scalar.sem_inc(s_y, 2)
                nc.scalar.sem_inc(s_st, 16)
                tokens(0)
                high(0, 0)
                high(0, 1)
                last = last_item(act)
                with act.Fori(0, last) as i:
                    item(i, True)
                item(last, False)
                act.wait_ge(s_st, last * 16 + 32)
                nc.scalar.sem_inc(s_end, 1)
                act.wait_ge(s_end, 1)

            @block.vector
            def _(dve):
                v = nc.vector

                def tokens_low(i):
                    s0 = slot_of(dve, i)
                    dve.wait_ge(s_xh, i + 1)
                    v.tensor_tensor(xe[:, 1, :, :], XgT[:, :, bass.ds(s0, P)], xe[:, 0, :, :].bitcast(F32),
                                    ALU.subtract).then_inc(s_xl, 1)

                def hidden(i, h):
                    dve.wait_ge(ring.gemm_done, i * C + (done0 + 2 * h + 1))
                    dve.wait_ge(s_h, i * 2 + (h + 2))
                    v.tensor_scalar(gt[:, h, :], pg[:, 2 * h, :], SWI_LIMIT, None, ALU.min).then_inc(s_gt, 1)
                    dve.wait_ge(ring.gemm_done, i * C + (done0 + 2 * h + 2))
                    dve.wait_ge(s_t, i * 2 + (h + 2))
                    v.tensor_scalar(up[:, h, :], pg[:, 2 * h + 1, :], SWI_LIMIT, -SWI_LIMIT,
                                    ALU.min, ALU.max).then_inc(s_up, 1)
                    dve.wait_ge(s_up, i * 2 + (h + 3))
                    v.scalar_tensor_tensor(out=up[:, h, :], in0=up[:, h, :], scalar=1.0, in1=gt[:, h, :],
                                           op0=ALU.add, op1=ALU.mult).then_inc(own, 1)
                    dve.wait_ge(own, i * 2 + (h + 1))
                    dve.wait_ge(s_sg, i * 2 + (h + 1))
                    v.tensor_tensor(up[:, h, :], up[:, h, :], sg[:, h, :], ALU.mult).then_inc(s_h, 1)

                def turned_low(i, h):
                    dve.wait_ge(s_tc, i * 2 + (h + 1))
                    hi, lo = (hidT[:, p, 4 * h:4 * h + 4, :].rearrange("p a b -> p (a b)") for p in range(2))
                    v.tensor_tensor(lo, pt[:, h, :], hi.bitcast(F32), ALU.subtract).then_inc(s_tl, 1)

                def dve_low(i, j):
                    low(dve, i, j, DVE_PARTS, s_lo)

                def item(i, more):
                    dve_low(i, 2)
                    hidden(i, 0)
                    dve_low(i, 3)
                    turned_low(i, 0)
                    dve_low(i, 4)
                    hidden(i, 1)
                    dve_low(i, 5)
                    turned_low(i, 1)
                    if more:
                        tokens_low(i + 1)
                        dve_low(i, 6)
                        dve_low(i, 7)

                v.sem_inc(s_up, 2)
                v.sem_inc(s_h, 2)
                tokens_low(0)
                dve_low(0, 0)
                dve_low(0, 1)
                last = last_item(dve)
                with dve.Fori(0, last) as i:
                    item(i, True)
                item(last, False)


def final(g, acc, gsel, y_dram, gate_row, final_g, out):
    nc = g.nc
    NS = N_PAIR // P
    with Phase(g, "final") as ph:
        sq = ph.sb("square", [P, D])
        ss = ph.sb("sums", [P, 4, 2])
        yl = ph.sb("y_list", [P, NS, D])
        gT = ph.sb("gselT", [P, NS, 2, P])
        pt = ph.ps("gselT", [P, 4, 512])
        pa = ph.ps("acc", [P, 4, 512])
        final_row = ph.sb("final_g", [P, D])[:, :]
        s_row = ph.sem("row_loaded")
        own, s_x, s_ss, s_ms, s_rt, s_y, s_out = (ph.sem(x) for x in ("chain", "x", "sum", "mean", "root", "y", "out"))
        s_yl = [ph.sem(f"list_loaded_{n}") for n in range(2)]
        s_gt, s_gc, s_acc = (ph.sem(x) for x in ("gselT", "gselT_copied", "acc"))
        with nc.Block() as block:
            @block.tensor
            def _(pe):
                for n in range(NS // 2):
                    for j in range(4):
                        s = 2 * n + j // 2
                        mm = nc.tensor.transpose(pt[:, n, j * P:(j + 1) * P], gsel[:, j % 2, s * P:(s + 1) * P],
                                                 blk(g, C_ID))
                    mm.then_inc(s_gt, 1)
                pe.wait_ge(s_gc, NS // 2)
                for half in range(2):
                    pe.wait_ge(s_yl[half], 16)
                    for s in range(half * NS // 2, (half + 1) * NS // 2):
                        for i in range(4):
                            mm = nc.tensor.matmul(pa[:, i, :], gT[:, s, i // 2, :],
                                                  yl[:, s, (i % 2) * 512:(i % 2) * 512 + 512],
                                                  start=(s == 0), stop=(s == NS - 1))
                mm.then_inc(s_acc, 1)

            @block.vector
            def _(dve):
                ch = Chain(dve, own)
                dve.wait_ge(s_row, 16)
                for n in range(NS // 2):
                    dve.wait_ge(s_gt, n + 1)
                    nc.vector.tensor_copy(gT[:, 2 * n:2 * n + 2, :, :].rearrange("p s t c -> p (s t c)"), pt[:, n, :])\
                        .then_inc(s_gc, 1)
                dve.wait_ge(s_acc, 1)
                for t in range(2):
                    a = acc[:, t, :]
                    ch.link(nc.vector.tensor_tensor(a, a, pa[:, 2 * t:2 * t + 2, :].rearrange("p a b -> p (a b)"),
                                                    ALU.add))
                    ch.link(nc.vector.tensor_tensor(a, a, gate_row, ALU.mult))
                    nc.vector.tensor_tensor(g.x[:, 2 + t, :], g.x[:, 2 + t, :], a, ALU.add).then_inc(s_x, 1)
                dve.wait_ge(s_ss, 2)
                nc.vector.tensor_scalar(ss[:, 1, :], ss[:, 0, :], 1.0 / D, EPS, ALU.mult, ALU.add).then_inc(s_ms, 1)
                dve.wait_ge(s_rt, 1)
                ch.link(nc.vector.reciprocal(ss[:, 3, :], ss[:, 2, :]))
                for t in range(2):
                    nc.vector.scalar_tensor_tensor(out=acc[:, t, :], in0=g.x[:, 2 + t, :], scalar=ss[:, 3, t:t + 1],
                                                   in1=final_row, op0=ALU.mult, op1=ALU.mult).then_inc(s_y, 1)

            @block.scalar
            def _(act):
                for t in range(2):
                    act.wait_ge(s_x, t + 1)
                    nc.scalar.activation(sq[:, :], g.x[:, 2 + t, :], ACT.Square, accum_out=ss[:, 0, t:t + 1])\
                        .then_inc(s_ss, 1)
                    act.wait_ge(s_ss, t + 1)
                act.wait_ge(s_ms, 1)
                nc.scalar.activation(ss[:, 2, :], ss[:, 1, :], ACT.Sqrt).then_inc(s_rt, 1)

            @block.sync
            def _(sync):
                sync.dma_start(final_row, final_g).then_inc(s_row, 16)
                h = NS // 2
                for half in range(2):
                    sync.dma_start(yl[:, half * h:(half + 1) * h, :],
                                   y_dram[half * h * P:(half + 1) * h * P, :].rearrange("(s p) n -> p s n", p=P))\
                        .then_inc(s_yl[half], 16)
                for t in range(2):
                    sync.wait_ge(s_y, t + 1)
                    sync.dma_start(out[0, t * P:(t + 1) * P, :], acc[:, t, :]).then_inc(s_out, 16)
                sync.wait_ge(s_out, 32)


def load(g, name, jobs):
    nc = g.nc
    with Phase(g, name) as ph:
        s = ph.sem("loaded")
        with nc.Block() as block:
            @block.sync
            def _(sync):
                for dst, src in jobs:
                    sync.dma_start(dst, src).then_inc(s, 16)
                sync.wait_ge(s, 16 * len(jobs))


def copy_to(g, dst):
    def out(ch, t, c0, w, ps):
        return g.nc.vector.tensor_copy(dst(t, c0, w), ps)
    return out


def row(ap):
    return ap.partition_broadcast(P)


def layer0(g, a):
    nc = g.nc
    adaln(g, "ada0", a["cond_col"], a["adab_col"][0], g.mod)
    mod = lambda j, t: g.mod[:, 8 * j:8 * j + 8, 0 if t >= 2 else 1]
    norm_T(g, "norm0a", ALL_TILES, g.xT, lambda t: mod(1, t), lambda t: mod(0, t))
    with ExitStack() as outer:
        osb = lambda n, s, dt=F32: outer.enter_context(nc.sbuf_tensor(n, s, dt))
        pb = osb("projB", [P, TT, 2064])
        gates = osb("gates", [P, TT, 16])
        small = osb("small", [P, 16 + 64 + 64])
        cat = g.xT[:, :, :].rearrange("p a b -> p (a b)").rearrange("p (t c) -> p t c", t=TT)
        with ExitStack() as inner:
            isb = lambda n, s, dt=F32: inner.enter_context(nc.sbuf_tensor(n, s, dt))
            pa = isb("projA", [P, TT, 1536])
            rope = isb("rope", [P, 2, 2, ML_D])
            load(g, "ldab", [(small[:, 0:16], row(a["gate_b"])), (small[:, 16:80], row(a["qn"])),
                             (small[:, 80:144], row(a["kn"])), (rope[:, :, :, :], a["rope"])])
            gemm_tok(g, "projAB", widths(AB_W), (g.xT, g.xT_low), ALL_TILES,
                     copy_to(g, lambda t, c0, w: pa[:, t, c0:c0 + w] if c0 < 1536
                             else pb[:, t, c0 - 1536:c0 - 1536 + w]))
            ab_prepare(g, pa, pb, small, rope, gates)
            qT = isb("qaT", [P, 4, 512])
            kT = isb("kaT", [P, 4, 512])
            turn(g, "turnA", [(pa[:, t, o + p * P:o + (p + 1) * P], dst[:, p, t * P:(t + 1) * P])
                              for t in ALL_TILES for o, dst in ((0, qT), (512, kT)) for p in range(4)])
            attention(g, pa, qT, kT, cat, a["rpb_cols"], a["window"])
        with ExitStack() as inner:
            isb = lambda n, s, dt=F32: inner.enter_context(nc.sbuf_tensor(n, s, dt))
            qT = isb("qbT", [P, 4, 512])
            kT = isb("kbT", [P, 4, 512])
            hs = isb("hs", [P, TT, 512])
            rowg = isb("rowg", [4, 4, 512])
            rowo = isb("rowo", [4, 6, 512])
            colg = isb("colg", [P, TT, 4, ML_H])
            sel = isb("sel", [4, 4, P])
            head_row = isb("head_row", [P, 512])
            turn(g, "turnB", [(pb[:, t, o + h * P:o + (h + 1) * P], dst[:, h, t * P:(t + 1) * P])
                              for t in ALL_TILES for o, dst in ((0, qT), (512, kT)) for h in range(4)]
                 + [(gates[:, t, 4 * q:4 * q + 4], rowg[:, q, t * P:(t + 1) * P]) for t in ALL_TILES for q in range(4)])
            load(g, "ldsel", [(sel[:, :, :], a["sel"]), (head_row[:, :], row(a["headn"]))])
            mlstm_rows(g, rowg, rowo, None)
            turn_small(g, "turnC", [(rowo[0:4, q, t * P:(t + 1) * P], colg[:, t, q, :])
                                    for t in ALL_TILES for q in range(4)])
            mlstm(g, pb, qT, kT, rowo, colg, sel, hs)
            ab_merge(g, pb, hs, head_row[:, :], cat)
    with ExitStack() as outer:
        osb = lambda n, s, dt=F32: outer.enter_context(nc.sbuf_tensor(n, s, dt))
        rows = osb("gate_rows0", [P, 4, D])
        gate_rows(g, "rows0", [lambda kt, j=j, i=i: g.mod[:, 8 * j + kt, i:i + 1] for j, i in
                               ((2, 0), (2, 1), (5, 0), (5, 1))], rows)
        with ExitStack() as inner:
            catT = inner.enter_context(nc.sbuf_tensor("catT", [P, KT, 512], F32))
            catT_low = rounded_alias(nc, catT)
            turn(g, "turnD", [(cat[:, t, k * P:(k + 1) * P], catT[:, k, t * P:(t + 1) * P])
                              for t in ALL_TILES for k in range(KT)])
            gemm_tok(g, "about", widths(D), (catT, catT_low), ALL_TILES,
                     residual(g, lambda t: rows[:, 0 if t >= 2 else 1, :], 0))
        norm_T(g, "norm0m", ALL_TILES, g.xT, lambda t: mod(4, t), lambda t: mod(3, t))
        mlp(g, "mlp0", ALL_TILES, lambda t: rows[:, 2 if t >= 2 else 3, :])


def turn_small(g, name, jobs):
    nc = g.nc
    with Phase(g, name) as ph:
        ps = ph.ps("turned", [P, len(jobs), 4])
        s, own = ph.sem("turned"), ph.sem("chain")
        with nc.Block() as block:
            @block.tensor
            def _(pe):
                for i, (src, dst) in enumerate(jobs):
                    nc.tensor.transpose(ps[:, i, :], src, blk(g, C_ID)[0:4, 0:4]).then_inc(s, 1)

            @block.vector
            def _(dve):
                dve.wait_ge(s, len(jobs))
                for i, (src, dst) in enumerate(jobs):
                    nc.vector.tensor_copy(dst, ps[:, i, :]).then_inc(own, 1)
                dve.wait_ge(own, len(jobs))


def layer1(g, a):
    nc = g.nc
    adaln(g, "ada1", a["cond_col"], a["adab_col"][1], g.mod)
    mod = lambda j, t: g.mod[:, 8 * j:8 * j + 8, 0 if t >= 2 else 1]
    norm_T(g, "norm1a", ALL_TILES, g.xT, lambda t: mod(1, t), lambda t: mod(0, t))
    scr = {n: nc.dram_tensor(f"rw_{n}", [2 if n == "r" else 4, P, D], F32, kind="Internal").ap()
           for n in ("k", "v", "kk", "r")}
    with ExitStack() as outer:
        osb = lambda n, s, dt=F32: outer.enter_context(nc.sbuf_tensor(n, s, dt))
        low_w = osb("low_w", [P, 512])
        low_a = osb("low_a", [P, 512])
        sg0 = osb("sg0", [P, 256])
        sg1 = osb("sg1", [32, 256])
        y = osb("rw_y", [P, 2, D])
        coef = osb("coef", [P, 2, 2, RW_H])
        with ExitStack() as inner:
            isb = lambda n, s, dt=F32: inner.enter_context(nc.sbuf_tensor(n, s, dt))
            xx = isb("xx", [P, KT, 512])
            xs = isb("xs", [P, KT, 512])
            xs_low = rounded_alias(nc, xs)
            stage = isb("stage", [P, TT, D])
            mu = isb("mu", [P, 6, KT])
            kkrow = isb("kkrow", [P, D])
            load(g, "ldmu", [(mu[:, :, :], a["mu_col"]), (kkrow[:, :], row(a["k_k"]))])
            rw_shift(g, xx)
            to_stage = copy_to(g, lambda t, c0, w: stage[:, t, c0:c0 + w])
            for n, m, tiles in (("k", 2, ALL_TILES), ("v", 3, ALL_TILES), ("r", 0, LAT_TILES)):
                rw_mix(g, f"mix_{n}", xx, xs, mu[:, m, :])
                gemm_tok(g, f"proj_{n}", widths(D), tuple(v[:, :, tiles[0] * P:] for v in (xs, xs_low)), tiles,
                         to_stage, depth=7)
                store(g, f"store_{n}", [(scr[n][t - tiles[0]], stage[:, t, :]) for t in tiles])
                if n == "k":
                    with nc.sbuf_tensor("kk", [P, TT, D], F32) as kk:
                        rw_kk(g, stage, kk, kkrow[:, :])
                        store(g, "store_kk", [(scr["kk"][t], kk[:, t, :]) for t in tiles])
            rw_mix(g, "mix_w", xx, xs, mu[:, 1, :])
            rw_lora(g, "lora_w", a["w1"], xs, 0, [(0, 128, low_w[:, :])], ACT.Tanh)
            rw_mix(g, "mix_a", xx, xs, mu[:, 4, :])
            rw_lora(g, "lora_a", a["a1"], xs, 0, [(0, 128, low_a[:, :])], ACT.Copy)
            rw_mix(g, "mix_g", xx, xs, mu[:, 5, :])
            rw_lora(g, "lora_g", a["g1"], xs, 256, [(0, 128, sg0[:, :]), (128, 160, sg1[:, :])], ACT.Sigmoid)
        with ExitStack() as inner:
            isb = lambda n, s, dt=F32: inner.enter_context(nc.sbuf_tensor(n, s, dt))
            w2 = isb("w2", [P, D])
            a2 = isb("a2", [P, D])
            w0 = isb("w0", [P, 2, D])
            a0 = isb("a0", [P, 2, D])
            ka = isb("ka", [P, D])
            rk = isb("rk", [P, D])
            load(g, "ldrw", [(w2[:, :], a["w2"]), (a2[:, :], a["a2"])]
                 + [(w0[:, z, :], row(a["w0"][z])) for z in range(2)]
                 + [(a0[:, z, :], row(a["a0"][z])) for z in range(2)]
                 + [(ka[:, :], row(a["k_a"])), (rk[:, :], row(a["r_k"]))])
            rw_chunks(g, scr, low_w, low_a, w2, a2, {"w0": w0, "a0": a0, "ka": ka[:, :], "rk": rk[:, :]}, y, coef)
        rows = osb("gate_rows1", [P, 2, D])
        gate_rows(g, "rows1", [lambda kt, j=j: g.mod[:, 8 * j + kt, 0:1] for j in (2, 5)], rows)
        with ExitStack() as inner:
            isb = lambda n, s, dt=F32: inner.enter_context(nc.sbuf_tensor(n, s, dt))
            v = isb("v_lat", [P, 2, D])
            lw = isb("lw", [P, D])
            lb = isb("lb", [P, D])
            g2a = isb("g2a", [P, D])
            g2b = isb("g2b", [32, D])
            ro = isb("readout", [P, 2, D])
            roT = isb("readoutT", [P, KT, 256])
            roT_low = rounded_alias(nc, roT)
            load(g, "ldro", [(v[:, t, :], scr["v"][2 + t]) for t in range(2)]
                 + [(lw[:, :], row(a["lnx_w"])), (lb[:, :], row(a["lnx_b"])), (g2a[:, :], a["g2"][0:P, :]),
                    (g2b[:, :], a["g2"][P:G_LORA, :])])
            rw_readout(g, y, coef, v, {"lw": lw[:, :], "lb": lb[:, :]}, sg0, sg1, g2a, g2b, ro)
            turn(g, "turnE", [(ro[:, t, k * P:(k + 1) * P], roT[:, k, t * P:(t + 1) * P])
                              for t in range(2) for k in range(KT)])
            gemm_tok(g, "rwout", widths(D), (roT, roT_low), LAT_TILES,
                     residual(g, lambda t: rows[:, 0, :], 0))
        norm_T(g, "norm1m", LAT_TILES, g.xT, lambda t: mod(4, t), lambda t: mod(3, t))
        mlp(g, "mlp1", LAT_TILES, lambda t: rows[:, 1, :])


def block2(g, a, out):
    nc = g.nc
    adaln(g, "ada2", a["cond2_col"], a["adab2_col"], g.mod)
    mod = lambda j, t: g.mod[:, 8 * j:8 * j + 8, 0]
    with ExitStack() as outer:
        osb = lambda n, s, dt=F32: outer.enter_context(nc.sbuf_tensor(n, s, dt))
        gains = osb("gains", [P, 2, KT])
        load(g, "ldgain", [(gains[:, :, :], a["norm_g_col"])])
        norm_T(g, "norm2a", LAT_TILES, g.xT, lambda t: mod(1, t), lambda t: mod(0, t), gains[:, 0, :], off=2)
        with ExitStack() as mid:
            msb = lambda n, s, dt=F32: mid.enter_context(nc.sbuf_tensor(n, s, dt))
            p2 = msb("proj2", [P, 2, 2080])
            og = msb("og", [P, 2, D])
            ys = msb("ys", [P, 2, D])
            x_high = rounded_alias(nc, ys)[:, :, :].rearrange("p a (b c) -> p (a b) c", c=256)
            gemm_tok(g, "proj2", widths(2080),
                     (g.xT[:, :, 0:256], g.xT_low[:, :, 0:256], x_high), LAT_TILES,
                     copy_to(g, lambda t, c0, w: p2[:, t - 2, c0:c0 + w]))
            with ExitStack() as inner:
                isb = lambda n, s, dt=F32: inner.enter_context(nc.sbuf_tensor(n, s, dt))
                feat = isb("feat", [P, 36, 256])
                taps = isb("taps", [P, 36, 4])
                cbias = isb("cbias", [P, 36])
                small = isb("small2", [P, 64])
                beta = isb("beta", [P, 2, 8])
                dt = isb("dt", [P, 2, SS_H])
                ga = isb("ga", [P, 2, 24])
                cums = isb("cums", [P, 4, 24])
                load(g, "ldconv", [(taps[:, :, :], a["taps_col"]), (cbias[:, :], a["cbias_col"]),
                                   (small[:, :], row(a["small2"]))])
                gd_conv(g, feat, taps, cbias, x_high, g.xT_low[:, :, 0:256])
                gd_l2(g, feat)
                gd_gates(g, p2, small, beta, dt, ga, cums)
                with ExitStack() as deep:
                    xtok = deep.enter_context(nc.sbuf_tensor("xtok", [P, 2, D], F32))
                    turn(g, "turnF", [(feat[:, 24 + f, t * P:(t + 1) * P], xtok[:, t, f * P:(f + 1) * P])
                                      for f in range(8) for t in range(2)])
                    ssd(g, feat, xtok, dt, ga, cums, small[:, 48:64], ys)
                with ExitStack() as deep:
                    ktok = deep.enter_context(nc.sbuf_tensor("ktok", [P, 2, D], F32))
                    vtok = deep.enter_context(nc.sbuf_tensor("vtok", [P, 2, D], F32))
                    turn(g, "turnG", [(feat[:, 8 + 8 * v + f, t * P:(t + 1) * P], dst[:, t, f * P:(f + 1) * P])
                                      for v, dst in enumerate((ktok, vtok)) for f in range(8) for t in range(2)])
                    gd_chunks(g, feat, ktok, vtok, beta, ga, cums, og)
            with ExitStack() as inner:
                isb = lambda n, s, dt=F32: inner.enter_context(nc.sbuf_tensor(n, s, dt))
                mix = isb("mix", [P, 2, 2 * D])
                gn = isb("gn", [P, P])
                sn = isb("sn", [P, D])
                load(g, "ldmix", [(gn[:, :], row(a["gdn_norm_g"])), (sn[:, :], row(a["ssd_norm_g"]))])
                gd_merge(g, p2, og, ys, {"gn": gn[:, :], "sn": sn[:, :]}, mix)
                mixT = isb("mixT", [P, 16, 256])
                turn(g, "turnH", [(mix[:, t, k * P:(k + 1) * P], mixT[:, k, t * P:(t + 1) * P])
                                  for t in range(2) for k in range(16)])
                rows = isb("gate_rows2", [P, 1, D])
                gate_rows(g, "rows2", [lambda kt: g.mod[:, 16 + kt, 0:1]], rows)
                gemm_rows(g, "mixout", 4, mixT, rows[:, 0, :])
        norm_T(g, "norm2m", LAT_TILES, g.xT, lambda t: mod(4, t), lambda t: mod(3, t), gains[:, 1, :], off=2)
        acc = osb("moe_acc", [P, 2, D])
        rank = osb("rank", [P, 2, TOP_K])
        topg = osb("top_gates", [P, 2, TOP_K])
        XgT = osb("slot_tokens", [P, KT, N_SLOT])
        table = osb("item_table", [1, 2 * N_ITEM + 1], I32)
        b16 = osb("bias_parts", [96, 2048], BF16)
        pick = osb("pick", [96, N_EXP], BF16)
        gsel = g.x[:, 0:2, :]
        rb = osb("rb", [P, N_EXP])
        rows = osb("rows3", [P, 1, D])
        y_dram = nc.dram_tensor("moe_y", [N_SLOT, D], F32, kind="Internal").ap()
        gate_rows(g, "rows3", [lambda kt: g.mod[:, 40 + kt, 0:1]], rows)
        with nc.sbuf_tensor("iota", [P, N_PAIR], F32) as iota:
            load(g, "ldmoe", [(rb[:, :], row(a["router_b"])), (iota[:, :], row(a["iota"]))])
            router(g, a["router_w"], rb[:, :], iota[:, :], a["b_down"], acc, rank[:, :, :], topg[:, :, :], XgT,
                   table, acc, gsel, a["b_gu"], b16, pick)
        experts(g, a["w_gu"], a["w_down"], b16, pick, XgT, table, y_dram)
        final(g, acc, gsel, y_dram, rows[:, 0, :], row(a["final_g"]), out)


def program(nc, a, out, parts=(0, 1, 2), x_out=None):
    g = G()
    g.nc = nc
    g.const = nc.alloc_sbuf_tensor("const", [P, N_BLOCKS * P], F32)
    g.x = nc.alloc_sbuf_tensor("x", [P, TT, D], F32)
    g.xT = nc.alloc_sbuf_tensor("xT", [P, KT, 512], F32)
    g.xT_low = rounded_alias(nc, g.xT)
    g.tmp = nc.alloc_sbuf_tensor("tmp", [P, D], F32)
    g.mod = nc.alloc_sbuf_tensor("mod", [P, 48, 2], F32)
    g.ring = ring = Ring(nc)
    if 0 in parts:
        plan_cols(ring, a["ada_w"][0], 6 * D, 1)
        plan_cols(ring, a["ab_w_in"], AB_W, 4)
        plan_cols(ring, a["ab_w_out"], D, 4)
        plan_cols(ring, a["mlp_w1"][0], D_FF, 4)
        plan_rows(ring, a["mlp_w2"][0], 4)
    if 1 in parts:
        plan_cols(ring, a["ada_w"][1], 6 * D, 1)
        for i, u in ((1, 4), (2, 4), (0, 2)):
            plan_cols(ring, a["w_rkv"][i], D, u)
        plan_cols(ring, a["rw_w_o"], D, 2)
        plan_cols(ring, a["mlp_w1"][1], D_FF, 4)
        plan_rows(ring, a["mlp_w2"][1], 4)
    if 2 in parts:
        plan_cols(ring, a["ada_w2"], 6 * D, 1)
        plan_cols(ring, a["w_in2"][:, 4608:6688], 2080, 2)
        plan_cols(ring, a["w_in2"][:, 0:4608], 4608, 4)
        plan_rows(ring, a["w_out2"], 1)
        wv = a["w_gu"][0].rearrange("(a p) n -> p a n", p=P)
        for c in (0, 1024, 512):
            ring.add(wv[:, :, c:c + 512], 0)
    xin = {t: a["ctx"][t * P:(t + 1) * P, :] if t < 2 else a["x"][(t - 2) * P:(t - 1) * P, :] for t in range(TT)}
    load(g, "ldx", [(g.const[:, :], a["const"])] + [(g.x[:, t, :], xin[t]) for t in range(TT)])
    if 0 in parts:
        layer0(g, a)
    if 1 in parts:
        layer1(g, a)
    if 2 in parts:
        block2(g, a, out)
    if x_out is not None:
        store(g, "stx", [(x_out[t], g.x[:, t, :]) for t in range(TT)])


def layout(i):
    def col(v, n=P):
        v = np.asarray(v)
        v = v.reshape(*v.shape[:-1], v.shape[-1] // n, n)
        return np.ascontiguousarray(np.moveaxis(v, -1, 0))

    f = np.asarray
    pad = np.zeros((NA_H, 15, 127), np.float32)
    pad[:, :, 48:79] = f(i["na_rpb"])[0]
    c = np.arange(GRID_W)
    rpb_cols = pad[:, 4:11][:, :, c[None, :] - c[:, None] + 63]
    sel = np.zeros((4, 4, P), np.float32)
    for h in range(4):
        sel[h, h, :] = 1.0
    z_r = lambda w: np.ascontiguousarray(f(w)[0].transpose(1, 0, 2).reshape(D, P).reshape(KT, P, P).transpose(1, 0, 2))
    conv = np.concatenate([f(i["gdn_conv_w_2"])[0], f(i["ssd_conv_w_2"])[0]], axis=1)
    return {
        "x": f(i["x"])[0], "ctx": f(i["ctx"])[0],
        "cond_col": np.stack([col(f(i["c"])[0]), col(f(i["c_ctx"]))], axis=2),
        "cond2_col": np.stack([col(f(i["c_2"])[0])] * 2, axis=2),
        "adab_col": np.stack([col(f(i["ada_b"])[l]) for l in range(2)]), "adab2_col": col(f(i["ada_b_2"])[0]),
        "ada_w": f(i["ada_w"]), "ab_w_in": f(i["ab_w_in"])[0], "ab_w_out": f(i["ab_w_out"])[0],
        "mlp_w1": f(i["mlp_w1"]), "mlp_w2": f(i["mlp_w2"]),
        "gate_b": f(i["ab_gate_b"])[0], "qn": f(i["na_q_norm"])[0], "kn": f(i["na_k_norm"])[0],
        "rpb_cols": rpb_cols, "headn": f(i["ml_head_norm"])[0].reshape(-1),
        "mu_col": col(f(i["rw_mu"])[0]), "w_rkv": f(i["rw_w_rkv"])[0],
        "w1": z_r(i["rw_w1"]), "a1": z_r(i["rw_a1"]),
        "g1": np.ascontiguousarray(f(i["rw_g1"])[0].reshape(KT, P, G_LORA).transpose(1, 0, 2)),
        "w2": f(i["rw_w2"])[0].reshape(P, D), "a2": f(i["rw_a2"])[0].reshape(P, D),
        "g2": f(i["rw_g2"])[0], "w0": f(i["rw_w0"])[0], "a0": f(i["rw_a0"])[0],
        "k_k": f(i["rw_k_k"])[0], "k_a": f(i["rw_k_a"])[0], "r_k": f(i["rw_r_k"])[0],
        "lnx_w": f(i["rw_lnx_w"])[0], "lnx_b": f(i["rw_lnx_b"])[0], "rw_w_o": f(i["rw_w_o"])[0],
        "ada_w2": f(i["ada_w_2"])[0], "w_in2": f(i["w_in_2"])[0][:, np.r_[0:3072, 5136:6672, 3072:5136, 6672:6688]], "w_out2": f(i["w_out_2"])[0],
        "norm_g_col": np.stack([col(f(i["norm1_g_2"])[0]), col(f(i["norm2_g_2"])[0])], axis=1),
        "taps_col": np.ascontiguousarray(conv.reshape(4, 36, P).transpose(2, 1, 0)),
        "cbias_col": np.concatenate([np.zeros((P, 24), np.float32), col(f(i["ssd_conv_b_2"])[0])], axis=1),
        "small2": np.concatenate([f(i[n])[0] for n in ("gdn_dt_bias_2", "ssd_dt_bias_2", "gdn_a_log_2",
                                                         "ssd_a_log_2", "ssd_d_2")]),
        "gdn_norm_g": f(i["gdn_norm_g_2"])[0], "ssd_norm_g": f(i["ssd_norm_g_2"])[0],
        "router_w": f(i["router_w_2"])[0],
        "router_b": f(i["router_b_2"])[0], "iota": np.arange(N_PAIR, dtype=np.float32),
        "w_gu": f(i["moe_w_gu_2"])[0], "w_down": f(i["moe_w_down_2"])[0], "b_down": f(i["moe_b_down_2"])[0],
        "b_gu": f(i["moe_b_gu_2"])[0], "final_g": f(i["final_g_2"]),
        "const": const_table(), "rope": rope_table(), "window": window_table(), "sel": sel,
    }


def kernel(**inputs):
    import concourse.bacc as bacc
    from concourse.bass_utils import run_bass_kernel_spmd

    nc = bacc.Bacc("TRN2", target_bir_lowering=False, num_devices=1)
    arrays = {f"in_{k}": np.ascontiguousarray(v) for k, v in layout(inputs).items()}
    aps = {k[3:]: nc.dram_tensor(k, v.shape, F32, kind="ExternalInput").ap() for k, v in arrays.items()}
    out = nc.dram_tensor("out", (1, 256, D), F32, kind="ExternalOutput").ap()
    program(nc, aps, out)
    r = run_bass_kernel_spmd(nc, [arrays], core_ids=[0])
    return r.results[0]["out"]
```
